# Optimizing a Trainium2 kernel written in Bass

```python
import math
import jax, jax.numpy as jnp
from jax import lax
import numpy as np

D_MODEL = 1024
BATCH = 1
SEQ = 1024
DEPTH = 1

CHUNK = 64
D_MIX = D_MODEL
W_GROUP = D_MIX // 4
GMLP_GROUPS = 4
GMLP_DG = W_GROUP // GMLP_GROUPS
GMLP_CHUNK = 128
DSA_HEADS = 4
DSA_HEAD_DIM = W_GROUP // DSA_HEADS
IDX_HEADS = 8
IDX_DIM = 32
DSA_TOPK = 256
DSA_QBLK = 128
POOL_GROUPS = 4
POOL_DG = W_GROUP // POOL_GROUPS
POOL_WINDOWS = (2, 4, 8, 16)
SWA_HEADS = 4
SWA_KV_HEADS = 2
SWA_HEAD_DIM = W_GROUP // SWA_HEADS
SWA_WINDOW = 128
REL_BUCKETS = 32
REL_MAX_DIST = 1024
D_FF = 2816
CONV_WIDTH = 3
EPS = 1e-6
NEG_INF = -1e30

IN_WIDTHS = (2 * W_GROUP,
             W_GROUP, W_GROUP, W_GROUP,
             IDX_HEADS * IDX_DIM, IDX_DIM, IDX_HEADS,
             W_GROUP,
             W_GROUP,
             SWA_KV_HEADS * SWA_HEAD_DIM,
             SWA_KV_HEADS * SWA_HEAD_DIM)
N_IN = (2 * W_GROUP + 3 * W_GROUP + IDX_HEADS * IDX_DIM + IDX_DIM + IDX_HEADS
        + W_GROUP + W_GROUP + 2 * SWA_KV_HEADS * SWA_HEAD_DIM)

kernel_name = "hybrid_parallel_mixer_streaming_encoder"

def _rms(x):
    xf = x.astype(jnp.float32)
    return (xf * lax.rsqrt(jnp.mean(xf * xf, axis=-1, keepdims=True) + EPS)).astype(x.dtype)

def rms_norm(x, g):
    return _rms(x) * g

def rel_bucket(rel):
    nb = REL_BUCKETS // 2
    max_exact = nb // 2
    ret = jnp.where(rel > 0, nb, 0)
    n = jnp.abs(rel)
    nf = jnp.maximum(n, 1).astype(jnp.float32)
    large = max_exact + (jnp.log(nf / max_exact) / math.log(REL_MAX_DIST / max_exact)
                         * (nb - max_exact)).astype(jnp.int32)
    large = jnp.minimum(large, nb - 1)
    return ret + jnp.where(n < max_exact, n, large)

def gmlp_mixer(z, ws, bs):
    bsz, seq = z.shape[:2]
    z = jax.nn.gelu(z)
    u, vv = z[..., :W_GROUP], z[..., W_GROUP:]
    vf = vv.reshape(bsz, seq, GMLP_GROUPS, GMLP_DG).astype(jnp.float32)
    mu = vf.mean(-1, keepdims=True)
    var = jnp.mean((vf - mu) ** 2, axis=-1, keepdims=True)
    vn = ((vf - mu) * lax.rsqrt(var + EPS)).astype(z.dtype)
    vn = vn.reshape(bsz, seq // GMLP_CHUNK, GMLP_CHUNK, GMLP_GROUPS, GMLP_DG)
    pos_chunk = jnp.arange(GMLP_CHUNK) // CHUNK
    mask = pos_chunk[:, None] >= pos_chunk[None, :]
    s = jnp.einsum('gij,bnjgd->bnigd', jnp.where(mask, ws, 0), vn) + bs.T[:, :, None]
    return u * s.reshape(bsz, seq, W_GROUP)

def dsa_mixer(q, k, v, qi, ki, wi, rel_tab):
    bsz, seq = q.shape[:2]
    topk = min(DSA_TOPK, seq // 4)
    nblk = seq // DSA_QBLK
    key_chunk = jnp.arange(seq) // CHUNK

    def to_blocks(a):
        return jnp.moveaxis(a.reshape(bsz, nblk, DSA_QBLK, *a.shape[2:]), 1, 0)

    def one_block(args):
        qi_b, wi_b, q_b, blk = args
        qpos = blk * DSA_QBLK + jnp.arange(DSA_QBLK)
        qchunk = qpos // CHUNK
        admissible = key_chunk[None, :] <= qchunk[:, None]
        dots = jnp.einsum('bqhd,bsd->bqhs', qi_b, ki).astype(jnp.float32) * (IDX_DIM ** -0.5)
        score = jnp.einsum('bqh,bqhs->bqs', wi_b.astype(jnp.float32) * (IDX_HEADS ** -0.5),
                           jax.nn.relu(dots))
        score = jnp.where(admissible[None], score, -jnp.inf)
        _, idx = lax.top_k(score, topk)
        valid = (idx // CHUNK) <= qchunk[None, :, None]
        k_sel = jax.vmap(lambda a, i: a[i])(k, idx)
        v_sel = jax.vmap(lambda a, i: a[i])(v, idx)
        bias = rel_tab[rel_bucket(idx - qpos[None, :, None])]
        logits = (jnp.einsum('bqhd,bqkhd->bqhk', q_b, k_sel).astype(jnp.float32)
                  * (DSA_HEAD_DIM ** -0.5) + jnp.moveaxis(bias, -1, 2).astype(jnp.float32))
        logits = jnp.where(valid[:, :, None, :], logits, NEG_INF)
        p = jax.nn.softmax(logits, axis=-1)
        return jnp.einsum('bqhk,bqkhd->bqhd', p.astype(v.dtype), v_sel)

    outs = lax.map(one_block, (to_blocks(qi), to_blocks(wi), to_blocks(q), jnp.arange(nblk)))
    return jnp.moveaxis(outs, 0, 1).reshape(bsz, seq, DSA_HEADS * DSA_HEAD_DIM)

def pool_mixer(z, w, scale):
    bsz, seq = z.shape[:2]
    zf = z.astype(jnp.float32)
    cs = jnp.cumsum(zf, axis=1)
    count = jnp.arange(1, seq + 1, dtype=jnp.float32)[:, None]
    outs = []
    for g, win in enumerate(POOL_WINDOWS):
        sl = slice(g * POOL_DG, (g + 1) * POOL_DG)
        c_g = cs[..., sl]
        lower = jnp.pad(c_g, ((0, 0), (win, 0), (0, 0)))[:, :seq]
        outs.append((c_g - lower) / jnp.minimum(count, win) - zf[..., sl])
    pooled = jnp.concatenate(outs, axis=-1).astype(z.dtype).reshape(bsz, seq, POOL_GROUPS, POOL_DG)
    y = jnp.einsum('bsgc,gcd->bsgd', pooled, w).reshape(bsz, seq, W_GROUP)
    return y * scale

def _shift_chunks(a, s):
    if s == 0:
        return a
    pad = [(0, 0)] * a.ndim
    pad[1] = (s, 0)
    return jnp.pad(a, pad)[:, :a.shape[1]]

def swa_mixer(q, k, v, sinks, rel_tab):
    bsz, seq = q.shape[:2]
    nc = seq // CHUNK
    nband = SWA_WINDOW // CHUNK
    gq = SWA_HEADS // SWA_KV_HEADS
    qc = q.reshape(bsz, nc, CHUNK, SWA_KV_HEADS, gq, SWA_HEAD_DIM)
    kc = k.reshape(bsz, nc, CHUNK, SWA_KV_HEADS, SWA_HEAD_DIM)
    vc = v.reshape(bsz, nc, CHUNK, SWA_KV_HEADS, SWA_HEAD_DIM)
    kb = jnp.concatenate([_shift_chunks(kc, s) for s in range(nband - 1, -1, -1)], axis=2)
    vb = jnp.concatenate([_shift_chunks(vc, s) for s in range(nband - 1, -1, -1)], axis=2)
    i = jnp.arange(CHUNK)[:, None]
    j = jnp.arange(nband * CHUNK)[None, :]
    rel = j - (nband - 1) * CHUNK - i
    bias = jnp.moveaxis(rel_tab[rel_bucket(rel)], -1, 0).reshape(
        SWA_KV_HEADS, gq, CHUNK, nband * CHUNK).astype(jnp.float32)
    logits = (jnp.einsum('bnqkgd,bnjkd->bnkgqj', qc, kb).astype(jnp.float32)
              * (SWA_HEAD_DIM ** -0.5) + bias)
    key_chunk = jnp.arange(nc)[:, None] - (nband - 1) + (jnp.arange(nband * CHUNK) // CHUNK)[None, :]
    logits = jnp.where((key_chunk >= 0)[None, :, None, None, None, :], logits, NEG_INF)
    sink = sinks.astype(jnp.float32).reshape(SWA_KV_HEADS, gq)[:, :, None, None]
    m = jnp.maximum(logits.max(-1, keepdims=True), sink)
    e = jnp.exp(logits - m)
    p = e / (e.sum(-1, keepdims=True) + jnp.exp(sink - m))
    out = jnp.einsum('bnkgqj,bnjkd->bnqkgd', p.astype(v.dtype), vb)
    return out.reshape(bsz, seq, SWA_HEADS * SWA_HEAD_DIM)

def conv_glu(h, w_up, conv_w, conv_b, w_down):
    a, gate = jnp.split(h @ w_up, 2, axis=-1)
    a = lax.conv_general_dilated(a, conv_w[:, None, :], window_strides=(1,),
                                 padding=((CONV_WIDTH - 1, 0),),
                                 dimension_numbers=('NWC', 'WIO', 'NWC'),
                                 feature_group_count=D_FF) + conv_b
    return (jax.nn.gelu(a) * gate) @ w_down

def setup_inputs(seed: int = 0) -> dict:
    key = jax.random.key(seed)
    ks = jax.random.split(key, 20)

    def nrm(k, shape, s):
        return jax.random.normal(k, shape, jnp.float32) * s

    return {
        "x": nrm(ks[0], (BATCH, SEQ, D_MODEL), 1.0),
        "c": nrm(ks[1], (BATCH, D_MODEL), 1.0),
        "w_ada": nrm(ks[2], (DEPTH, D_MODEL, 6 * D_MODEL), 0.5 * D_MODEL ** -0.5),
        "b_ada": nrm(ks[3], (DEPTH, 6 * D_MODEL), 0.01),
        "norm1_g": 1.0 + nrm(ks[4], (DEPTH, D_MODEL), 0.02),
        "norm2_g": 1.0 + nrm(ks[5], (DEPTH, D_MODEL), 0.02),
        "w_in": nrm(ks[6], (DEPTH, D_MODEL, N_IN), D_MODEL ** -0.5),
        "gmlp_ws": nrm(ks[7], (DEPTH, GMLP_GROUPS, GMLP_CHUNK, GMLP_CHUNK), GMLP_CHUNK ** -0.5),
        "gmlp_bs": 1.0 + nrm(ks[8], (DEPTH, GMLP_GROUPS, GMLP_CHUNK), 0.02),
        "pool_w": nrm(ks[9], (DEPTH, POOL_GROUPS, POOL_DG, POOL_DG), POOL_DG ** -0.5),
        "pool_scale": 0.5 + nrm(ks[10], (DEPTH, W_GROUP), 0.1),
        "swa_sinks": nrm(ks[11], (DEPTH, SWA_HEADS), 0.5),
        "rel_bias": nrm(ks[12], (REL_BUCKETS, DSA_HEADS + SWA_HEADS), 0.5),
        "mix_out_g": 1.0 + nrm(ks[13], (DEPTH, D_MIX), 0.02),
        "w_out": nrm(ks[14], (DEPTH, D_MIX, D_MODEL), D_MIX ** -0.5),
        "ffn_w_up": nrm(ks[15], (DEPTH, D_MODEL, 2 * D_FF), D_MODEL ** -0.5),
        "ffn_conv_w": nrm(ks[16], (DEPTH, CONV_WIDTH, D_FF), CONV_WIDTH ** -0.5),
        "ffn_conv_b": nrm(ks[17], (DEPTH, D_FF), 0.01),
        "ffn_w_down": nrm(ks[18], (DEPTH, D_FF, D_MODEL), D_FF ** -0.5),
        "final_g": 1.0 + nrm(ks[19], (D_MODEL,), 0.02),
    }

def reference(x, c, w_ada, b_ada, norm1_g, norm2_g, w_in, gmlp_ws, gmlp_bs, pool_w, pool_scale,
              swa_sinks, rel_bias, mix_out_g, w_out, ffn_w_up, ffn_conv_w, ffn_conv_b, ffn_w_down,
              final_g):
    bsz, seq, _ = x.shape
    offs = np.cumsum(IN_WIDTHS)[:-1].tolist()
    cond = jax.nn.silu(c)
    for l in range(DEPTH):
        mod = cond @ w_ada[l] + b_ada[l]
        sh1, sc1, g1, sh2, sc2, g2 = [m[:, None, :] for m in jnp.split(mod, 6, axis=-1)]

        h = rms_norm(x, norm1_g[l]) * (1.0 + sc1) + sh1
        z = h @ w_in[l]
        za, zq, zk, zv, zqi, zki, zwi, zc, zdq, zdk, zdv = jnp.split(z, offs, axis=-1)
        ya = gmlp_mixer(za, gmlp_ws[l], gmlp_bs[l])
        yb = dsa_mixer(zq.reshape(bsz, seq, DSA_HEADS, DSA_HEAD_DIM),
                       zk.reshape(bsz, seq, DSA_HEADS, DSA_HEAD_DIM),
                       zv.reshape(bsz, seq, DSA_HEADS, DSA_HEAD_DIM),
                       zqi.reshape(bsz, seq, IDX_HEADS, IDX_DIM), zki, zwi,
                       rel_bias[:, :DSA_HEADS])
        yc = pool_mixer(zc, pool_w[l], pool_scale[l])
        yd = swa_mixer(zdq.reshape(bsz, seq, SWA_HEADS, SWA_HEAD_DIM),
                       zdk.reshape(bsz, seq, SWA_KV_HEADS, SWA_HEAD_DIM),
                       zdv.reshape(bsz, seq, SWA_KV_HEADS, SWA_HEAD_DIM),
                       swa_sinks[l], rel_bias[:, DSA_HEADS:])
        y = _rms(jnp.stack([ya, yb, yc, yd], axis=2)).reshape(bsz, seq, D_MIX) * mix_out_g[l]
        x = x + g1 * (y @ w_out[l])

        h = rms_norm(x, norm2_g[l]) * (1.0 + sc2) + sh2
        x = x + g2 * conv_glu(h, ffn_w_up[l], ffn_conv_w[l], ffn_conv_b[l], ffn_w_down[l])
    return rms_norm(x, final_g)


_drawn_inputs = setup_inputs


def setup_inputs(seed=0):
    import zlib

    import numpy as np

    out = dict(_drawn_inputs(seed))
    spreads = {}
    factors = {'b_ada': 3.544,
     'norm1_g': 5.956,
     'norm2_g': 8.0,
     'gmlp_bs': 8.0,
     'swa_sinks': 8.0,
     'mix_out_g': 8.0,
     'ffn_conv_b': 8.0,
     'final_g': 2.83}
    for name, (base, spread) in spreads.items():
        noise = np.random.default_rng([zlib.crc32(name.encode()), seed]).standard_normal(out[name].shape)
        drawn = base * np.exp(spread * noise) if base else spread * noise
        out[name] = __import__('jax').numpy.asarray(drawn.astype(out[name].dtype))
    for name, factor in factors.items():
        out[name] = (out[name] * factor).astype(out[name].dtype)
    return out
```

```python
from contextlib import ExitStack

import numpy as np

import concourse.bass as bass
from concourse import mybir

F32 = mybir.dt.float32
F32R = mybir.dt.float32r
ALU = mybir.AluOpType
ACT = mybir.ActivationFunctionType
AX = mybir.AxisListType.X

P = 128
D = 1024
S = 1024
KD = D // P
NBLK = S // P
HALF = 512
HB = HALF // P
W = 256
DFF = 2816
NF = DFF // P
GROUPS = (8, 8, 6)
EPS = 1e-6
NEG = -1e30
IDX_HEADS, IDX_DIM = 8, 32
HEADS, HD = 4, 64
TOPK = 256
ROUNDS = TOPK // 8
NO_KEY = -3.0e38
TAKEN = -3.4e38
TAKEN_BELOW = -3.2e38

U_QI, U_KIWI, U_Q, U_K, U_V, U_C, U_DQ, U_DK, U_DV, U_A = 0, 2, 3, 5, 7, 9, 11, 13, 14, 15
N_IN = 19
N_OUT = KD
N_FFN = 2 * NF + len(GROUPS) * KD
N_HALF = N_OUT + N_FFN
N_UNITS = N_IN + N_HALF
WI_COL = 32
TOP_BLOCKS = range(2, NBLK)
LATE_BLOCKS = range(HB, NBLK)

BASE = 16512


def score_columns():
    at, n = {}, 0
    for b in TOP_BLOCKS:
        at[b] = n
        n += P * (b + 1)
    return at, n


def dot_chunks():
    return [(b, k0, min(512, P * (b + 1) - k0), h)
            for b in TOP_BLOCKS for k0 in range(0, P * (b + 1), 512) for h in range(IDX_HEADS)]


def build(nc, a, out):
    with ExitStack() as ctx:
        def at(name, shape, offset):
            return nc.alloc_sbuf_tensor_at(name, shape, F32, offset=BASE + offset)

        def sem(name):
            return ctx.enter_context(nc.semaphore(name))

        RA, RB, RC, RD, RE, RG, RH = 0, 65536, 98304, 131072, 155648, 163840, 180736
        RM = RH + 24576
        w_ada0 = at("w_ada0", [P, KD, 2 * D], RA)
        h_hi = at("h_hi", [P, KD, S], RA)
        h_lo = at("h_lo", [P, KD, S], RA + 32768)
        pooled = at("pooled", [P, 2, S], RA)
        win_a = at("win_a", [P, 16 + S], RA + 8192)
        win_b = at("win_b", [P, 16 + S], RA + 12352)
        vn = at("vn", [P, NBLK, W], RA + 16512)
        gm = at("gm", [P, NBLK, 2 * W], RA + 24704)
        gm_sq = at("gm_sq", [P, NBLK, W], RA + 41088)
        y_hi = at("y_hi", [P, KD, HALF], RA)
        y_lo = at("y_lo", [P, KD, HALF], RA + 16384)
        act_hi = at("act_hi", [P, 8, HALF], RA)
        act_lo = at("act_lo", [P, 8, HALF], RA + 16384)
        out_t = at("out_t", [P, KD, HALF], RA + 32768)
        bias_t = at("bias_t", [P, HEADS, S], RA + 49152)
        xn2 = at("xn2", [P, HB, D], RA + 49152)
        conv_in = at("conv_in", [P, 2 + HALF], RA + 49152)
        conv_t = at("conv_t", [P, HALF], RA + 53248)
        act_f = at("act_f", [P, HALF], RA + 57344)
        fin_g = at("fin_g", [P, D], RA + 49152)
        fin_o = at("fin_o", [P, 2, D], RA + 53248)
        qi = at("qi", [P, 2, S], RB)
        ki = at("ki", [P, S], RB + 8192)
        dq = at("dq", [P, 2, S], RB + 12288)
        dk = at("dk", [P, S], RB + 20480)
        dv = at("dv", [P, NBLK, P], RB + 24576)
        swa_bias = at("swa_bias", [P, HEADS, 2 * P], RB + 28672)
        p_t = at("p_t", [P, 2, NBLK, P], RB)
        h2_hi = at("h2_hi", [P, KD, HALF], RB)
        h2_lo = at("h2_lo", [P, KD, HALF], RB + 16384)
        x_sb = at("x_sb", [P, NBLK, D], RC)
        za_t = at("za_t", [P, 4, S], RC)
        kiwi = at("kiwi", [P, S], RC)
        stage = [at("stage_0", [P, S], RC + 24704), at("stage_1", [P, S], RC + 4096)]
        relu_r = at("relu_r", [P, 4, 512], RC + 8192)
        zc = [at("zc_0", [P, 16 + S], RC + 16384), at("zc_1", [P, 16 + S], RC + 20544)]
        y = at("y", [P, NBLK, D], RC)
        x2 = [at(f"x2_{h}", [P, HB, D], RC + 16384 * h) for h in range(2)]
        q = at("q", [P, 2, S], RD)
        k = at("k", [P, 2, S], RD + 8192)
        v = at("v", [P, NBLK, W], RD + 16384)
        w_ada1 = at("w_ada1", [P, 2, KD, P], RE)
        logit = at("logit", [P, 2, S], RE)
        junk = at("junk", [P, D], RD)
        nt_tmp = [at("nt_tmp_x", [P, 2, HALF], RG + 9216), at("nt_tmp", [P, 2, HALF], RE)]
        junk2 = at("junk2", [P, D], RE + 4096)
        onehot = at("onehot", [32, S + P], RG)
        fbias = at("fbias", [HEADS * 2, S + P], RG + 4608)
        SC, n_sc = score_columns()
        score = at("score", [P, n_sc], RG)
        w_raw = at("w_raw", [P, 2, KD, P], RH)
        w_hi = at("w_hi", [P, 2, KD, P], RH + 8192)
        w_lo = at("w_lo", [P, 2, KD, P], RH + 16384)

        small_at = [RM]

        def small(name, shape):
            t = at(name, shape, small_at[0])
            small_at[0] += -(-4 * int(np.prod(shape[1:])) // 32) * 32
            assert BASE + small_at[0] <= 229344, small_at[0]
            return t

        ident = small("ident", [P, P])
        ws_t = small("ws_t", [P, 4, P])
        pool_w = small("pool_w", [P, 2, 64])
        pool_s = small("pool_s", [P, W])
        pool_c = small("pool_c", [P, 2, 16])
        b_ada = small("b_ada", [P, 48])
        norm_g = small("norm_g", [P, 2, KD])
        mix_g = small("mix_g", [P, KD])
        conv_w = small("conv_w", [P, NF, 4])
        gm_b = small("gm_b", [P, 4])
        sinks = small("sinks", [P, HEADS])
        rel = small("rel", [32, 8])
        c_col = small("c_col", [P, KD])
        cond = small("cond", [P, KD])
        mod = small("mod", [P, 48])
        scale_g = small("scale_g", [P, 2, KD])
        halo = small("halo", [P, NF, 2])
        eps = small("eps", [P, 1])
        st = small("st", [P, 32])
        st2 = small("st2", [P, 32])
        st3 = small("st3", [P, 32])
        wis = small("wis", [P, len(TOP_BLOCKS), IDX_HEADS])
        tick = small("tick", [P, 1])
        top8 = small("top8", [P, len(TOP_BLOCKS), 8])
        sm_max = small("sm_max", [P, 2, HEADS])
        sm_neg = small("sm_neg", [P, 2, HEADS])
        sm_sum = small("sm_sum", [P, 2, HEADS])
        sm_snk = small("sm_snk", [P, 2, HEADS])
        sm_rec = small("sm_rec", [P, 2, HEADS])

        ps = ctx.enter_context(nc.psum_tensor("ps", [P, 8, 512], F32))

        def r(ap):
            return ap.bitcast(F32R)

        f_dram = nc.dram_tensor("f_dram", (8, S + P), F32, kind="Internal")
        bias_rows = bass.AP(tensor=f_dram, offset=0, ap=[[1, P], [S + P, HEADS], [1, S]])

        def backwards(ap):
            *dims, (step, n) = ap.ap
            return bass.AP(tensor=ap.tensor, offset=ap.offset + step * (n - 1), ap=[*dims, [-step, n]])

        s_par = sem("s_par")
        s_rel = sem("s_rel")
        s_x = [sem(f"s_x{i}") for i in range(2)]
        s_aw0 = [sem(f"s_aw0{i}") for i in range(4)]
        s_aw1 = [sem(f"s_aw1{i}") for i in range(2)]
        s_eps = sem("s_eps")
        s_cond = sem("s_cond")
        s_ada = sem("s_ada")
        s_mod = sem("s_mod")
        s_f, s_fs, s_fd, s_tb, s_swb = sem("s_f"), sem("s_fs"), sem("s_fd"), sem("s_tb"), sem("s_swb")
        s_ss, s_sd, s_xn = sem("s_ss"), sem("s_sd"), sem("s_xn")
        s_nt, s_ne, s_nh, s_nl = sem("s_nt"), sem("s_ne"), sem("s_nh"), sem("s_nl")
        s_raw = [sem(f"s_raw{i}") for i in range(2)]
        s_whi, s_wlo, s_gemm = sem("s_whi"), sem("s_wlo"), sem("s_gemm")
        s_ev = sem("s_ev")
        s_wi, s_wis = sem("s_wi"), sem("s_wis")
        s_dot, s_relu, s_acc = sem("s_dot"), sem("s_relu"), sem("s_acc")
        s_max, s_rep = sem("s_max"), sem("s_rep")
        s_vt, s_ve = sem("s_vt"), sem("s_ve")
        s_gt, s_ge = sem("s_gt"), sem("s_ge")
        s_lnv, s_lns, s_vn = sem("s_lnv"), sem("s_lns"), sem("s_vn")
        s_gs, s_gy = sem("s_gs"), sem("s_gy")
        s_pad, s_pl, s_pm, s_py = sem("s_pad"), sem("s_pl"), sem("s_pm"), sem("s_py")
        s_wl, s_wm, s_wx, s_wt, s_we, s_wo, s_wy = (sem(f"s_w_{x}") for x in "l m x t e o y".split())
        s_al, s_am, s_ax, s_at, s_ae, s_ao, s_ay = (sem(f"s_a_{x}") for x in "l m x t e o y".split())
        s_yq, s_yr, s_yn = sem("s_yq"), sem("s_yr"), sem("s_yn")
        s_x2 = sem("s_x2")
        s_dev = [sem(f"s_dev{i}") for i in range(2)]
        s_rt, s_rd = sem("s_rt"), sem("s_rd")
        s_q2, s_r2, s_n2 = sem("s_q2"), sem("s_r2"), sem("s_n2")
        s_hin = sem("s_hin")
        s_cin, s_conv, s_gelu, s_act, s_ahi, s_alo, s_c1 = (
            sem(f"s_{x}") for x in "cin conv gelu act ahi alo c1".split())
        s_fg, s_fo, s_out = sem("s_fg"), sem("s_fo"), [sem(f"s_out{i}") for i in range(2)]
        s_vc, s_sc_, s_pc = sem("s_vchain"), sem("s_schain"), sem("s_pchain")

        DOTS = dot_chunks()
        chain = {}

        def link(eng, s, ins):
            chain[s.name] = chain.get(s.name, 0) + 1
            ins.then_inc(s, 1)
            eng.wait_ge(s, chain[s.name])

        def half_base(h):
            return N_IN + N_HALF * h

        def group_bases(h):
            n, f, res = half_base(h) + N_OUT, 0, []
            for g, nf in enumerate(GROUPS):
                res.append((g, nf, n, n + 2 * nf, f))
                n += 2 * nf + KD
                f += nf
            return res

        N_SEQ = N_IN + 2 * N_HALF

        def raw_ready(n):
            return s_raw[n % 2], 16 * (n // 2 + 1)

        block = ctx.enter_context(nc.Block())

        @block.sync
        def _(sp):
            sp.dma_start(rel[:], a["rel_bias"]).then_inc(s_rel, 16)
            sp.dma_start(onehot[:], a["onehot"]).then_inc(s_rel, 16)
            for name, dst in (("c", c_col), ("b_ada", b_ada), ("norm_g", norm_g), ("mix_g", mix_g),
                              ("conv_w", conv_w), ("gm_b", gm_b), ("ident", ident), ("ws_t", ws_t),
                              ("pool_w", pool_w), ("pool_c", pool_c)):
                sp.dma_start(dst[:], a[name]).then_inc(s_par, 16)
            sp.dma_start(sinks[:], a["sinks"].partition_broadcast(P)).then_inc(s_par, 16)
            sp.dma_start(pool_s[:], a["pool_s"].partition_broadcast(P)).then_inc(s_par, 16)
            for i in range(4):
                sp.dma_start(w_ada0[:, :, 512 * i:512 * i + 512],
                             a["w_ada"].rearrange("(p j) n -> p j n", p=P)[:, :, 512 * i:512 * i + 512]
                             ).then_inc(s_aw0[i], 16)
                if i < 2:
                    xs = a["x"].rearrange("(t p) d -> p t d", p=P)
                    sp.dma_start(x_sb[:, 4 * i:4 * i + 4, :], xs[:, 4 * i:4 * i + 4, :]).then_inc(s_x[i], 16)
            w = a["w"].rearrange("u p k c -> u p (k c)")

            def load(n):
                if n >= 2:
                    sp.wait_ge(s_wlo, n - 1)
                sp.dma_start(w_raw[:, n % 2], w[n]).then_inc(s_raw[n % 2], 16)

            load(0)
            load(1)
            for n in range(16):
                for c in (16 + 2 * n, 17 + 2 * n):
                    if c >= 18:
                        sp.wait_ge(s_ada, c - 1)
                    sp.dma_start(w_ada1[:, c % 2],
                                 a["w_ada"].rearrange("(p j) n -> p j n", p=P)[:, :, P * c:P * c + P]
                                 ).then_inc(s_aw1[c % 2], 16)
                load(n + 2)
            load(18)
            for h in range(2):
                nb = half_base(h)
                with sp.Fori(0, N_HALF // 2, 1) as i:
                    for j in range(2):
                        sp.wait_ge(s_wlo, nb + j - 1 + 2 * i)
                        sp.dma_start(w_raw[:, (nb + j) % 2], w[N_IN + j + 2 * i]
                                     ).then_inc(s_raw[(nb + j) % 2], 16)
            sp.wait_ge(s_wlo, N_SEQ - 1)
            sp.dma_start(w_raw[:, N_SEQ % 2], w[0]).then_inc(s_raw[N_SEQ % 2], 16)

        @block.gpsimd
        def _(pool):
            def w_lo_unit(slot, ready, i=None):
                pool.wait_ge(s_whi, ready)
                pool.tensor_tensor(r(w_lo[:, slot]), w_raw[:, slot], w_hi[:, slot],
                                   ALU.subtract).then_inc(s_wlo, 1)

            def lo(n):
                w_lo_unit(n % 2, n + 1)

            pool.memset(eps[:], EPS).then_inc(s_eps, 1)
            pool.memset(halo[:], 0.0).then_inc(s_eps, 1)
            pool.wait_ge(s_par, 16 * 12)
            pool.wait_ge(s_eps, 2)
            pool.memset(ws_t[64:128, :, 0:64], 0.0).then_inc(s_eps, 1)
            pool.wait_ge(s_eps, 3)
            lo(0)
            for n in range(N_IN):
                if n == U_C:
                    pool.wait_ge(s_nt, 16)
                    pool.memset(zc[0][:, 0:16], 0.0).then_inc(s_pad, 1)
                    pool.memset(zc[1][:, 0:16], 0.0).then_inc(s_pad, 1)
                lo(n + 1)
            pool.wait_ge(s_ev, U_C + 2)
            pool.wait_ge(s_gemm, N_IN)
            pool.wait_ge(s_pad, 2)

            def plink(ins):
                link(pool, s_pc, ins)

            for tile, first in ((0, 2), (1, 8)):
                src = zc[tile]
                bufs = [win_a, win_b]
                cur, win, n = src, 1, 0
                while win < 2 * first:
                    dst = bufs[n % 2]
                    lo_p = 64 if 2 * win == 2 * first else 0
                    plink(pool.tensor_tensor(dst[lo_p:P, 2 * win - 1:], cur[lo_p:P, 2 * win - 1:],
                                             cur[lo_p:P, win - 1:16 + S - win], ALU.add))
                    prev, cur = cur, dst
                    win, n = 2 * win, n + 1
                for p0, s_, wn in ((0, prev, first), (64, cur, 2 * first)):
                    rows = slice(p0, p0 + 64)
                    o = pooled[rows, tile]
                    plink(pool.tensor_tensor(o[:, 0:16], s_[rows, 16:32], pool_c[rows, tile], ALU.mult))
                    plink(pool.tensor_scalar(o[:, 16:], s_[rows, 32:], 1.0 / wn, None, ALU.mult))
                    ins = pool.tensor_tensor(o, o, src[rows, 16:], ALU.subtract)
                    if (tile, p0) == (1, 64):
                        ins.then_inc(s_pl, 1)
                    else:
                        plink(ins)

            pool.wait_ge(s_pl, 1)
            for h in range(2):
                nb = half_base(h)

                def pairs(base, count):
                    with pool.Fori(0, count, 1) as i:
                        for j in (1, 2):
                            w_lo_unit((base + j) % 2, base + j + 1 + 2 * i)

                pairs(nb, N_OUT // 2)
                for g, nf, nu, nd, f0 in group_bases(h):
                    F = 1 + NF * h + f0
                    with pool.Fori(0, nf, 1) as i:
                        for j in (1, 2):
                            w_lo_unit((nu + j) % 2, nu + j + 1 + 2 * i)
                        pool.wait_ge(s_ahi, F + 1 + i)
                        pool.tensor_tensor(r(act_lo[:, i]), act_f[:], act_hi[:, i],
                                           ALU.subtract).then_inc(s_alo, 1)
                    pairs(nd, KD // 2)

        @block.scalar
        def _(act):
            def slink(ins):
                link(act, s_sc_, ins)

            def split_hi(slot, ready_sem, ready, used):
                act.wait_ge(ready_sem, ready)
                if used is not None:
                    act.wait_ge(s_gemm, used)
                act.activation(r(w_hi[:, slot]), w_raw[:, slot], ACT.Copy).then_inc(s_whi, 1)

            def hi(n):
                rs, rv = raw_ready(n)
                split_hi(n % 2, rs, rv, n - 1 if n >= 2 else None)

            def hi_in(n, i):
                rs, rv = raw_ready(n)
                split_hi(n % 2, rs, rv + 16 * i, n - 1 + 2 * i)

            act.wait_ge(s_par, 16 * 12)
            act.activation(cond[:], c_col[:], ACT.Silu).then_inc(s_cond, 1)
            act.wait_ge(s_f, 1)
            act.activation(fbias[:].rearrange("p (a b) -> p a b", a=3), ps[0:8, 4:7, 0:384],
                           ACT.Copy).then_inc(s_fs, 1)
            act.wait_ge(s_fs, 1)
            act.dma_start(f_dram.ap(), fbias[:]).then_inc(s_fd, 16)
            for t in range(NBLK):
                act.wait_ge(s_x[t // 4], 16)
                if t > 0:
                    act.wait_ge(s_ss, t)
                act.activation(junk[:], x_sb[:, t], ACT.Square, accum_out=st[:, t:t + 1]).then_inc(s_ss, 1)
            act.wait_ge(s_eps, 1)
            act.wait_ge(s_ss, NBLK)
            act.activation(st2[:, 0:NBLK], st[:, 0:NBLK], ACT.Sqrt, bias=eps[:], scale=1.0 / D).then_inc(s_sd, 1)

            def norm_evac(g0, scale, bias, groups, tmp):
                for g in range(groups):
                    act.wait_ge(s_nt, g0 + g + 1)
                    if g >= 2:
                        act.wait_ge(s_nl, g0 + g - 1)
                    act.activation(tmp[:, g % 2], ps[:, (g0 + g) % 4], ACT.Identity,
                                   bias=bias(g) if bias else 0.0, scale=scale(g)).then_inc(s_ne, 1)

            act.wait_ge(s_fd, 16)
            act.wait_ge(s_mod, 1)
            norm_evac(0, lambda g: scale_g[:, 0, g % KD:g % KD + 1], lambda g: mod[:, g % KD:g % KD + 1],
                      2 * KD, nt_tmp[0])

            act.dma_start(swa_bias[:], bass.AP(tensor=f_dram, offset=HEADS * (S + P), ap=[[1, P], [S + P, HEADS], [1, 2 * P]])).then_inc(s_swb, 16)

            dots_done = [0]

            def relus(b):
                while dots_done[0] < len(DOTS) and DOTS[dots_done[0]][0] == b:
                    i = dots_done[0]
                    n = DOTS[i][2]
                    act.wait_ge(s_dot, i + 1)
                    if i >= 4:
                        act.wait_ge(s_acc, i - 3)
                    act.activation(relu_r[:, i % 4, 0:n], ps[:, 4 + i % 2, 0:n], ACT.Relu,
                                   scale=IDX_DIM ** -0.5).then_inc(s_relu, 1)
                    dots_done[0] += 1

            def v_evac(g):
                act.wait_ge(s_vt, g + 1)
                col, blk = g // 2, HB * (g % 2)
                dst = v[:, blk:blk + HB, P * col:P * col + P] if col < 2 else dv[:, blk:blk + HB]
                act.activation(dst, ps[:, 6].rearrange("p (b c) -> p b c", b=HB), ACT.Copy).then_inc(s_ve, 1)

            def evac(n):
                act.wait_ge(s_gemm, n + 1)
                src = ps[:, 2 * (n % 2):2 * (n % 2) + 2].rearrange("p b c -> p (b c)")
                f = ACT.Copy
                if n == U_KIWI:
                    act.wait_ge(s_nt, 16)
                    for g in range(4):
                        act.activation(ki[32 * g:32 * g + 32], src[0:32], ACT.Copy)
                    dst = kiwi[:]
                elif n < U_KIWI:
                    dst = qi[:, n]
                elif n < U_K:
                    dst = q[:, n - U_Q]
                elif n < U_V:
                    dst = k[:, n - U_K]
                elif n < U_C:
                    dst = stage[n - U_V][:]
                elif n < U_DQ:
                    dst = zc[n - U_C][:, 16:]
                elif n < U_DK:
                    dst = dq[:, n - U_DQ]
                elif n == U_DK:
                    dst = dk[:]
                elif n == U_DV:
                    act.wait_ge(s_vt, 4)
                    dst = stage[0][:]
                else:
                    if n == U_A:
                        act.wait_ge(s_acc, len(DOTS))
                    dst, f = za_t[:, n - U_A], ACT.Gelu_apprx_tanh
                act.activation(dst, src, f).then_inc(s_ev, 1)

            hi(0)
            extra = {3: 2, 5: 3, 7: 4, 9: 5, 11: 6, 13: 7}
            for n in range(N_IN):
                hi(n + 1)
                evac(n)
                if n in extra:
                    relus(extra[n])
                if n == 10:
                    for g in range(4):
                        v_evac(g)
                if n == 16:
                    for g in range(4, 6):
                        v_evac(g)
            for b in range(NBLK):
                act.wait_ge(s_gt, b + 1)
                act.activation(gm[:, b], ps[:, 4 + b % 2], ACT.Copy).then_inc(s_ge, 1)
            act.wait_ge(s_lnv, 1)
            act.activation(st2[:, 0:32], st[:, 0:32], ACT.Sqrt, bias=eps[:], scale=1.0 / 64).then_inc(s_lns, 1)
            act.wait_ge(s_vn, 1)
            act.dma_start(bias_t[:], bias_rows).then_inc(s_tb, 16)

            for b in range(NBLK):
                c0 = P if b == 0 else 0
                act.wait_ge(s_wm, b + 1)
                lg = logit[:, b % 2].rearrange("p (h c) -> p h c", h=HEADS)
                for h in range(HEADS):
                    act.activation(lg[:, h, c0:], lg[:, h, c0:], ACT.Exp, bias=sm_neg[:, b % 2, h:h + 1],
                                   accum_out=sm_sum[:, b % 2, h:h + 1])
                act.activation(sm_snk[:, b % 2], sm_snk[:, b % 2], ACT.Exp).then_inc(s_wx, 1)
                for j in range(2):
                    act.wait_ge(s_wt, 2 * b + j + 1)
                    if b >= 2 and j == 0:
                        act.wait_ge(s_wo, b - 1)
                    src = ps[:, 6 if j == 0 else 1].rearrange("p (h c) -> p h c", h=4)
                    if c0:
                        act.activation(p_t[:, b % 2, 4 * j + 1:4 * j + 4:2], src[:, 1::2], ACT.Copy).then_inc(s_we, 1)
                    else:
                        act.activation(p_t[:, b % 2, 4 * j:4 * j + 4], src, ACT.Copy).then_inc(s_we, 1)

            n_pt = [0]
            for h in range(2):
                nb = half_base(h)
                if h == 1:
                    act.wait_ge(s_fo, HB)
                    for s_ in s_out:
                        act.wait_ge(s_, 16 * 2)
                    act.dma_start(bias_t[:], bias_rows).then_inc(s_tb, 16)
                for i in range(HB * HEADS):
                    b, hd = HB * h + i // HEADS, i % HEADS
                    I = HB * HEADS * h + i
                    n = P * (b + 1)
                    act.wait_ge(s_am, I + 1)
                    act.activation(logit[:, I % 2, 0:n], logit[:, I % 2, 0:n], ACT.Exp,
                                   bias=sm_neg[:, b % 2, hd:hd + 1],
                                   accum_out=sm_sum[:, b % 2, hd:hd + 1]).then_inc(s_ax, 1)
                    for t in range(0, b + 1, 4):
                        m = min(4, b + 1 - t)
                        act.wait_ge(s_at, n_pt[0] + 1)
                        if t == 0 and I >= 2:
                            act.wait_ge(s_ao, I - 1)
                        act.activation(p_t[:, I % 2, t:t + m],
                                       ps[:, 6 if n_pt[0] % 2 == 0 else 1].rearrange("p (h c) -> p h c", h=4)[:, 0:m],
                                       ACT.Copy).then_inc(s_ae, 1)
                        n_pt[0] += 1
                act.wait_ge(s_ay, HB * (h + 1))
                act.wait_ge(s_gy, NBLK)
                act.wait_ge(s_py, NBLK)
                act.wait_ge(s_wy, NBLK)
                for i in range(16):
                    act.wait_ge(s_yq, 16 * h + i)
                    act.activation(junk2[:, 0:W], y[:, HB * h + i // 4, W * (i % 4):W * (i % 4) + W], ACT.Square,
                                   accum_out=st[:, i:i + 1]).then_inc(s_yq, 1)
                act.wait_ge(s_yq, 16 * (h + 1))
                act.activation(st2[:, 0:16], st[:, 0:16], ACT.Sqrt, bias=eps[:], scale=1.0 / W).then_inc(s_yr, 1)
                g0 = 16 + 16 * h
                norm_evac(g0, lambda g: mix_g[:, g:g + 1], None, KD, nt_tmp[1])
                act.wait_ge(s_nt, g0 + KD)
                act.dma_start(x2[h][:], a["x"].rearrange("(t p) d -> p t d", p=P)[:, HB * h:HB * h + HB, :]
                              ).then_inc(s_x2, 16)

                def evac_loop(base, J0, gate, write):
                    with act.Fori(0, KD // 2, 1) as i:
                        for j in range(2):
                            hi_in(base + 1 + j, i)
                            if write:
                                act.wait_ge(s_gemm, base + 1 + j + 2 * i)
                                act.activation(out_t[:, j + 2 * i], ps[:, 2 + j], ACT.Copy,
                                               scale=mod[:, bass.ds(gate + j + 2 * i, 1)]
                                               ).then_inc(s_dev[j], 1)

                act.wait_ge(s_mod, 2)
                evac_loop(nb, 0, 2 * KD, True)

                def row_norm(hh):
                    for t in range(HB):
                        act.wait_ge(s_q2, HB * (2 * h + hh) + t)
                        act.activation(junk2[:], x2[h][:, t], ACT.Square, accum_out=st[:, t:t + 1]).then_inc(s_q2, 1)
                    act.wait_ge(s_q2, HB * (2 * h + hh + 1))
                    act.activation(st2[:, 0:HB], st[:, 0:HB], ACT.Sqrt, bias=eps[:], scale=1.0 / D).then_inc(s_r2, 1)

                act.wait_ge(s_rd, 16 * h + 8)
                row_norm(0)
                norm_evac(g0 + KD, lambda g: scale_g[:, 1, g:g + 1],
                          lambda g: mod[:, 3 * KD + g:3 * KD + g + 1], KD, nt_tmp[1])
                for g, nf, nu, nd, f0 in group_bases(h):
                    F = 1 + NF * h + f0
                    with act.Fori(0, nf, 1) as i:
                        hi_in(nu + 1, i)
                        act.wait_ge(s_gemm, nu + 1 + 2 * i)
                        act.wait_ge(s_conv, F + i)
                        act.activation(conv_in[:, 0:2], halo[:, f0 + i], ACT.Copy).then_inc(s_hin, 1)
                        act.activation(conv_t[:], ps[:, 0], ACT.Identity, bias=conv_w[:, f0 + i, 3:4],
                                       scale=conv_w[:, f0 + i, 2:3])
                        act.wait_ge(s_hin, F + 1 + i)
                        act.activation(conv_in[:, 2:], ps[:, 0], ACT.Copy)
                        act.activation(halo[:, f0 + i], ps[:, 0, HALF - 2:], ACT.Copy).then_inc(s_cin, 1)
                        hi_in(nu + 2, i)
                        act.wait_ge(s_conv, F + 1 + i)
                        act.activation(conv_t[:], conv_t[:], ACT.Gelu_apprx_tanh).then_inc(s_gelu, 1)
                        act.wait_ge(s_act, F + 1 + i)
                        act.activation(r(act_hi[:, i]), act_f[:], ACT.Copy).then_inc(s_ahi, 1)
                    evac_loop(nd, 8 + 8 * g, 5 * KD, g == 0)
                act.dma_start(fin_g[:], a["final_g"].partition_broadcast(P)).then_inc(s_fg, 16)
                act.wait_ge(s_rd, 16 * h + 16)
                row_norm(1)
                for t in range(HB):
                    act.wait_ge(s_fo, HB * h + t + 1)
                    act.dma_start(out.rearrange("(t p) d -> p t d", p=P)[:, HB * h + t, :], fin_o[:, t % 2]
                                  ).then_inc(s_out[t % 2], 16)
            for s_ in s_out:
                act.wait_ge(s_, 16 * 4)

        @block.vector
        def _(dve):
            def vlink(ins):
                link(dve, s_vc, ins)

            dve.wait_ge(s_par, 16 * 12)
            dve.wait_ge(s_sd, 1)
            vlink(dve.reciprocal(st3[:, 0:NBLK], st2[:, 0:NBLK]))
            for t in range(NBLK):
                dve.tensor_scalar(x_sb[:, t], x_sb[:, t], st3[:, t:t + 1], None, ALU.mult).then_inc(s_xn, 1)
            dve.wait_ge(s_ada, 16)
            vlink(dve.tensor_tensor(mod[:, 0:16], ps[:, 7, 0:16], b_ada[:, 0:16], ALU.add))
            vlink(dve.tensor_scalar(scale_g[:, 0], mod[:, KD:2 * KD], 1.0, None, ALU.add))
            dve.tensor_tensor(scale_g[:, 0], scale_g[:, 0], norm_g[:, 0], ALU.mult).then_inc(s_mod, 1)

            def norm_split(g0, groups, tmp, hi_t, lo_t):
                for g in range(groups):
                    dve.wait_ge(s_ne, g0 + g + 1)
                    dve.tensor_copy(r(hi_t(g)), tmp[:, g % 2]).then_inc(s_nh, 1)
                    dve.wait_ge(s_nh, g0 + g + 1)
                    dve.tensor_tensor(r(lo_t(g)), tmp[:, g % 2], hi_t(g), ALU.subtract).then_inc(s_nl, 1)

            def hcols(t):
                return lambda g: t[:, g % KD, HALF * (g // KD):HALF * (g // KD) + HALF]

            norm_split(0, 2 * KD, nt_tmp[0], hcols(h_hi), hcols(h_lo))

            dve.wait_ge(s_wi, 1)
            dve.tensor_scalar(wis[:], ps[:, 6, 0:48].rearrange("p (b h) -> p b h", b=6), IDX_HEADS ** -0.5, None,
                              ALU.mult).then_inc(s_wis, 1)
            dve.wait_ge(s_wis, 1)
            done = [0]

            def accumulate(b):
                while done[0] < len(DOTS) and DOTS[done[0]][0] == b:
                    i = done[0]
                    _, k0, n, h = DOTS[i]
                    dst = score[:, SC[b] + k0:SC[b] + k0 + n]
                    wgt = wis[:, b - 2, h:h + 1]
                    dve.wait_ge(s_relu, i + 1)
                    if h == 0:
                        dve.tensor_scalar(dst, relu_r[:, i % 4, 0:n], wgt, None, ALU.mult).then_inc(s_acc, 1)
                    else:
                        dve.wait_ge(s_acc, i)
                        dve.scalar_tensor_tensor(out=dst, in0=relu_r[:, i % 4, 0:n], scalar=wgt, in1=dst,
                                                 op0=ALU.mult, op1=ALU.add).then_inc(s_acc, 1)
                    done[0] += 1
                dve.wait_ge(s_acc, done[0])
                vlink(dve.memset(score[0:64, SC[b] + P * (b + 1) - 64:SC[b] + P * (b + 1)], NO_KEY))

            def sc_of(b):
                return score[:, SC[b]:SC[b] + P * (b + 1)]

            def wait_apart(s_, value):
                dve.wait_ge(s_, value)
                dve.memset(tick[:], 0.0)

            def top_round(blocks, base):
                m = len(blocks)
                wait_apart(s_rep, base)
                for b in blocks:
                    dve.max(top8[:, b - 2], sc_of(b)).then_inc(s_max, 1)
                wait_apart(s_max, base + m)
                for b in blocks:
                    dve.match_replace(sc_of(b), top8[:, b - 2], sc_of(b), TAKEN).then_inc(s_rep, 1)

            def top_single(b, base):
                with dve.Fori(0, ROUNDS, 1) as i:
                    top_round([b], base + i)

            def mask_of(b):
                vlink(dve.tensor_scalar(sc_of(b), sc_of(b), TAKEN_BELOW, NEG, ALU.is_gt, ALU.mult))

            accumulate(2)
            top_single(2, 0)
            dve.wait_ge(s_rep, ROUNDS)
            mask_of(2)
            accumulate(3)
            top_single(3, ROUNDS)
            dve.wait_ge(s_rep, 2 * ROUNDS)
            mask_of(3)
            for b in LATE_BLOCKS:
                accumulate(b)
            dve.wait_ge(s_ada, 48)
            vlink(dve.tensor_tensor(mod[:, 16:48], ps[:, 7, 16:48], b_ada[:, 16:48], ALU.add))
            vlink(dve.tensor_scalar(scale_g[:, 1], mod[:, 4 * KD:5 * KD], 1.0, None, ALU.add))
            dve.tensor_tensor(scale_g[:, 1], scale_g[:, 1], norm_g[:, 1], ALU.mult).then_inc(s_mod, 1)

            dve.wait_ge(s_ge, NBLK)
            v4 = gm[:, :, W:]
            mean = st3[:, 0:32]

            def g64(ap):
                return ap.rearrange("p b (g c) -> p b g c", c=64)

            def per_g(ap):
                return ap.rearrange("p (b g) -> p b g", g=4)

            for b in range(NBLK):
                ins = dve.tensor_reduce(st3[:, 4 * b:4 * b + 4], v4[:, b].rearrange("p (g c) -> p g c", c=64), AX, ALU.add)
            vlink(ins)
            vlink(dve.tensor_scalar(mean, mean, 1.0 / 64, None, ALU.mult))
            for b in range(NBLK):
                ins = dve.tensor_tensor(vn[:, b].rearrange("p (g c) -> p g c", c=64),
                                        v4[:, b].rearrange("p (g c) -> p g c", c=64),
                                        st3[:, 4 * b:4 * b + 4].unsqueeze(2).to_broadcast([P, 4, 64]), ALU.subtract)
            vlink(ins)
            vlink(dve.tensor_tensor(gm_sq[:], vn[:], vn[:], ALU.mult))
            for b in range(NBLK):
                ins = dve.tensor_reduce(st[:, 4 * b:4 * b + 4], gm_sq[:, b].rearrange("p (g c) -> p g c", c=64), AX, ALU.add)
            ins.then_inc(s_lnv, 1)
            dve.wait_ge(s_lns, 1)
            vlink(dve.reciprocal(st3[:, 0:32], st2[:, 0:32]))
            for b in range(NBLK):
                x_ = vn[:, b].rearrange("p (g c) -> p g c", c=64)
                ins = dve.tensor_tensor(x_, x_, st3[:, 4 * b:4 * b + 4].unsqueeze(2).to_broadcast([P, 4, 64]), ALU.mult)
            ins.then_inc(s_vn, 1)

            dve.wait_ge(s_swb, 16)
            vlink(dve.memset(swa_bias[:, :, 192:256], NEG))
            vlink(dve.memset(swa_bias[64:128, :, 128:192], NEG))
            vlink(dve.memset(swa_bias[0:64, :, 0:64], NEG))

            def swa_softmax(b):
                c0 = P if b == 0 else 0
                lg = logit[:, b % 2].rearrange("p (h c) -> p h c", h=HEADS)
                src = ps[:, 4 - 2 * (b % 2):6 - 2 * (b % 2)].rearrange("p a (h c) -> p (a h) c", h=2)
                dve.wait_ge(s_wl, b + 1)
                if b >= 2:
                    dve.wait_ge(s_wt, 2 * b - 2)
                vlink(dve.scalar_tensor_tensor(out=lg[:, :, c0:], in0=src[:, :, c0:], scalar=HD ** -0.5,
                                               in1=backwards(swa_bias[:, :, 0:2 * P - c0]), op0=ALU.mult, op1=ALU.add))
                vlink(dve.tensor_reduce(sm_max[:, b % 2], lg[:, :, c0:], AX, ALU.max))
                vlink(dve.tensor_tensor(sm_max[:, b % 2], sm_max[:, b % 2], sinks[:], ALU.max))
                vlink(dve.tensor_tensor(sm_snk[:, b % 2], sinks[:], sm_max[:, b % 2], ALU.subtract))
                dve.tensor_scalar(sm_neg[:, b % 2], sm_max[:, b % 2], -1.0, None, ALU.mult).then_inc(s_wm, 1)

            def swa_out(b):
                dve.wait_ge(s_wx, b + 1)
                vlink(dve.tensor_tensor(sm_rec[:, b % 2], sm_sum[:, b % 2], sm_snk[:, b % 2], ALU.add))
                vlink(dve.reciprocal(sm_rec[:, b % 2], sm_rec[:, b % 2]))
                dve.wait_ge(s_wo, b + 1)
                dve.tensor_tensor(y[:, b, 3 * W:].rearrange("p (h c) -> p h c", h=HEADS),
                                  ps[:, 7 if b % 2 == 0 else 0, 0:W].rearrange("p (h c) -> p h c", h=HEADS),
                                  sm_rec[:, b % 2].unsqueeze(2).to_broadcast([P, HEADS, HD]),
                                  ALU.mult).then_inc(s_wy, 1)

            swa_softmax(0)
            dve.wait_ge(s_pl, 1)
            for b in range(NBLK):
                if b + 1 < NBLK:
                    swa_softmax(b + 1)
                swa_out(b)
            for b in range(NBLK):
                dve.wait_ge(s_gs, b + 1)
                vlink(dve.tensor_tensor(vn[:, b].rearrange("p (g c) -> p g c", c=64),
                                        ps[:, 6 if b % 2 == 0 else 1, 0:W].rearrange("p (g c) -> p g c", c=64),
                                        gm_b[:].unsqueeze(2).to_broadcast([P, 4, 64]), ALU.add))
                dve.tensor_tensor(y[:, b, 0:W], vn[:, b], gm[:, b, 0:W], ALU.mult).then_inc(s_gy, 1)
            for b in range(NBLK):
                dve.wait_ge(s_pm, b + 1)
                for par, bank in enumerate((7, 0) if b % 2 == 0 else (6, 1)):
                    cols = slice(par * 64, par * 64 + 64)
                    ins = dve.tensor_tensor(
                        y[:, b, 2 * W:3 * W].rearrange("p (a c) -> p a c", a=2)[:, :, cols],
                        ps[:, bank, 0:W].rearrange("p (a c) -> p a c", a=2)[:, :, cols],
                        pool_s[:].rearrange("p (a c) -> p a c", a=2)[:, :, cols], ALU.mult)
                ins.then_inc(s_py, 1)

            R0 = 2 * ROUNDS
            m = len(LATE_BLOCKS)
            rounds = [0]
            for h in range(2):
                dve.wait_ge(s_tb, 16 * (h + 1))
                vlink(dve.memset(bias_t[0:64, :, 0:64], NEG))

                def soft(i):
                    b, hd = HB * h + i // HEADS, i % HEADS
                    I = HB * HEADS * h + i
                    n = P * (b + 1)
                    lg = logit[:, I % 2, 0:n]
                    bank = 4 - 2 * (I % 2)
                    src = ps[:, bank:bank + 2].rearrange("p a c -> p (a c)")[:, 0:n]
                    dve.wait_ge(s_al, I + 1)
                    if I >= 2:
                        dve.wait_ge(s_ao, I - 1)
                    vlink(dve.scalar_tensor_tensor(out=lg, in0=src, scalar=HD ** -0.5,
                                                   in1=backwards(bias_t[:, hd, 0:n]), op0=ALU.mult, op1=ALU.add))
                    if b >= 2:
                        vlink(dve.tensor_tensor(lg, lg, sc_of(b), ALU.add))
                    vlink(dve.tensor_reduce(sm_max[:, b % 2, hd:hd + 1], lg, AX, ALU.max))
                    dve.tensor_scalar(sm_neg[:, b % 2, hd:hd + 1], sm_max[:, b % 2, hd:hd + 1], -1.0, None,
                                      ALU.mult).then_inc(s_am, 1)

                soft(0)
                for i in range(HB * HEADS):
                    if i + 1 < HB * HEADS:
                        soft(i + 1)
                    if i % HEADS == HEADS - 1:
                        b = HB * h + i // HEADS
                        dve.wait_ge(s_ax, HEADS * (b + 1))
                        vlink(dve.reciprocal(sm_rec[:, b % 2], sm_sum[:, b % 2]))
                        dve.wait_ge(s_ao, HEADS * (b + 1))
                        dve.tensor_tensor(y[:, b, W:2 * W].rearrange("p (h c) -> p h c", h=HEADS),
                                          ps[:, 7 if b % 2 == 0 else 0, 0:W].rearrange("p (h c) -> p h c", h=HEADS),
                                          sm_rec[:, b % 2].unsqueeze(2).to_broadcast([P, HEADS, HD]),
                                          ALU.mult).then_inc(s_ay, 1)
                dve.wait_ge(s_yr, h + 1)
                vlink(dve.reciprocal(st3[:, 0:16], st2[:, 0:16]))
                yh = y[:, HB * h:HB * h + HB].rearrange("p b (m c) -> p (b m) c", m=4)
                dve.tensor_tensor(yh, yh, st3[:, 0:16].unsqueeze(2).to_broadcast([P, 16, W]),
                                  ALU.mult).then_inc(s_yn, 1)
                g0 = 16 + 16 * h
                norm_split(g0, KD, nt_tmp[1], lambda g: y_hi[:, g], lambda g: y_lo[:, g])

                def add_residual(r0):
                    dve.wait_ge(s_x2, 16 * (h + 1))
                    for g in range(8):
                        t, jh = g // 2, g % 2
                        dve.wait_ge(s_rt, r0 + g + 1)
                        xs = x2[h][:, t, HALF * jh:HALF * jh + HALF]
                        dve.tensor_tensor(xs, xs, ps[:, 4 + g % 2], ALU.add).then_inc(s_rd, 1)

                def row_scale(hh):
                    dve.wait_ge(s_r2, 2 * h + hh + 1)
                    vlink(dve.reciprocal(st3[:, 0:HB], st2[:, 0:HB]))

                add_residual(16 * h)
                row_scale(0)
                for t in range(HB):
                    dve.tensor_scalar(xn2[:, t], x2[h][:, t], st3[:, t:t + 1], None, ALU.mult).then_inc(s_n2, 1)
                norm_split(g0 + KD, KD, nt_tmp[1], lambda g: h2_hi[:, g], lambda g: h2_lo[:, g])
                for g, nf, nu, nd, f0 in group_bases(h):
                    F = 1 + NF * h + f0
                    with dve.Fori(0, nf, 1) as i:
                        dve.wait_ge(s_cin, F + 1 + i)
                        dve.scalar_tensor_tensor(out=conv_t[:], in0=conv_in[:, 1:HALF + 1],
                                                 scalar=conv_w[:, f0 + i, 1:2], in1=conv_t[:],
                                                 op0=ALU.mult, op1=ALU.add).then_inc(s_c1, 1)
                        dve.wait_ge(s_c1, F + 1 + i)
                        dve.scalar_tensor_tensor(out=conv_t[:], in0=conv_in[:, 0:HALF],
                                                 scalar=conv_w[:, f0 + i, 0:1], in1=conv_t[:],
                                                 op0=ALU.mult, op1=ALU.add).then_inc(s_conv, 1)
                        dve.wait_ge(s_gelu, F + 1 + i)
                        dve.wait_ge(s_gemm, nu + 2 + 2 * i)
                        dve.wait_ge(s_alo, F + i)
                        dve.tensor_tensor(act_f[:], conv_t[:], ps[:, 1], ALU.mult).then_inc(s_act, 1)
                        if h == 0:
                            top_round(LATE_BLOCKS, R0 + m * rounds[0] + m * i)
                    if h == 0:
                        rounds[0] += nf
                        if g == 2:
                            for _ in range(ROUNDS - rounds[0]):
                                top_round(LATE_BLOCKS, R0 + m * rounds[0])
                                rounds[0] += 1
                            dve.wait_ge(s_rep, R0 + m * ROUNDS)
                            for b in LATE_BLOCKS:
                                mask_of(b)
                    if g > 0 or h == 0:
                        with dve.Fori(0, KD // 2, 1) as i:
                            for j in range(2):
                                if g > 0:
                                    dve.wait_ge(s_gemm, nd + j + 1 + 2 * i)
                                    o = out_t[:, j + 2 * i]
                                    dve.scalar_tensor_tensor(out=o, in0=ps[:, 2 + j],
                                                             scalar=mod[:, bass.ds(5 * KD + j + 2 * i, 1)],
                                                             in1=o, op0=ALU.mult, op1=ALU.add).then_inc(s_dev[j], 1)
                            if h == 0 and g < 2:
                                top_round(LATE_BLOCKS, R0 + m * rounds[0] + m * i)
                        if h == 0 and g < 2:
                            rounds[0] += KD // 2
                add_residual(16 * h + 8)
                row_scale(1)
                dve.wait_ge(s_fg, 16 * (h + 1))
                for t in range(HB):
                    if HB * h + t >= 2:
                        dve.wait_ge(s_out[t % 2], 16 * ((HB * h + t) // 2))
                    dve.scalar_tensor_tensor(out=fin_o[:, t % 2], in0=x2[h][:, t], scalar=st3[:, t:t + 1],
                                             in1=fin_g[:], op0=ALU.mult, op1=ALU.mult).then_inc(s_fo, 1)

        @block.tensor
        def _(pe):
            for s_ in (s_hin, s_cin, s_conv, s_gelu, s_act, s_ahi, s_alo, s_c1, *s_dev):
                pe.sem_inc(s_, 1)
            pe.wait_ge(s_rel, 32)
            for i in range(3):
                last = pe.matmul(ps[0:8, 4 + i, 0:384], rel[:], onehot[:, 384 * i:384 * i + 384], start=True, stop=True)
            last.then_inc(s_f, 1)
            pe.wait_ge(s_cond, 1)

            def ada(c):
                if c < 16:
                    if c % 4 == 0:
                        pe.wait_ge(s_aw0[c // 4], 16)
                    wt = lambda j: w_ada0[:, j, P * c:P * c + P]
                else:
                    pe.wait_ge(s_aw1[c % 2], 16 * ((c - 16) // 2 + 1))
                    if c == 16:
                        pe.wait_ge(s_mod, 1)
                    wt = lambda j: w_ada1[:, c % 2, j]
                for j in range(KD):
                    mm = pe.matmul(ps[:, 7, c:c + 1], wt(j), cond[:, j:j + 1], start=(j == 0), stop=(j == KD - 1))
                mm.then_inc(s_ada, 1)

            for c in range(16):
                ada(c)

            def norm_transposes(g0, groups, src, ready):
                for g in range(groups):
                    if ready:
                        ready(g)
                    if g >= 4:
                        pe.wait_ge(s_ne, g0 + g - 3)
                    for t in range(4):
                        tr = pe.transpose(ps[:, (g0 + g) % 4, P * t:P * t + P], src(g, t), ident[:])
                    tr.then_inc(s_nt, 1)

            norm_transposes(0, 2 * KD, lambda g, t: x_sb[:, 4 * (g // KD) + t, P * (g % KD):P * (g % KD) + P],
                            lambda g: pe.wait_ge(s_xn, 4 * (g // KD) + 4) if g % KD == 0 else None)

            def gemm(slot, nk, parts, ready, *waits):
                pe.wait_ge(s_wlo, ready)
                for s_, val in waits:
                    pe.wait_ge(s_, val)
                for kk in range(nk):
                    first, last_k = kk == 0, kk == nk - 1
                    for bank, xh, xl in parts:
                        pe.matmul(ps[:, bank], r(w_hi[:, slot, kk]), r(xh(kk)), start=first, stop=False)
                        pe.matmul(ps[:, bank], r(w_hi[:, slot, kk]), r(xl(kk)), start=False, stop=False)
                    for bank, xh, xl in parts:
                        mm = pe.matmul(ps[:, bank], r(w_lo[:, slot, kk]), r(xh(kk)), start=False, stop=last_k)
                mm.then_inc(s_gemm, 1)

            def in_parts(n):
                return [(2 * (n % 2) + i,
                         lambda kk, i=i: h_hi[:, kk, HALF * i:HALF * i + HALF],
                         lambda kk, i=i: h_lo[:, kk, HALF * i:HALF * i + HALF]) for i in range(2)]

            done = [0]

            def dots(b):
                while done[0] < len(DOTS) and DOTS[done[0]][0] == b:
                    i = done[0]
                    _, k0, n, h = DOTS[i]
                    if i >= 2:
                        pe.wait_ge(s_relu, i - 1)
                    rows = slice(32 * (h % 4), 32 * (h % 4) + 32)
                    pe.matmul(ps[:, 4 + i % 2, 0:n], qi[rows, h // 4, P * b:P * b + P], ki[rows, k0:k0 + n],
                              start=True, stop=True).then_inc(s_dot, 1)
                    done[0] += 1

            def v_turn(g, src):
                if g > 0:
                    pe.wait_ge(s_ve, g)
                for t in range(HB):
                    blk = HB * (g % 2) + t
                    tr = pe.transpose(ps[:, 6, P * t:P * t + P], src[:, P * blk:P * blk + P], ident[:])
                tr.then_inc(s_vt, 1)

            pe.wait_ge(s_nl, 16)
            pe.wait_ge(s_ne, 16)
            dot_after = {3: 2, 5: 3, 7: 4, 9: 5, 11: 6, 13: 7}
            for n in range(N_IN):
                gemm(n % 2, KD, in_parts(n), n + 1, *([(s_ev, n - 1)] if n >= 2 else []))
                if n == 3:
                    pe.wait_ge(s_ev, U_KIWI + 1)
                    pe.wait_ge(s_fs, 1)
                    for b in TOP_BLOCKS:
                        mm = pe.matmul(ps[:, 6, 8 * (b - 2):8 * (b - 2) + 8], kiwi[:, P * b:P * b + P],
                                       ident[:, WI_COL:WI_COL + IDX_HEADS], start=True, stop=True)
                    mm.then_inc(s_wi, 1)
                if n in dot_after:
                    dots(dot_after[n])
                if n == 10:
                    pe.wait_ge(s_wis, 1)
                    pe.wait_ge(s_ev, U_V + 2)
                    for g in range(4):
                        v_turn(g, stage[g // 2])
                if n == 16:
                    pe.wait_ge(s_ev, U_DV + 1)
                    for g in range(4, 6):
                        v_turn(g, stage[0])
                if n < 16:
                    ada(16 + 2 * n)
                    ada(17 + 2 * n)

            pe.wait_ge(s_ev, N_IN)
            pe.wait_ge(s_relu, len(DOTS))
            for b in range(NBLK):
                if b >= 2:
                    pe.wait_ge(s_ge, b - 1)
                for t in range(4):
                    tr = pe.transpose(ps[:, 4 + b % 2, P * t:P * t + P], za_t[:, t, P * b:P * b + P], ident[:])
                tr.then_inc(s_gt, 1)

            pe.wait_ge(s_ve, 6)
            pe.wait_ge(s_ge, NBLK)
            pe.wait_ge(s_mod, 2)

            def swa_logits(b):
                c0 = P if b == 0 else 0
                if b >= 2:
                    pe.wait_ge(s_wm, b - 1)
                bank = 4 - 2 * (b % 2)
                for h in range(HEADS):
                    rows = slice(64 * (h // 2), 64 * (h // 2) + 64)
                    mm = pe.matmul(ps[:, bank + h // 2, 2 * P * (h % 2) + c0:2 * P * (h % 2) + 2 * P],
                                   dq[rows, h % 2, P * b:P * b + P], dk[rows, P * (b - 1) + c0:P * (b + 1)],
                                   start=True, stop=True)
                mm.then_inc(s_wl, 1)

            swa_logits(0)
            for b in range(NBLK):
                if b + 1 < NBLK:
                    swa_logits(b + 1)
                cs = [1] if b == 0 else [0, 1]
                pe.wait_ge(s_wx, b + 1)
                lg = logit[:, b % 2].rearrange("p (h c) -> p h c", h=HEADS)
                for j in range(2):
                    if b >= 1:
                        pe.wait_ge(s_we, 2 * b - 1 + j)
                    for hh in range(2):
                        for c in cs:
                            at_ = P * (2 * hh + c)
                            tr = pe.transpose(ps[:, 6 if j == 0 else 1, at_:at_ + P],
                                              lg[:, 2 * j + hh, P * c:P * c + P], ident[:])
                    tr.then_inc(s_wt, 1)
                pe.wait_ge(s_we, 2 * b + 2)
                if b >= 2:
                    pe.wait_ge(s_wy, b - 1)
                for h in range(HEADS):
                    for c in cs:
                        mm = pe.matmul(ps[:, 7 if b % 2 == 0 else 0, HD * h:HD * h + HD],
                                       p_t[:, b % 2, 2 * h + c], dv[:, b - 1 + c, HD * (h // 2):HD * (h // 2) + HD],
                                       start=(c == cs[0]), stop=(c == 1))
                mm.then_inc(s_wo, 1)
            pe.wait_ge(s_vn, 1)
            pe.wait_ge(s_eps, 3)
            pe.wait_ge(s_we, 2 * NBLK)
            for b in range(NBLK):
                if b >= 2:
                    pe.wait_ge(s_gy, b - 1)
                for g in range(4):
                    mm = pe.matmul(ps[:, 6 if b % 2 == 0 else 1, 64 * g:64 * g + 64], ws_t[:, g],
                                   vn[:, b, 64 * g:64 * g + 64], start=True, stop=True)
                mm.then_inc(s_gs, 1)
            pe.wait_ge(s_pl, 1)
            pe.wait_ge(s_wy, NBLK)
            pe.wait_ge(s_gy, NBLK)
            for b in range(NBLK):
                if b >= 2:
                    pe.wait_ge(s_py, b - 1)
                for g in range(4):
                    rows = slice(64 * (g % 2), 64 * (g % 2) + 64)
                    bank = ((7, 0) if b % 2 == 0 else (6, 1))[g % 2]
                    mm = pe.matmul(ps[:, bank, 64 * g:64 * g + 64],
                                   pooled[rows, g // 2, P * b:P * b + P], pool_w[rows, g // 2],
                                   start=True, stop=True)
                mm.then_inc(s_pm, 1)

            n_pt = [0]
            for h in range(2):
                def logits(i):
                    b, hd = HB * h + i // HEADS, i % HEADS
                    I = HB * HEADS * h + i
                    n = P * (b + 1)
                    if I >= 2:
                        pe.wait_ge(s_am, I - 1)
                    bank = 4 - 2 * (I % 2)
                    rows = slice(64 * (hd % 2), 64 * (hd % 2) + 64)
                    for c in range(0, n, 512):
                        w_ = min(512, n - c)
                        mm = pe.matmul(ps[:, bank + c // 512, 0:w_], q[rows, hd // 2, P * b:P * b + P],
                                       k[rows, hd // 2, c:c + w_], start=True, stop=True)
                    mm.then_inc(s_al, 1)

                if h == 0:
                    pe.wait_ge(s_wm, NBLK)
                    pe.wait_ge(s_gy, NBLK)
                    pe.wait_ge(s_py, NBLK)
                else:
                    pe.wait_ge(s_dev[0], 17)
                    pe.wait_ge(s_dev[1], 17)
                    pe.wait_ge(s_rd, 16)
                logits(0)
                for i in range(HB * HEADS):
                    if i + 1 < HB * HEADS:
                        logits(i + 1)
                    b, hd = HB * h + i // HEADS, i % HEADS
                    I = HB * HEADS * h + i
                    pe.wait_ge(s_ax, I + 1)
                    for t0 in range(0, b + 1, 4):
                        if n_pt[0] >= 2:
                            pe.wait_ge(s_ae, n_pt[0] - 1)
                        for t in range(t0, min(t0 + 4, b + 1)):
                            tr = pe.transpose(ps[:, 6 if n_pt[0] % 2 == 0 else 1, P * (t - t0):P * (t - t0) + P],
                                              logit[:, I % 2, P * t:P * t + P], ident[:])
                        tr.then_inc(s_at, 1)
                        n_pt[0] += 1
                    pe.wait_ge(s_ae, n_pt[0])
                    if hd == 0 and b >= 2:
                        pe.wait_ge(s_ay, b - 1)
                    for t in range(b + 1):
                        mm = pe.matmul(ps[:, 7 if b % 2 == 0 else 0, HD * hd:HD * hd + HD], p_t[:, I % 2, t],
                                       v[:, t, HD * hd:HD * hd + HD], start=(t == 0), stop=(t == b))
                    mm.then_inc(s_ao, 1)
                pe.wait_ge(s_yn, h + 1)
                pe.wait_ge(s_ay, HB * (h + 1))
                g0 = 16 + 16 * h
                norm_transposes(g0, KD, lambda g, t: y[:, HB * h + t, P * g:P * g + P], None)
                pe.wait_ge(s_ne, g0 + KD)
                pe.wait_ge(s_nl, g0 + KD)

                def column_loop(base, J0, nk, xh, xl):
                    with pe.Fori(0, KD // 2, 1) as i:
                        for j in range(2):
                            gemm((base + j) % 2, nk, [(2 + j, xh, xl)], base + j + 1 + 2 * i,
                                 (s_dev[j], 1 + J0 // 2 + i))

                def turn_back(r0):
                    for g in range(8):
                        t, jh = g // 2, g % 2
                        if g >= 2:
                            pe.wait_ge(s_rd, r0 + g - 1)
                        for j in range(4):
                            tr = pe.transpose(ps[:, 4 + g % 2, P * j:P * j + P],
                                              out_t[:, 4 * jh + j, P * t:P * t + P], ident[:])
                        tr.then_inc(s_rt, 1)

                nb = half_base(h)
                J = 4 * KD * h
                column_loop(nb, J, KD, lambda kk: y_hi[:, kk], lambda kk: y_lo[:, kk])
                pe.wait_ge(s_dev[0], J // 2 + 5)
                pe.wait_ge(s_dev[1], J // 2 + 5)
                turn_back(16 * h)
                norm_transposes(g0 + KD, KD, lambda g, t: xn2[:, t, P * g:P * g + P],
                                lambda g: pe.wait_ge(s_n2, HB * (h + 1)) if g == 0 else None)
                pe.wait_ge(s_ne, g0 + 2 * KD)
                pe.wait_ge(s_nl, g0 + 2 * KD)
                for g, nf, nu, nd, f0 in group_bases(h):
                    F = 1 + NF * h + f0
                    with pe.Fori(0, nf, 1) as i:
                        for j, s_ in ((0, s_cin), (1, s_act)):
                            gemm((nu + j) % 2, KD, [(j, lambda kk: h2_hi[:, kk], lambda kk: h2_lo[:, kk])],
                                 nu + j + 1 + 2 * i, (s_, F + i))
                    J += KD
                    pe.wait_ge(s_alo, F + nf)
                    column_loop(nd, J, nf, lambda kk: act_hi[:, kk], lambda kk: act_lo[:, kk])
                pe.wait_ge(s_dev[0], J // 2 + 5)
                pe.wait_ge(s_dev[1], J // 2 + 5)
                turn_back(16 * h + 8)


def bias_onehot():
    rel = P - 1 - np.arange(S + P)
    n = np.abs(rel)
    nf = np.maximum(n, 1).astype(np.float32)
    large = 8 + (np.log(nf / np.float32(8)) / np.float32(np.log(1024 / 8)) * np.float32(8)).astype(np.int32)
    bucket = np.where(rel > 0, 16, 0) + np.where(n < 8, n, np.minimum(large, 15))
    return (np.arange(32)[:, None] == bucket[None, :]).astype(np.float32)


def pool_counts():
    t = np.arange(1, 17, dtype=np.float32)
    rows = [1 / np.minimum(t, np.float32(w)) for w in (2, 4, 8, 16)]
    c = np.stack([np.stack([rows[0], rows[2]]), np.stack([rows[1], rows[3]])])
    return np.repeat(c, 64, axis=0).astype(np.float32)


def weight_units(w_in, w_out, w_up, w_down):
    def cols(*runs):
        part = np.concatenate([w_in[:, x0:x1] for x0, x1 in runs], axis=1)
        if part.shape[1] < P:
            part = np.concatenate([part, np.zeros((D, P - part.shape[1]), np.float32)], axis=1)
        return part

    def unit(m):
        return m.reshape(-1, P, P).transpose(1, 0, 2)

    def tiles(x0, n):
        return [cols((x0 + P * i, x0 + P * i + P)) for i in range(n)]

    zc, zdq = 1576, 1832
    units = (tiles(1280, 2) + [cols((1536, 1576))] + tiles(512, 2) + tiles(768, 2) + tiles(1024, 2)
             + tiles(zc, 2)
             + [cols((zdq + 64 * i, zdq + 64 * i + 64), (zdq + 128 + 64 * i, zdq + 192 + 64 * i)) for i in range(2)]
             + tiles(2088, 1) + tiles(2216, 1) + tiles(0, 4))
    units = [unit(u) for u in units]
    units += [unit(w_out[:, P * j:P * j + P]) for j in range(KD)]
    f0 = 0
    for nf in GROUPS:
        for f in range(f0, f0 + nf):
            units += [unit(w_up[:, P * f:P * f + P]), unit(w_up[:, DFF + P * f:DFF + P * f + P])]
        rows = w_down[P * f0:P * (f0 + nf)]
        if nf < KD:
            rows = np.concatenate([rows, np.zeros((P * (KD - nf), D), np.float32)], axis=0)
        units += [unit(rows[:, P * j:P * j + P]) for j in range(KD)]
        f0 += nf
    return np.ascontiguousarray(np.stack(units))


def kernel(x, c, w_ada, b_ada, norm1_g, norm2_g, w_in, gmlp_ws, gmlp_bs, pool_w, pool_scale,
           swa_sinks, rel_bias, mix_out_g, w_out, ffn_w_up, ffn_conv_w, ffn_conv_b, ffn_w_down,
           final_g):
    import concourse.bacc as bacc
    from concourse.bass_utils import run_bass_kernel_spmd

    def by_feature(vec):
        return np.asarray(vec).reshape(-1, P).T

    arrays = {
        "x": np.asarray(x)[0],
        "c": np.asarray(c).reshape(P, KD),
        "w_ada": np.asarray(w_ada)[0],
        "b_ada": by_feature(np.asarray(b_ada)[0]),
        "norm_g": np.stack([by_feature(np.asarray(norm1_g)[0]), by_feature(np.asarray(norm2_g)[0])], axis=1),
        "mix_g": by_feature(np.asarray(mix_out_g)[0]),
        "conv_w": np.stack([by_feature(t) for t in (*np.asarray(ffn_conv_w)[0], np.asarray(ffn_conv_b)[0])], axis=2),
        "gm_b": np.asarray(gmlp_bs)[0].T,
        "ident": np.eye(P, dtype=np.float32),
        "ws_t": np.asarray(gmlp_ws)[0].transpose(2, 0, 1),
        "pool_w": np.asarray(pool_w)[0].reshape(2, P, 64).transpose(1, 0, 2),
        "pool_c": pool_counts(),
        "sinks": np.asarray(swa_sinks)[0],
        "pool_s": np.asarray(pool_scale)[0],
        "rel_bias": np.asarray(rel_bias),
        "onehot": bias_onehot(),
        "final_g": np.asarray(final_g),
        "w": weight_units(np.asarray(w_in)[0], np.asarray(w_out)[0], np.asarray(ffn_w_up)[0],
                          np.asarray(ffn_w_down)[0]),
    }
    arrays = {n: np.ascontiguousarray(v) for n, v in arrays.items()}
    nc = bacc.Bacc("TRN2", target_bir_lowering=False, num_devices=1)
    ins = {n: nc.dram_tensor(f"in_{n}", v.shape, F32, kind="ExternalInput").ap() for n, v in arrays.items()}
    out = nc.dram_tensor("out", (S, D), F32, kind="ExternalOutput").ap()
    build(nc, ins, out)
    res = run_bass_kernel_spmd(nc, [{f"in_{n}": v for n, v in arrays.items()}], core_ids=[0])
    return res.results[0]["out"].reshape(1, S, D)
```

```python
from contextlib import ExitStack

import numpy as np

import concourse.bass as bass
from concourse import mybir

F32 = mybir.dt.float32
F32R = mybir.dt.float32r
ALU = mybir.AluOpType
ACT = mybir.ActivationFunctionType
AX = mybir.AxisListType.X

P = 128
D = 1024
S = 1024
KD = D // P
NBLK = S // P
HALF = 512
HB = HALF // P
W = 256
DFF = 2816
NF = DFF // P
GROUPS = (8, 8, 6)
EPS = 1e-6
NEG = -1e30
IDX_HEADS, IDX_DIM = 8, 32
HEADS, HD = 4, 64
TOPK = 256
ROUNDS = TOPK // 8
NO_KEY = -3.0e38
TAKEN = -3.4e38
TAKEN_BELOW = -3.2e38

U_QI, U_KIWI, U_Q, U_K, U_V, U_C, U_DQ, U_DK, U_DV, U_A = 0, 2, 3, 5, 7, 9, 11, 13, 14, 15
N_IN = 19
N_OUT = KD
N_FFN = 2 * NF + len(GROUPS) * KD
N_HALF = N_OUT + N_FFN
N_UNITS = N_IN + N_HALF
WI_COL = 32
TOP_BLOCKS = range(2, NBLK)
LATE_BLOCKS = range(HB, NBLK)

BASE = 16512


def score_columns():
    at, n = {}, 0
    for b in TOP_BLOCKS:
        at[b] = n
        n += P * (b + 1)
    return at, n


def dot_chunks():
    return [(b, k0, min(512, P * (b + 1) - k0), h)
            for b in TOP_BLOCKS for k0 in range(0, P * (b + 1), 512) for h in range(IDX_HEADS)]


def build(nc, a, out):
    with ExitStack() as ctx:
        def at(name, shape, offset):
            return nc.alloc_sbuf_tensor_at(name, shape, F32, offset=BASE + offset)

        def sem(name):
            return ctx.enter_context(nc.semaphore(name))

        RA, RB, RC, RD, RE, RG, RH = 0, 65536, 98304, 131072, 155648, 163840, 180736
        RM = RH + 24576
        h_hi = at("h_hi", [P, KD, S], RA)
        h_lo = at("h_lo", [P, KD, S], RA + 32768)
        pooled = at("pooled", [P, 2, S], RA)
        win_a = at("win_a", [P, 16 + S], RA + 8192)
        win_b = at("win_b", [P, 16 + S], RA + 12352)
        vn = at("vn", [P, NBLK, W], RA + 16512)
        gm = at("gm", [P, NBLK, 2 * W], RA + 24704)
        gm_sq = at("gm_sq", [P, NBLK, W], RA + 41088)
        y_hi = at("y_hi", [P, KD, HALF], RA)
        y_lo = at("y_lo", [P, KD, HALF], RA + 16384)
        act_hi = at("act_hi", [P, 8, HALF], RA)
        act_lo = at("act_lo", [P, 8, HALF], RA + 16384)
        x2 = at("x2", [P, KD, HALF], RA + 32768)
        bias_0 = at("bias_0", [P, HEADS, S], RA + 49152)
        conv_in = at("conv_in", [P, 2, 2 + HALF], RA + 49152)
        conv_t = at("conv_t", [P, 2, HALF], RA + 53760)
        act_f = at("act_f", [P, 2, HALF], RA + 57856)
        h2_t = at("h2_t", [P, 2, HALF], RA + 57856)
        fin_o = at("fin_o", [P, 4, HALF], RA + 49152)
        qi = at("qi", [P, 2, S], RB)
        ki = at("ki", [P, S], RB + 8192)
        dq = at("dq", [P, 2, S], RB + 12288)
        dk = at("dk", [P, S], RB + 20480)
        dv = at("dv", [P, NBLK, P], RB + 24576)
        swa_bias = at("swa_bias", [P, HEADS, 2 * P], RB + 28672)
        p_t = at("p_t", [P, 2, NBLK, P], RB)
        h2_hi = at("h2_hi", [P, KD, HALF], RB)
        h2_lo = at("h2_lo", [P, KD, HALF], RB + 16384)
        sq_x = at("sq_x", [P, 2, HALF], RB)
        sum_x = at("sum_x", [P, HALF], RB + 4096)
        diag_x = at("diag_x", [P, HALF], RB + 8192)
        h_t = at("h_t", [P, 2, HALF], RB + 12288)
        logit4 = at("logit4", [P, 4, S], RB + 8192)
        junk = at("junk", [P, 4, W], RB + 24576)
        cond = at("cond", [P, D], RB + 28672)
        x_sb = at("x_sb", [P, KD, S], RC)
        za_t = at("za_t", [P, 4, S], RC)
        kiwi = at("kiwi", [P, S], RC)
        stage = [at("stage_0", [P, S], RC + 24704), at("stage_1", [P, S], RC + 4096)]
        relu_r = at("relu_r", [P, 4, 512], RC + 8192)
        zc = [at("zc_0", [P, 16 + S], RC + 16384), at("zc_1", [P, 16 + S], RC + 20544)]
        y = at("y", [P, NBLK, D], RC)
        bias_1 = at("bias_1", [P, HEADS, S], RC)
        q = at("q", [P, 2, S], RD)
        k = at("k", [P, 2, S], RD + 8192)
        v = at("v", [P, NBLK, W], RD + 16384)
        w_ada0 = at("w_ada0", [P, 2, 4, D], RD)
        w_ada1 = at("w_ada1", [P, 2, D], RE)
        logit = at("logit", [P, 2, S], RE)
        bias_m = at("bias_m", [P, 2, S], RE)
        diag_y = at("diag_y", [P, 4, HB, P], RE)
        sq2 = at("sq2", [P, 2, HALF], RE)
        sum2 = at("sum2", [P, HALF], RE + 4096)
        diag2 = at("diag2", [P, HALF], RE + 6144)
        onehot = at("onehot", [32, S + P], RG)
        fbias = at("fbias", [HEADS * 2, S + P], RG + 4608)
        SC, n_sc = score_columns()
        score = at("score", [P, n_sc], RG)
        w_raw = at("w_raw", [P, 2, KD, P], RH)
        w_hi = at("w_hi", [P, 2, KD, P], RH + 8192)
        w_lo = at("w_lo", [P, 2, KD, P], RH + 16384)

        small_at = [RM]

        def small(name, shape):
            t = at(name, shape, small_at[0])
            small_at[0] += -(-4 * int(np.prod(shape[1:])) // 32) * 32
            assert BASE + small_at[0] <= 229344, small_at[0]
            return t

        ident = small("ident", [P, P])
        ws_t = small("ws_t", [P, 4, P])
        pool_w = small("pool_w", [P, 2, 64])
        pool_s = small("pool_s", [P, W])
        pool_c = small("pool_c", [P, 2, 16])
        b_ada = small("b_ada", [P, 48])
        norm_g = small("norm_g", [P, 2, KD])
        mix_g = small("mix_g", [P, KD])
        fin_g = small("fin_g", [P, KD])
        ones = small("ones", [P, P])
        conv_w = small("conv_w", [P, NF, 4])
        gm_b = small("gm_b", [P, 4])
        sinks = small("sinks", [P, HEADS])
        rel = small("rel", [32, 8])
        ada = small("ada", [P, 48])
        root_s = small("root_s", [P, HB])
        root_r = small("root_r", [P, HB])
        mod = small("mod", [P, 48])
        scale_g = small("scale_g", [P, 2, KD])
        halo = small("halo", [P, NF, 2])
        eps = small("eps", [P, 1])
        st = small("st", [P, 32])
        st2 = small("st2", [P, 32])
        st3 = small("st3", [P, 32])
        wis = small("wis", [P, len(TOP_BLOCKS), IDX_HEADS])
        tick = small("tick", [P, 1])
        top8 = small("top8", [P, len(TOP_BLOCKS), 8])
        sm_max = small("sm_max", [P, 2, HEADS])
        sm_neg = small("sm_neg", [P, 2, HEADS])
        sm_sum = small("sm_sum", [P, 2, HEADS])
        sm_snk = small("sm_snk", [P, 2, HEADS])
        sm_rec = small("sm_rec", [P, 2, HEADS])

        ps = ctx.enter_context(nc.psum_tensor("ps", [P, 8, 512], F32))

        def r(ap):
            return ap.bitcast(F32R)

        f_dram = nc.dram_tensor("f_dram", (8, S + P), F32, kind="Internal")
        bias_rows = bass.AP(tensor=f_dram, offset=0, ap=[[1, P], [S + P, HEADS], [1, S]])

        def backwards(ap):
            *dims, (step, n) = ap.ap
            return bass.AP(tensor=ap.tensor, offset=ap.offset + step * (n - 1), ap=[*dims, [-step, n]])

        s_par = sem("s_par")
        s_rel = sem("s_rel")
        s_x = [sem(f"s_x{i}") for i in range(2)]
        s_aw0 = [sem(f"s_aw0{i}") for i in range(4)]
        s_aw1 = [sem(f"s_aw1{i}") for i in range(2)]
        s_eps = sem("s_eps")
        s_cload, s_cond = sem("s_cload"), sem("s_cond")
        s_ada = sem("s_ada")
        s_adp, s_ads = sem("s_adp"), sem("s_ads")
        s_mod = sem("s_mod")
        s_f, s_fs, s_fd, s_tb, s_swb = sem("s_f"), sem("s_fs"), sem("s_fd"), sem("s_tb"), sem("s_swb")
        s_sq, s_sa, s_ms = sem("s_sq"), sem("s_sa"), sem("s_ms")
        s_sd, s_dg, s_bc = sem("s_sd"), sem("s_dg"), sem("s_bc")
        s_nt, s_tt, s_nh, s_nl = sem("s_nt"), sem("s_tt"), sem("s_nh"), sem("s_nl")
        s_raw = [sem(f"s_raw{i}") for i in range(2)]
        s_whi, s_wlo, s_gemm = sem("s_whi"), sem("s_wlo"), sem("s_gemm")
        s_ev = sem("s_ev")
        s_wi, s_wis = sem("s_wi"), sem("s_wis")
        s_dot, s_relu, s_acc = sem("s_dot"), sem("s_relu"), sem("s_acc")
        s_max, s_rep = sem("s_max"), sem("s_rep")
        s_vt, s_ve = sem("s_vt"), sem("s_ve")
        s_gt, s_ge = sem("s_gt"), sem("s_ge")
        s_lnv, s_lns, s_vn = sem("s_lnv"), sem("s_lns"), sem("s_vn")
        s_gs, s_gy = sem("s_gs"), sem("s_gy")
        s_pad, s_pl, s_pm, s_py = sem("s_pad"), sem("s_pl"), sem("s_pm"), sem("s_py")
        s_wl, s_wm, s_wx, s_wt, s_we, s_wo, s_wy = (sem(f"s_w_{x}") for x in "l m x t e o y".split())
        s_al, s_am, s_ax, s_at, s_ae, s_ao, s_ay = (sem(f"s_a_{x}") for x in "l m x t e o y".split())
        s_bi, s_mk, s_bm, s_ar = sem("s_bi"), sem("s_mk"), sem("s_bm"), sem("s_ar")
        s_yq, s_yr, s_yn = sem("s_yq"), sem("s_yr"), sem("s_yn")
        s_x2, s_res = sem("s_x2"), sem("s_res")
        s_hin = sem("s_hin")
        s_cin, s_conv, s_gelu, s_act, s_ahi, s_alo, s_c1 = (
            sem(f"s_{x}") for x in "cin conv gelu act ahi alo c1".split())
        s_fo, s_out = sem("s_fo"), [sem(f"s_out{i}") for i in range(4)]
        s_vc, s_sc_, s_pc = sem("s_vchain"), sem("s_schain"), sem("s_pchain")

        DOTS = dot_chunks()
        chain = {}

        def link(eng, s, ins):
            chain[s.name] = chain.get(s.name, 0) + 1
            ins.then_inc(s, 1)
            eng.wait_ge(s, chain[s.name])

        def half_base(h):
            return N_IN + N_HALF * h

        def group_bases(h):
            n, f, res = half_base(h) + N_OUT, 0, []
            for g, nf in enumerate(GROUPS):
                res.append((g, nf, n, n + 2 * nf, f))
                n += 2 * nf + KD
                f += nf
            return res

        N_SEQ = N_IN + 2 * N_HALF

        def ada_tiles(chunk):
            return [2 * chunk, 2 * chunk + 1, KD + 2 * chunk, KD + 2 * chunk + 1]

        DOT_UNIT = 3
        DOT_STEPS = len(DOTS) // IDX_HEADS
        Y_BANKS = (0, 1, 6, 7)
        ADA_STEPS = 16
        EARLY = [b for b in TOP_BLOCKS if b not in LATE_BLOCKS]
        early_steps = {s_: 3 if s_ < 3 else 2 for s_ in range(1, ADA_STEPS)}
        assert sum(early_steps.values()) == ROUNDS

        def raw_ready(n):
            return s_raw[n % 2], 16 * (n // 2 + 1)

        block = ctx.enter_context(nc.Block())

        @block.sync
        def _(sp):
            sp.dma_start(cond[:], a["c"].partition_broadcast(P)).then_inc(s_cload, 16)
            sp.dma_start(rel[:], a["rel_bias"]).then_inc(s_rel, 16)
            sp.dma_start(onehot[:], a["onehot"]).then_inc(s_rel, 16)
            for name, dst in (("b_ada", b_ada), ("norm_g", norm_g), ("mix_g", mix_g), ("fin_g", fin_g),
                              ("conv_w", conv_w), ("gm_b", gm_b), ("ident", ident), ("ws_t", ws_t),
                              ("pool_w", pool_w), ("pool_c", pool_c)):
                sp.dma_start(dst[:], a[name]).then_inc(s_par, 16)
            sp.dma_start(sinks[:], a["sinks"].partition_broadcast(P)).then_inc(s_par, 16)
            sp.dma_start(pool_s[:], a["pool_s"].partition_broadcast(P)).then_inc(s_par, 16)
            xs = a["x"].rearrange("(k p) s -> p k s", p=P)
            for i in range(2):
                sp.dma_start(x_sb[:, :, HALF * i:HALF * i + HALF], xs[:, :, HALF * i:HALF * i + HALF]
                             ).then_inc(s_x[i], 16)
            w = a["w"].rearrange("u p k c -> u p (k c)")

            def load(n):
                if n >= 2:
                    sp.wait_ge(s_wlo, n - 1)
                sp.dma_start(w_raw[:, n % 2], w[n]).then_inc(s_raw[n % 2], 16)

            wa = a["w_ada"].rearrange("(c p) d -> p c d", p=P)
            for i in range(4):
                if i >= 2:
                    sp.wait_ge(s_ada, 2 * (i - 1))
                    sp.wait_ge(s_ads, 2 * (i - 1))
                for half, c0 in enumerate((2 * i, KD + 2 * i)):
                    sp.dma_start(w_ada0[:, i % 2, 2 * half:2 * half + 2], wa[:, c0:c0 + 2]).then_inc(s_aw0[i], 16)
                if i < 2:
                    load(i)
            for n in range(N_IN):
                if n + 2 < N_IN:
                    load(n + 2)
                step = n - DOT_UNIT
                if 0 <= step < ADA_STEPS:
                    for c in (16 + 2 * step, 17 + 2 * step):
                        sp.wait_ge(s_ada, max(8, c - 9))
                        sp.wait_ge(s_ads, 8)
                        sp.dma_start(w_ada1[:, c % 2], wa[:, c]).then_inc(s_aw1[c % 2], 16)
            for h in range(2):
                nb = half_base(h)
                with sp.Fori(0, N_HALF // 2, 1) as i:
                    for j in range(2):
                        sp.wait_ge(s_wlo, nb + j - 1 + 2 * i)
                        sp.dma_start(w_raw[:, (nb + j) % 2], w[N_IN + j + 2 * i]
                                     ).then_inc(s_raw[(nb + j) % 2], 16)
            for n in range(N_SEQ, N_SEQ + 2):
                sp.wait_ge(s_wlo, n - 1)
                sp.dma_start(w_raw[:, n % 2], w[0]).then_inc(s_raw[n % 2], 16)

        @block.gpsimd
        def _(pool):
            def w_lo_unit(slot, ready, i=None):
                pool.wait_ge(s_whi, ready)
                pool.tensor_tensor(r(w_lo[:, slot]), w_raw[:, slot], w_hi[:, slot],
                                   ALU.subtract).then_inc(s_wlo, 1)

            def lo(n):
                w_lo_unit(n % 2, n + 1)

            pool.memset(eps[:], EPS).then_inc(s_eps, 1)
            pool.memset(halo[:], 0.0).then_inc(s_eps, 1)
            pool.memset(ones[:], 1.0).then_inc(s_eps, 1)
            pool.wait_ge(s_par, 16 * 12)
            pool.wait_ge(s_eps, 3)
            pool.memset(ws_t[64:128, :, 0:64], 0.0).then_inc(s_eps, 1)
            pool.wait_ge(s_eps, 4)

            def ada_products(chunk):
                pool.wait_ge(s_cond, 1)
                pool.wait_ge(s_aw0[chunk], 32)
                for j in (2, 3):
                    t = w_ada0[:, chunk % 2, j]
                    pool.tensor_tensor(t, t, cond[:], ALU.mult).then_inc(s_adp, 1)

            ada_products(0)
            lo(0)
            for chunk in range(1, 4):
                ada_products(chunk)
            for n in range(N_IN):
                if n == U_C:
                    pool.wait_ge(s_nl, 16)
                    pool.memset(zc[0][:, 0:16], 0.0).then_inc(s_pad, 1)
                    pool.memset(zc[1][:, 0:16], 0.0).then_inc(s_pad, 1)
                lo(n + 1)
            pool.wait_ge(s_ev, U_C + 2)
            pool.wait_ge(s_gemm, N_IN)
            pool.wait_ge(s_pad, 2)

            def plink(ins):
                link(pool, s_pc, ins)

            for tile, first in ((0, 2), (1, 8)):
                src = zc[tile]
                bufs = [win_a, win_b]
                cur, win, n = src, 1, 0
                while win < 2 * first:
                    dst = bufs[n % 2]
                    lo_p = 64 if 2 * win == 2 * first else 0
                    plink(pool.tensor_tensor(dst[lo_p:P, 2 * win - 1:], cur[lo_p:P, 2 * win - 1:],
                                             cur[lo_p:P, win - 1:16 + S - win], ALU.add))
                    prev, cur = cur, dst
                    win, n = 2 * win, n + 1
                for p0, s_, wn in ((0, prev, first), (64, cur, 2 * first)):
                    rows = slice(p0, p0 + 64)
                    o = pooled[rows, tile]
                    plink(pool.tensor_tensor(o[:, 0:16], s_[rows, 16:32], pool_c[rows, tile], ALU.mult))
                    plink(pool.tensor_scalar(o[:, 16:], s_[rows, 32:], 1.0 / wn, None, ALU.mult))
                    ins = pool.tensor_tensor(o, o, src[rows, 16:], ALU.subtract)
                    if (tile, p0) == (1, 64):
                        ins.then_inc(s_pl, 1)
                    else:
                        plink(ins)

            pool.wait_ge(s_pl, 1)
            lo(N_IN + 1)
            for h in range(2):
                nb = half_base(h)

                def pairs(base, count):
                    with pool.Fori(0, count, 1) as i:
                        for j in (2, 3):
                            w_lo_unit((base + j) % 2, base + j + 1 + 2 * i)

                pool.wait_ge(s_bi, h + 1)
                pool.wait_ge(s_mk, h + 1)
                for b in range(max(2, HB * h), HB * (h + 1)):
                    for hd in range(HEADS):
                        I = HEADS * b + hd
                        if I >= 10:
                            pool.wait_ge(s_ar, I - 1)
                        sc = score[:, SC[b]:SC[b] + P * (b + 1)]
                        pool.tensor_tensor(bias_m[:, I % 2, 0:P * (b + 1)],
                                           backwards((bias_1 if h else bias_0)[:, hd, 0:P * (b + 1)]), sc,
                                           ALU.add).then_inc(s_bm, 1)
                pairs(nb, N_OUT // 2)
                for g, nf, nu, nd, f0 in group_bases(h):
                    F = 2 + NF * h + f0
                    with pool.Fori(0, nf // 2, 1) as i:
                        for u in range(2):
                            for j in (2, 3):
                                w_lo_unit((nu + j) % 2, nu + j + 1 + 2 * u + 4 * i)
                            pool.wait_ge(s_ahi, F + 1 + u + 2 * i)
                            pool.tensor_tensor(r(act_lo[:, u + 2 * i]), act_f[:, u], act_hi[:, u + 2 * i],
                                               ALU.subtract).then_inc(s_alo, 1)
                    pairs(nd, KD // 2)

        @block.scalar
        def _(act):
            def slink(ins):
                link(act, s_sc_, ins)

            def split_hi(slot, ready_sem, ready, used):
                act.wait_ge(ready_sem, ready)
                if used is not None:
                    act.wait_ge(s_gemm, used)
                act.activation(r(w_hi[:, slot]), w_raw[:, slot], ACT.Copy).then_inc(s_whi, 1)

            def hi(n):
                rs, rv = raw_ready(n)
                split_hi(n % 2, rs, rv, n - 1 if n >= 2 else None)

            def hi_in(n, i, step=2):
                rs, rv = raw_ready(n)
                split_hi(n % 2, rs, rv + 8 * step * i, n - 1 + step * i)

            act.wait_ge(s_cload, 16)
            act.activation(cond[:], cond[:], ACT.Silu).then_inc(s_cond, 1)
            act.wait_ge(s_f, 1)
            act.activation(fbias[:].rearrange("p (a b) -> p a b", a=3), ps[0:8, 4:7, 0:384],
                           ACT.Copy).then_inc(s_fs, 1)
            act.wait_ge(s_fs, 1)
            act.dma_start(f_dram.ap(), fbias[:]).then_inc(s_fd, 16)
            act.wait_ge(s_fd, 16)

            def squares(n0, count, src, ring):
                for n in range(n0, n0 + count):
                    if n >= 2:
                        act.wait_ge(s_sa, n - 1)
                    act.activation(ring[:, n % 2], src(n - n0), ACT.Square, scale=D ** -0.5).then_inc(s_sq, 1)

            def root(m, bank):
                act.wait_ge(s_ms, m + 1)
                act.activation(root_s[:], ps[:, bank, 0:HB], ACT.Sqrt, bias=eps[:]).then_inc(s_sd, 1)

            for i in range(2):
                act.wait_ge(s_x[i], 16)
                squares(KD * i, KD, lambda g: x_sb[:, g, HALF * i:HALF * i + HALF], sq_x)
                root(i, 4 + i)

            def split_tiles(t0, n0, count, tmp, hi_t, bias):
                for g in range(count):
                    act.wait_ge(s_tt, t0 + g + 1)
                    act.activation(r(hi_t(g)), tmp[:, g % 2], ACT.Identity, bias=bias(g)).then_inc(s_nh, 1)


            for i in range(4):
                for j in (2, 3):
                    act.wait_ge(s_adp, 2 * i + j - 1)
                    c = ada_tiles(i)[j]
                    t = w_ada0[:, i % 2, j]
                    act.activation(t, t, ACT.Copy, accum_out=ada[:, c:c + 1]).then_inc(s_ads, 1)
                if i == 0:
                    hi(0)
                split_tiles(4 * i, 4 * i, 4, h_t, lambda n: h_hi[:, 2 * i + n // 2, HALF * (n % 2):HALF * (n % 2) + HALF],
                            lambda n: mod[:, 2 * i + n // 2:2 * i + n // 2 + 1])


            def relus(quad):
                for i in range(4 * quad, 4 * quad + 4):
                    n = DOTS[i][2]
                    act.wait_ge(s_dot, i + 1)
                    if i >= 4:
                        act.wait_ge(s_acc, i - 3)
                    act.activation(relu_r[:, i % 4, 0:n], ps[:, 4 + i % 4, 0:n], ACT.Relu,
                                   scale=IDX_DIM ** -0.5).then_inc(s_relu, 1)

            def v_evac(g):
                act.wait_ge(s_vt, g + 1)
                col, blk = g // 2, HB * (g % 2)
                dst = v[:, blk:blk + HB, P * col:P * col + P] if col < 2 else dv[:, blk:blk + HB]
                act.activation(dst, ps[:, 6].rearrange("p (b c) -> p b c", b=HB), ACT.Copy).then_inc(s_ve, 1)

            def evac(n):
                act.wait_ge(s_gemm, n + 1)
                src = ps[:, 2 * (n % 2):2 * (n % 2) + 2].rearrange("p b c -> p (b c)")
                f = ACT.Copy
                if n == U_KIWI:
                    for g in range(4):
                        act.activation(ki[32 * g:32 * g + 32], src[0:32], ACT.Copy)
                    dst = kiwi[:]
                elif n < U_KIWI:
                    dst = qi[:, n]
                elif n < U_K:
                    dst = q[:, n - U_Q]
                elif n < U_V:
                    dst = k[:, n - U_K]
                elif n < U_C:
                    dst = stage[n - U_V][:]
                elif n < U_DQ:
                    dst = zc[n - U_C][:, 16:]
                elif n < U_DK:
                    dst = dq[:, n - U_DQ]
                elif n == U_DK:
                    dst = dk[:]
                elif n == U_DV:
                    act.wait_ge(s_vt, 4)
                    dst = stage[0][:]
                else:
                    if n == U_A:
                        act.wait_ge(s_acc, len(DOTS))
                    dst, f = za_t[:, n - U_A], ACT.Gelu_apprx_tanh
                act.activation(dst, src, f).then_inc(s_ev, 1)

            for n in range(N_IN):
                hi(n + 1)
                step = n - DOT_UNIT
                if 0 <= step < DOT_STEPS:
                    relus(2 * step)
                evac(n)
                if 0 <= step < DOT_STEPS:
                    relus(2 * step + 1)
                if n == 13:
                    for g in range(4):
                        v_evac(g)
                if n == 16:
                    for g in range(4, 6):
                        v_evac(g)
            act.wait_ge(s_ada, 40)
            act.dma_start(swa_bias[:], bass.AP(tensor=f_dram, offset=HEADS * (S + P), ap=[[1, P], [S + P, HEADS], [1, 2 * P]])).then_inc(s_swb, 16)
            for b in range(NBLK):
                act.wait_ge(s_gt, b + 1)
                act.activation(gm[:, b], ps[:, 4 + b % 2], ACT.Copy).then_inc(s_ge, 1)
            act.wait_ge(s_lnv, 1)
            act.activation(st2[:, 0:32], st[:, 0:32], ACT.Sqrt, bias=eps[:], scale=1.0 / 64).then_inc(s_lns, 1)
            hi(N_IN + 1)
            act.wait_ge(s_vn, 1)
            act.dma_start(bias_0[:], bias_rows).then_inc(s_tb, 16)

            for b in range(NBLK):
                c0 = P if b == 0 else 0
                act.wait_ge(s_wm, b + 1)
                lg = logit[:, b % 2].rearrange("p (h c) -> p h c", h=HEADS)
                for h in range(HEADS):
                    act.activation(lg[:, h, c0:], lg[:, h, c0:], ACT.Exp, bias=sm_neg[:, b % 2, h:h + 1],
                                   accum_out=sm_sum[:, b % 2, h:h + 1])
                act.activation(sm_snk[:, b % 2], sm_snk[:, b % 2], ACT.Exp).then_inc(s_wx, 1)
                for j in range(2):
                    act.wait_ge(s_wt, 2 * b + j + 1)
                    if b >= 2 and j == 0:
                        act.wait_ge(s_wo, b - 1)
                    src = ps[:, 6 if j == 0 else 1].rearrange("p (h c) -> p h c", h=4)
                    if c0:
                        act.activation(p_t[:, b % 2, 4 * j + 1:4 * j + 4:2], src[:, 1::2], ACT.Copy).then_inc(s_we, 1)
                    else:
                        act.activation(p_t[:, b % 2, 4 * j:4 * j + 4], src, ACT.Copy).then_inc(s_we, 1)

            n_pt = [0]
            for h in range(2):
                nb = half_base(h)
                def exps(i):
                    b = HB * h + i // 2
                    for e in range(2):
                        hd = 2 * (i % 2) + e
                        I = HEADS * b + hd
                        lg = logit4[:, I % 4, 0:P * (b + 1)]
                        act.wait_ge(s_am, I + 1)
                        act.activation(lg, lg, ACT.Exp, bias=sm_neg[:, b % 2, hd:hd + 1],
                                       accum_out=sm_sum[:, b % 2, hd:hd + 1]).then_inc(s_ax, 1)

                def probs_back(i):
                    b = HB * h + i // 2
                    for e in range(2):
                        I = HEADS * b + 2 * (i % 2) + e
                        for t in range(0, b + 1, 4):
                            m = min(4, b + 1 - t)
                            act.wait_ge(s_at, n_pt[0] + 1)
                            if t == 0 and I >= 2:
                                act.wait_ge(s_ao, I - 1)
                            act.activation(p_t[:, I % 2, t:t + m],
                                           ps[:, 6 if n_pt[0] % 2 == 0 else 1].rearrange("p (h c) -> p h c", h=4)[:, 0:m],
                                           ACT.Copy).then_inc(s_ae, 1)
                            n_pt[0] += 1

                def y_squares(b):
                    act.wait_ge(s_ay, b + 1)
                    if b == 0:
                        act.wait_ge(s_gy, NBLK)
                        act.wait_ge(s_py, NBLK)
                        act.wait_ge(s_wy, NBLK)
                    else:
                        act.wait_ge(s_yq, 4 * b)
                    for m in range(4):
                        at_ = 4 * (b % HB) + m
                        act.activation(junk[:, m], y[:, b, W * m:W * m + W], ACT.Square,
                                       accum_out=st[:, at_:at_ + 1]).then_inc(s_yq, 1)

                exps(0)
                for i in range(2 * HB):
                    probs_back(i)
                    if i % 2 == 0 and i > 0:
                        y_squares(HB * h + i // 2 - 1)
                    if i + 1 < 2 * HB:
                        exps(i + 1)
                y_squares(HB * h + HB - 1)
                act.wait_ge(s_yq, 16 * (h + 1))
                act.activation(st2[:, 0:16], st[:, 0:16], ACT.Sqrt, bias=eps[:], scale=1.0 / W).then_inc(s_yr, 1)
                if h == 1:
                    act.wait_ge(s_fo, KD)
                act.dma_start(x2[:], a["x"].rearrange("(k p) s -> p k s", p=P)[:, :, HALF * h:HALF * h + HALF]
                              ).then_inc(s_x2, 16)
                n0 = 16 + 16 * h
                for g in range(KD):
                    act.wait_ge(s_nt, KD * h + g + 1)
                    act.activation(r(y_hi[:, g]), ps[:, Y_BANKS[g % 4]], ACT.Copy, scale=mix_g[:, g:g + 1]).then_inc(s_nh, 1)
                if h == 0:
                    act.dma_start(bias_1[:], bias_rows).then_inc(s_tb, 16)

                def column_loop(base, J, q0):
                    with act.Fori(0, KD // 2, 1) as i:
                        for j in range(2):
                            hi_in(base + 2 + j, i)
                            if q0:
                                act.wait_ge(s_sa, q0 + j - 1 + 2 * i)
                                act.wait_ge(s_res, J + j + 3 + 2 * i)
                                act.activation(sq2[:, j], x2[:, j + 2 * i], ACT.Square,
                                               scale=D ** -0.5).then_inc(s_sq, 1)

                J = 4 * KD * h
                column_loop(nb, J, n0)
                root(2 + 2 * h, 6)
                split_tiles(16 + KD * h, n0 + KD, KD, h2_t, lambda g: h2_hi[:, g],
                            lambda g: mod[:, 3 * KD + g:3 * KD + g + 1])
                if h == 1:
                    for s_ in s_out:
                        act.wait_ge(s_, 16 * 2)
                for g, nf, nu, nd, f0 in group_bases(h):
                    F = 2 + NF * h + f0
                    with act.Fori(0, nf // 2, 1) as i:
                        for u in range(2):
                            f = F + u + 2 * i
                            hi_in(nu + 2 + 2 * u, i, 4)
                            act.wait_ge(s_conv, f - 1)
                            act.activation(conv_in[:, u, 0:2], halo[:, f0 + u + 2 * i], ACT.Copy).then_inc(s_hin, 1)
                            act.activation(conv_t[:, u], ps[:, u], ACT.Identity, bias=conv_w[:, f0 + u + 2 * i, 3:4],
                                           scale=conv_w[:, f0 + u + 2 * i, 2:3])
                            act.wait_ge(s_hin, f + 1)
                            act.activation(conv_in[:, u, 2:], ps[:, u], ACT.Copy)
                            act.activation(halo[:, f0 + u + 2 * i], ps[:, u, HALF - 2:], ACT.Copy).then_inc(s_cin, 1)
                            act.wait_ge(s_conv, f + 1)
                            act.activation(conv_t[:, u], conv_t[:, u], ACT.Gelu_apprx_tanh).then_inc(s_gelu, 1)
                            hi_in(nu + 3 + 2 * u, i, 4)
                            act.wait_ge(s_act, f + 1)
                            act.activation(r(act_hi[:, u + 2 * i]), act_f[:, u], ACT.Copy).then_inc(s_ahi, 1)
                    column_loop(nd, J + 8 + 8 * g, n0 + KD if g == 2 else 0)
                root(3 + 2 * h, 6)
                for g in range(KD):
                    act.wait_ge(s_fo, KD * h + g + 1)
                    act.dma_start(out.rearrange("(k p) s -> p k s", p=P)[:, g, HALF * h:HALF * h + HALF],
                                  fin_o[:, g % 4]).then_inc(s_out[g % 4], 16)
            for s_ in s_out:
                act.wait_ge(s_, 16 * 4)

        @block.vector
        def _(dve):
            def vlink(ins):
                link(dve, s_vc, ins)

            dve.wait_ge(s_par, 16 * 12)

            def add_squares(n0, count, ring, acc):
                for n in range(n0, n0 + count):
                    dve.wait_ge(s_sq, n + 1)
                    dve.tensor_tensor(acc, acc, ring[:, n % 2], ALU.add).then_inc(s_sa, 1)
                    dve.wait_ge(s_sa, n + 1)

            def root(m, diag):
                dve.wait_ge(s_sd, m + 1)
                vlink(dve.reciprocal(root_r[:], root_s[:]))
                for t in range(HB):
                    ins = dve.tensor_scalar(diag[:, P * t:P * t + P], ident[:], root_r[:, t:t + 1], None, ALU.mult)
                ins.then_inc(s_dg, 1)
                dve.wait_ge(s_bc, m + 1)

            def ada_tile(c, src, loaded, value):
                dve.wait_ge(loaded, value)
                dve.wait_ge(s_cond, 1)
                dve.scalar_tensor_tensor(out=src, in0=src, scalar=1.0, in1=cond[:], op0=ALU.mult, op1=ALU.mult,
                                         accum_out=ada[:, c:c + 1]).then_inc(s_ada, 1)

            for i in range(2):
                vlink(dve.memset(sum_x[:], 0.0))
                add_squares(KD * i, KD, sq_x, sum_x[:])
                root(i, diag_x[:])

            def split_tiles(t0, n0, count, make, tmp, lo_t, shift):
                if n0:
                    dve.wait_ge(s_nl, n0)
                make(0).then_inc(s_tt, 1)
                for g in range(count):
                    if g + 1 < count:
                        if g >= 1:
                            dve.wait_ge(s_nl, n0 + g)
                        make(g + 1).then_inc(s_tt, 1)
                    dve.wait_ge(s_nh, n0 + g + 1)
                    lo_, hi_ = lo_t(g)
                    dve.scalar_tensor_tensor(out=r(lo_), in0=tmp[:, g % 2], scalar=shift(g), in1=hi_,
                                             op0=ALU.add, op1=ALU.subtract).then_inc(s_nl, 1)

            def xcols(t, n):
                return t[:, n // 2, HALF * (n % 2):HALF * (n % 2) + HALF]

            for i in range(4):
                for j in range(2):
                    ada_tile(2 * i + j, w_ada0[:, i % 2, j], s_aw0[i], 32)
                dve.wait_ge(s_ada, 2 * i + 2)
                dve.wait_ge(s_ads, 2 * i + 2)
                for c0 in (2 * i, KD + 2 * i):
                    ins = dve.tensor_tensor(mod[:, c0:c0 + 2], ada[:, c0:c0 + 2], b_ada[:, c0:c0 + 2], ALU.add)
                vlink(ins)
                sg = scale_g[:, 0, 2 * i:2 * i + 2]
                vlink(dve.tensor_scalar(sg, mod[:, KD + 2 * i:KD + 2 * i + 2], 1.0, None, ALU.add))
                vlink(dve.tensor_tensor(sg, sg, norm_g[:, 0, 2 * i:2 * i + 2], ALU.mult))
                split_tiles(4 * i, 4 * i, 4,
                            lambda n, i=i: dve.scalar_tensor_tensor(
                                out=h_t[:, n % 2], in0=xcols(x_sb, 4 * i + n),
                                scalar=scale_g[:, 0, 2 * i + n // 2:2 * i + n // 2 + 1], in1=ps[:, 4 + n % 2],
                                op0=ALU.mult, op1=ALU.mult),
                            h_t, lambda n, i=i: (xcols(h_lo, 4 * i + n), xcols(h_hi, 4 * i + n)),
                            lambda n, i=i: mod[:, 2 * i + n // 2:2 * i + n // 2 + 1])

            dve.wait_ge(s_wi, 1)
            dve.tensor_scalar(wis[:], ps[:, 6, 0:48].rearrange("p (b h) -> p b h", b=6), IDX_HEADS ** -0.5, None,
                              ALU.mult).then_inc(s_wis, 1)
            dve.wait_ge(s_wis, 1)
            def accumulate(quad):
                for i in range(4 * quad, 4 * quad + 4):
                    b, k0, n, h = DOTS[i]
                    dst = score[:, SC[b] + k0:SC[b] + k0 + n]
                    wgt = wis[:, b - 2, h:h + 1]
                    dve.wait_ge(s_relu, i + 1)
                    if h == 0:
                        dve.tensor_scalar(dst, relu_r[:, i % 4, 0:n], wgt, None, ALU.mult).then_inc(s_acc, 1)
                    else:
                        dve.wait_ge(s_acc, i)
                        dve.scalar_tensor_tensor(out=dst, in0=relu_r[:, i % 4, 0:n], scalar=wgt, in1=dst,
                                                 op0=ALU.mult, op1=ALU.add).then_inc(s_acc, 1)
                if h == IDX_HEADS - 1 and k0 + n == P * (b + 1):
                    dve.wait_ge(s_acc, 4 * quad + 4)
                    vlink(dve.memset(score[0:64, SC[b] + P * (b + 1) - 64:SC[b] + P * (b + 1)], NO_KEY))

            def sc_of(b):
                return score[:, SC[b]:SC[b] + P * (b + 1)]

            def wait_apart(s_, value):
                dve.wait_ge(s_, value)
                dve.memset(tick[:], 0.0)

            def top_max(blocks, base):
                wait_apart(s_rep, base)
                for b in blocks:
                    dve.max(top8[:, b - 2], sc_of(b)).then_inc(s_max, 1)

            def top_mark(blocks, base):
                wait_apart(s_max, base + len(blocks))
                for b in blocks:
                    dve.match_replace(sc_of(b), top8[:, b - 2], sc_of(b), TAKEN).then_inc(s_rep, 1)

            def top_round(blocks, base):
                top_max(blocks, base)
                top_mark(blocks, base)

            def mask_of(b):
                vlink(dve.tensor_scalar(sc_of(b), sc_of(b), TAKEN_BELOW, NEG, ALU.is_gt, ALU.mult))

            taken = 0
            for step in range(ADA_STEPS):
                if step < DOT_STEPS:
                    accumulate(2 * step)
                for c in (16 + 2 * step, 17 + 2 * step):
                    ada_tile(c, w_ada1[:, c % 2], s_aw1[c % 2], 16 * (step + 1))
                if step < DOT_STEPS:
                    accumulate(2 * step + 1)
                if step in early_steps:
                    with dve.Fori(0, early_steps[step], 1) as i:
                        top_round(EARLY, len(EARLY) * (taken + i))
                    taken += early_steps[step]
            dve.wait_ge(s_rep, len(EARLY) * ROUNDS)
            for b in EARLY:
                mask_of(b)
            dve.sem_inc(s_mk, 1)
            dve.wait_ge(s_ada, 40)
            vlink(dve.tensor_tensor(mod[:, 16:48], ada[:, 16:48], b_ada[:, 16:48], ALU.add))
            vlink(dve.tensor_scalar(scale_g[:, 1], mod[:, 4 * KD:5 * KD], 1.0, None, ALU.add))
            dve.tensor_tensor(scale_g[:, 1], scale_g[:, 1], norm_g[:, 1], ALU.mult).then_inc(s_mod, 1)

            dve.wait_ge(s_ge, NBLK)
            v4 = gm[:, :, W:]
            mean = st3[:, 0:32]

            def g64(ap):
                return ap.rearrange("p b (g c) -> p b g c", c=64)

            def per_g(ap):
                return ap.rearrange("p (b g) -> p b g", g=4)

            for b in range(NBLK):
                ins = dve.tensor_reduce(st3[:, 4 * b:4 * b + 4], v4[:, b].rearrange("p (g c) -> p g c", c=64), AX, ALU.add)
            vlink(ins)
            vlink(dve.tensor_scalar(mean, mean, 1.0 / 64, None, ALU.mult))
            for b in range(NBLK):
                ins = dve.tensor_tensor(vn[:, b].rearrange("p (g c) -> p g c", c=64),
                                        v4[:, b].rearrange("p (g c) -> p g c", c=64),
                                        st3[:, 4 * b:4 * b + 4].unsqueeze(2).to_broadcast([P, 4, 64]), ALU.subtract)
            vlink(ins)
            vlink(dve.tensor_tensor(gm_sq[:], vn[:], vn[:], ALU.mult))
            for b in range(NBLK):
                ins = dve.tensor_reduce(st[:, 4 * b:4 * b + 4], gm_sq[:, b].rearrange("p (g c) -> p g c", c=64), AX, ALU.add)
            ins.then_inc(s_lnv, 1)
            dve.wait_ge(s_lns, 1)
            vlink(dve.reciprocal(st3[:, 0:32], st2[:, 0:32]))
            for b in range(NBLK):
                x_ = vn[:, b].rearrange("p (g c) -> p g c", c=64)
                ins = dve.tensor_tensor(x_, x_, st3[:, 4 * b:4 * b + 4].unsqueeze(2).to_broadcast([P, 4, 64]), ALU.mult)
            ins.then_inc(s_vn, 1)

            dve.wait_ge(s_swb, 16)
            vlink(dve.memset(swa_bias[:, :, 192:256], NEG))
            vlink(dve.memset(swa_bias[64:128, :, 128:192], NEG))
            vlink(dve.memset(swa_bias[0:64, :, 0:64], NEG))

            def swa_softmax(b):
                c0 = P if b == 0 else 0
                lg = logit[:, b % 2].rearrange("p (h c) -> p h c", h=HEADS)
                src = ps[:, 4 - 2 * (b % 2):6 - 2 * (b % 2)].rearrange("p a (h c) -> p (a h) c", h=2)
                dve.wait_ge(s_wl, b + 1)
                if b >= 2:
                    dve.wait_ge(s_wt, 2 * b - 2)
                vlink(dve.scalar_tensor_tensor(out=lg[:, :, c0:], in0=src[:, :, c0:], scalar=HD ** -0.5,
                                               in1=backwards(swa_bias[:, :, 0:2 * P - c0]), op0=ALU.mult, op1=ALU.add))
                vlink(dve.tensor_reduce(sm_max[:, b % 2], lg[:, :, c0:], AX, ALU.max))
                vlink(dve.tensor_tensor(sm_max[:, b % 2], sm_max[:, b % 2], sinks[:], ALU.max))
                vlink(dve.tensor_tensor(sm_snk[:, b % 2], sinks[:], sm_max[:, b % 2], ALU.subtract))
                dve.tensor_scalar(sm_neg[:, b % 2], sm_max[:, b % 2], -1.0, None, ALU.mult).then_inc(s_wm, 1)

            def swa_out(b):
                dve.wait_ge(s_wx, b + 1)
                vlink(dve.tensor_tensor(sm_rec[:, b % 2], sm_sum[:, b % 2], sm_snk[:, b % 2], ALU.add))
                vlink(dve.reciprocal(sm_rec[:, b % 2], sm_rec[:, b % 2]))
                dve.wait_ge(s_wo, b + 1)
                dve.tensor_tensor(y[:, b, 3 * W:].rearrange("p (h c) -> p h c", h=HEADS),
                                  ps[:, 7 if b % 2 == 0 else 0, 0:W].rearrange("p (h c) -> p h c", h=HEADS),
                                  sm_rec[:, b % 2].unsqueeze(2).to_broadcast([P, HEADS, HD]),
                                  ALU.mult).then_inc(s_wy, 1)

            swa_softmax(0)
            dve.wait_ge(s_pl, 1)
            for b in range(NBLK):
                if b + 1 < NBLK:
                    swa_softmax(b + 1)
                swa_out(b)
            for b in range(NBLK):
                dve.wait_ge(s_gs, b + 1)
                vlink(dve.tensor_tensor(vn[:, b].rearrange("p (g c) -> p g c", c=64),
                                        ps[:, 6 if b % 2 == 0 else 1, 0:W].rearrange("p (g c) -> p g c", c=64),
                                        gm_b[:].unsqueeze(2).to_broadcast([P, 4, 64]), ALU.add))
                dve.tensor_tensor(y[:, b, 0:W], vn[:, b], gm[:, b, 0:W], ALU.mult).then_inc(s_gy, 1)
            for b in range(NBLK):
                dve.wait_ge(s_pm, b + 1)
                for par, bank in enumerate((7, 0) if b % 2 == 0 else (6, 1)):
                    cols = slice(par * 64, par * 64 + 64)
                    ins = dve.tensor_tensor(
                        y[:, b, 2 * W:3 * W].rearrange("p (a c) -> p a c", a=2)[:, :, cols],
                        ps[:, bank, 0:W].rearrange("p (a c) -> p a c", a=2)[:, :, cols],
                        pool_s[:].rearrange("p (a c) -> p a c", a=2)[:, :, cols], ALU.mult)
                ins.then_inc(s_py, 1)

            R0 = 2 * ROUNDS
            m = len(LATE_BLOCKS)
            rounds = [0]
            for h in range(2):
                nb = half_base(h)
                dve.wait_ge(s_tb, 16 * (h + 1))
                bias_t = bias_1 if h else bias_0
                dve.memset(bias_t[0:64, :, 0:64], NEG).then_inc(s_bi, 1)
                dve.wait_ge(s_bi, h + 1)

                def soft(i):
                    b = HB * h + i // 2
                    n = P * (b + 1)
                    for e in range(2):
                        hd = 2 * (i % 2) + e
                        I = HEADS * b + hd
                        dve.wait_ge(s_al, I + 1)
                        if I >= 4:
                            dve.wait_ge(s_ao, I - 3)
                        if b >= 2:
                            dve.wait_ge(s_bm, I - 7)
                            bias = bias_m[:, I % 2, 0:n]
                        else:
                            bias = backwards(bias_t[:, hd, 0:n])
                        dve.scalar_tensor_tensor(out=logit4[:, I % 4, 0:n],
                                                 in0=ps[:, 2 + 2 * e:4 + 2 * e].rearrange("p a c -> p (a c)")[:, 0:n],
                                                 scalar=HD ** -0.5, in1=bias,
                                                 op0=ALU.mult, op1=ALU.add).then_inc(s_ar, 1)
                    for e in range(2):
                        hd = 2 * (i % 2) + e
                        I = HEADS * b + hd
                        dve.wait_ge(s_ar, I + 1)
                        vlink(dve.tensor_reduce(sm_max[:, b % 2, hd:hd + 1], logit4[:, I % 4, 0:n], AX, ALU.max))
                        dve.tensor_scalar(sm_neg[:, b % 2, hd:hd + 1], sm_max[:, b % 2, hd:hd + 1], -1.0, None,
                                          ALU.mult).then_inc(s_am, 1)

                soft(0)
                for i in range(2 * HB):
                    if i + 1 < 2 * HB:
                        soft(i + 1)
                    if i % 2 == 1:
                        b = HB * h + i // 2
                        dve.wait_ge(s_ax, HEADS * (b + 1))
                        vlink(dve.reciprocal(sm_rec[:, b % 2], sm_sum[:, b % 2]))
                        dve.wait_ge(s_ao, HEADS * (b + 1))
                        dve.tensor_tensor(y[:, b, W:2 * W].rearrange("p (h c) -> p h c", h=HEADS),
                                          ps[:, 7 if b % 2 == 0 else 0, 0:W].rearrange("p (h c) -> p h c", h=HEADS),
                                          sm_rec[:, b % 2].unsqueeze(2).to_broadcast([P, HEADS, HD]),
                                          ALU.mult).then_inc(s_ay, 1)
                dve.wait_ge(s_yr, h + 1)
                vlink(dve.reciprocal(st3[:, 0:16], st2[:, 0:16]))
                for m_ in range(4):
                    dve.tensor_tensor(diag_y[:, m_], ident[:].unsqueeze(1).to_broadcast([P, HB, P]),
                                      st3[:, 0:16].rearrange("p (t m) -> p m t", m=4)[:, m_].unsqueeze(2)
                                      .to_broadcast([P, HB, P]), ALU.mult).then_inc(s_yn, 1)
                n0 = 16 + 16 * h
                for g in range(KD):
                    dve.wait_ge(s_nh, n0 + g + 1)
                    dve.scalar_tensor_tensor(out=r(y_lo[:, g]), in0=ps[:, Y_BANKS[g % 4]], scalar=mix_g[:, g:g + 1],
                                             in1=y_hi[:, g], op0=ALU.mult, op1=ALU.subtract).then_inc(s_nl, 1)

                def column_loop(base, gate, q0, beside):
                    if q0:
                        vlink(dve.memset(sum2[:], 0.0))
                    with dve.Fori(0, KD // 2, 1) as i:
                        for j in range(2):
                            dve.wait_ge(s_gemm, base + j + 1 + 2 * i)
                            o = x2[:, j + 2 * i]
                            dve.scalar_tensor_tensor(out=o, in0=ps[:, 2 + j], scalar=mod[:, bass.ds(gate + j + 2 * i, 1)],
                                                     in1=o, op0=ALU.mult, op1=ALU.add).then_inc(s_res, 1)
                            if q0:
                                dve.wait_ge(s_sq, q0 + j + 1 + 2 * i)
                                dve.wait_ge(s_sa, q0 + j + 2 * i)
                                dve.tensor_tensor(sum2[:], sum2[:], sq2[:, j], ALU.add).then_inc(s_sa, 1)
                        beside(i)

                dve.wait_ge(s_x2, 16 * (h + 1))
                column_loop(nb, 2 * KD, n0, lambda i: None)
                root(2 + 2 * h, diag2[:])
                split_tiles(16 + KD * h, n0 + KD, KD,
                            lambda g: dve.scalar_tensor_tensor(out=h2_t[:, g % 2], in0=x2[:, g],
                                                               scalar=scale_g[:, 1, g:g + 1], in1=ps[:, 6],
                                                               op0=ALU.mult, op1=ALU.mult),
                            h2_t, lambda g: (h2_lo[:, g], h2_hi[:, g]),
                            lambda g: mod[:, 3 * KD + g:3 * KD + g + 1])
                for g, nf, nu, nd, f0 in group_bases(h):
                    F = 2 + NF * h + f0
                    with dve.Fori(0, nf // 2, 1) as i:
                        for u in range(2):
                            f = F + u + 2 * i
                            dve.wait_ge(s_cin, f + 1)
                            dve.wait_ge(s_act, f - 1)
                            dve.scalar_tensor_tensor(out=conv_t[:, u], in0=conv_in[:, u, 1:HALF + 1],
                                                     scalar=conv_w[:, f0 + u + 2 * i, 1:2], in1=conv_t[:, u],
                                                     op0=ALU.mult, op1=ALU.add).then_inc(s_c1, 1)
                            dve.wait_ge(s_c1, f + 1)
                            dve.scalar_tensor_tensor(out=conv_t[:, u], in0=conv_in[:, u, 0:HALF],
                                                     scalar=conv_w[:, f0 + u + 2 * i, 0:1], in1=conv_t[:, u],
                                                     op0=ALU.mult, op1=ALU.add).then_inc(s_conv, 1)
                            base = R0 + m * rounds[0] + m * u + 2 * m * i
                            if h == 0:
                                top_max(LATE_BLOCKS, base)
                            dve.wait_ge(s_gelu, f + 1)
                            dve.wait_ge(s_gemm, nu + 2 + 2 * u + 4 * i)
                            dve.wait_ge(s_alo, f - 1)
                            dve.tensor_tensor(act_f[:, u], conv_t[:, u], ps[:, 4 + u], ALU.mult).then_inc(s_act, 1)
                            if h == 0:
                                top_mark(LATE_BLOCKS, base)
                    if h == 0:
                        rounds[0] += nf
                    q0 = n0 + KD if g == 2 else 0
                    if h == 0 and g < 2:
                        column_loop(nd, 5 * KD, q0, lambda i: top_round(LATE_BLOCKS, R0 + m * rounds[0] + m * i))
                        rounds[0] += KD // 2
                    else:
                        if h == 0:
                            top_round(LATE_BLOCKS, R0 + m * rounds[0])
                            rounds[0] += 1
                        column_loop(nd, 5 * KD, q0, lambda i: None)
                root(3 + 2 * h, diag2[:])
                for g in range(KD):
                    if h or g >= 4:
                        dve.wait_ge(s_out[g % 4], 16 * (2 * h + (g >= 4)))
                    dve.scalar_tensor_tensor(out=fin_o[:, g % 4], in0=x2[:, g], scalar=fin_g[:, g:g + 1],
                                             in1=ps[:, 6], op0=ALU.mult, op1=ALU.mult).then_inc(s_fo, 1)
                if h == 0:
                    while rounds[0] < ROUNDS:
                        top_round(LATE_BLOCKS, R0 + m * rounds[0])
                        rounds[0] += 1
                    dve.wait_ge(s_rep, R0 + m * ROUNDS)
                    for b in LATE_BLOCKS:
                        mask_of(b)
                    dve.sem_inc(s_mk, 1)

        @block.tensor
        def _(pe):
            for s_ in (s_hin, s_cin, s_conv, s_gelu, s_act, s_ahi, s_alo, s_c1):
                pe.sem_inc(s_, 2)
            pe.sem_inc(s_res, 2)
            pe.wait_ge(s_rel, 32)
            for i in range(3):
                last = pe.matmul(ps[0:8, 4 + i, 0:384], rel[:], onehot[:, 384 * i:384 * i + 384], start=True, stop=True)
            last.then_inc(s_f, 1)

            def over_features(m, bank, sums, diag):
                pe.wait_ge(s_sa, KD * (m + 1))
                for t in range(HB):
                    mm = pe.matmul(ps[:, bank, t:t + 1], sums[:, P * t:P * t + P], ones[:, 0:1], start=True, stop=True)
                mm.then_inc(s_ms, 1)
                pe.wait_ge(s_dg, m + 1)
                pe.matmul(ps[:, bank], ones[:], diag[:], start=True, stop=True).then_inc(s_bc, 1)

            pe.wait_ge(s_eps, 4)
            pe.wait_ge(s_fs, 1)
            over_features(0, 4, sum_x, diag_x)
            over_features(1, 5, sum_x, diag_x)

            def gemm(slot, nk, parts, ready, *waits, tiles=None, beside=None):
                pe.wait_ge(s_wlo, ready)
                for s_, val in waits:
                    pe.wait_ge(s_, val)
                for kk in range(nk):
                    first, last_k = kk == 0, kk == nk - 1
                    if tiles:
                        pe.wait_ge(*tiles(kk))
                    for bank, xh, xl in parts:
                        pe.matmul(ps[:, bank], r(w_hi[:, slot, kk]), r(xh(kk)), start=first, stop=False)
                        pe.matmul(ps[:, bank], r(w_hi[:, slot, kk]), r(xl(kk)), start=False, stop=False)
                    for bank, xh, xl in parts:
                        mm = pe.matmul(ps[:, bank], r(w_lo[:, slot, kk]), r(xh(kk)), start=False, stop=last_k)
                    if beside and not last_k:
                        beside(kk)
                mm.then_inc(s_gemm, 1)

            def in_parts(n):
                return [(2 * (n % 2) + i,
                         lambda kk, i=i: h_hi[:, kk, HALF * i:HALF * i + HALF],
                         lambda kk, i=i: h_lo[:, kk, HALF * i:HALF * i + HALF]) for i in range(2)]

            def dots(quad):
                if quad == 0:
                    pe.wait_ge(s_wis, 1)
                    pe.wait_ge(s_ev, U_KIWI + 1)
                else:
                    pe.wait_ge(s_relu, 4 * quad)
                for i in range(4 * quad, 4 * quad + 4):
                    b, k0, n, h = DOTS[i]
                    rows = slice(32 * (h % 4), 32 * (h % 4) + 32)
                    pe.matmul(ps[:, 4 + i % 4, 0:n], qi[rows, h // 4, P * b:P * b + P], ki[rows, k0:k0 + n],
                              start=True, stop=True).then_inc(s_dot, 1)

            def v_turn(g, src):
                if g > 0:
                    pe.wait_ge(s_ve, g)
                for t in range(HB):
                    blk = HB * (g % 2) + t
                    tr = pe.transpose(ps[:, 6, P * t:P * t + P], src[:, P * blk:P * blk + P], ident[:])
                tr.then_inc(s_vt, 1)

            for n in range(N_IN):
                if n == DOT_UNIT:
                    pe.wait_ge(s_ev, U_KIWI + 1)
                    pe.wait_ge(s_nl, 16)
                    for b in TOP_BLOCKS:
                        mm = pe.matmul(ps[:, 6, 8 * (b - 2):8 * (b - 2) + 8], kiwi[:, P * b:P * b + P],
                                       ident[:, WI_COL:WI_COL + IDX_HEADS], start=True, stop=True)
                    mm.then_inc(s_wi, 1)
                step = n - DOT_UNIT
                gemm(n % 2, KD, in_parts(n), n + 1, *([(s_ev, n - 1)] if n >= 2 else []),
                     tiles=(lambda kk: (s_nl, 2 * kk + 2)) if n == 0 else None,
                     beside=(lambda kk: {2: lambda: dots(2 * step), 6: lambda: dots(2 * step + 1)}.get(kk, int)())
                     if 0 <= step < DOT_STEPS else None)
                if n == 13:
                    pe.wait_ge(s_relu, len(DOTS))
                    pe.wait_ge(s_ev, U_V + 2)
                    for g in range(4):
                        v_turn(g, stage[g // 2])
                if n == 16:
                    pe.wait_ge(s_ev, U_DV + 1)
                    for g in range(4, 6):
                        v_turn(g, stage[0])

            pe.wait_ge(s_ev, N_IN)
            pe.wait_ge(s_relu, len(DOTS))
            for b in range(NBLK):
                if b >= 2:
                    pe.wait_ge(s_ge, b - 1)
                for t in range(4):
                    tr = pe.transpose(ps[:, 4 + b % 2, P * t:P * t + P], za_t[:, t, P * b:P * b + P], ident[:])
                tr.then_inc(s_gt, 1)

            pe.wait_ge(s_ve, 6)
            pe.wait_ge(s_ge, NBLK)
            pe.wait_ge(s_mod, 1)

            def swa_logits(b):
                c0 = P if b == 0 else 0
                if b >= 2:
                    pe.wait_ge(s_wm, b - 1)
                bank = 4 - 2 * (b % 2)
                for h in range(HEADS):
                    rows = slice(64 * (h // 2), 64 * (h // 2) + 64)
                    mm = pe.matmul(ps[:, bank + h // 2, 2 * P * (h % 2) + c0:2 * P * (h % 2) + 2 * P],
                                   dq[rows, h % 2, P * b:P * b + P], dk[rows, P * (b - 1) + c0:P * (b + 1)],
                                   start=True, stop=True)
                mm.then_inc(s_wl, 1)

            swa_logits(0)
            for b in range(NBLK):
                if b + 1 < NBLK:
                    swa_logits(b + 1)
                cs = [1] if b == 0 else [0, 1]
                pe.wait_ge(s_wx, b + 1)
                lg = logit[:, b % 2].rearrange("p (h c) -> p h c", h=HEADS)
                for j in range(2):
                    if b >= 1:
                        pe.wait_ge(s_we, 2 * b - 1 + j)
                    for hh in range(2):
                        for c in cs:
                            at_ = P * (2 * hh + c)
                            tr = pe.transpose(ps[:, 6 if j == 0 else 1, at_:at_ + P],
                                              lg[:, 2 * j + hh, P * c:P * c + P], ident[:])
                    tr.then_inc(s_wt, 1)
                pe.wait_ge(s_we, 2 * b + 2)
                if b >= 2:
                    pe.wait_ge(s_wy, b - 1)
                for h in range(HEADS):
                    for c in cs:
                        mm = pe.matmul(ps[:, 7 if b % 2 == 0 else 0, HD * h:HD * h + HD],
                                       p_t[:, b % 2, 2 * h + c], dv[:, b - 1 + c, HD * (h // 2):HD * (h // 2) + HD],
                                       start=(c == cs[0]), stop=(c == 1))
                mm.then_inc(s_wo, 1)
            pe.wait_ge(s_vn, 1)
            pe.wait_ge(s_eps, 4)
            pe.wait_ge(s_we, 2 * NBLK)
            for b in range(NBLK):
                if b >= 2:
                    pe.wait_ge(s_gy, b - 1)
                for g in range(4):
                    mm = pe.matmul(ps[:, 6 if b % 2 == 0 else 1, 64 * g:64 * g + 64], ws_t[:, g],
                                   vn[:, b, 64 * g:64 * g + 64], start=True, stop=True)
                mm.then_inc(s_gs, 1)
            pe.wait_ge(s_pl, 1)
            pe.wait_ge(s_wy, NBLK)
            pe.wait_ge(s_gy, NBLK)
            for b in range(NBLK):
                if b >= 2:
                    pe.wait_ge(s_py, b - 1)
                for g in range(4):
                    rows = slice(64 * (g % 2), 64 * (g % 2) + 64)
                    bank = ((7, 0) if b % 2 == 0 else (6, 1))[g % 2]
                    mm = pe.matmul(ps[:, bank, 64 * g:64 * g + 64],
                                   pooled[rows, g // 2, P * b:P * b + P], pool_w[rows, g // 2],
                                   start=True, stop=True)
                mm.then_inc(s_pm, 1)

            n_pt = [0]
            for h in range(2):
                def logits(i):
                    b, t = HB * h + i // 2, i % 2
                    I = HEADS * b + 2 * t
                    n = P * (b + 1)
                    if I > 0:
                        pe.wait_ge(s_ar, I)
                    for c in range(0, n, 512):
                        w_ = min(512, n - c)
                        for e in range(2):
                            rows = slice(64 * e, 64 * e + 64)
                            mm = pe.matmul(ps[:, 2 + 2 * e + c // 512, 0:w_], q[rows, t, P * b:P * b + P],
                                           k[rows, t, c:c + w_], start=True, stop=True)
                            if c + w_ == n:
                                mm.then_inc(s_al, 1)

                if h == 0:
                    pe.wait_ge(s_wm, NBLK)
                    pe.wait_ge(s_gy, NBLK)
                    pe.wait_ge(s_py, NBLK)
                else:
                    pe.wait_ge(s_res, 2 + 4 * KD)
                logits(0)
                for i in range(2 * HB):
                    if i + 1 < 2 * HB:
                        logits(i + 1)
                    b = HB * h + i // 2
                    turned = []
                    for e in range(2):
                        I = HEADS * b + 2 * (i % 2) + e
                        pe.wait_ge(s_ax, I + 1)
                        for t0 in range(0, b + 1, 4):
                            if n_pt[0] >= 2:
                                pe.wait_ge(s_ae, n_pt[0] - 1)
                            for t in range(t0, min(t0 + 4, b + 1)):
                                tr = pe.transpose(ps[:, 6 if n_pt[0] % 2 == 0 else 1, P * (t - t0):P * (t - t0) + P],
                                                  logit4[:, I % 4, P * t:P * t + P], ident[:])
                            tr.then_inc(s_at, 1)
                            n_pt[0] += 1
                        turned.append(n_pt[0])
                    for e in range(2):
                        hd = 2 * (i % 2) + e
                        I = HEADS * b + hd
                        pe.wait_ge(s_ae, turned[e])
                        if hd == 0 and b >= 2:
                            pe.wait_ge(s_ay, b - 1)
                        for t in range(b + 1):
                            mm = pe.matmul(ps[:, 7 if b % 2 == 0 else 0, HD * hd:HD * hd + HD], p_t[:, I % 2, t],
                                           v[:, t, HD * hd:HD * hd + HD], start=(t == 0), stop=(t == b))
                        mm.then_inc(s_ao, 1)
                pe.wait_ge(s_ay, HB * (h + 1))
                n0 = 16 + 16 * h
                for g in range(KD):
                    pe.wait_ge(s_yn, 4 * h + g // 2 + 1)
                    if g >= 4:
                        pe.wait_ge(s_nl, n0 + g - 3)
                    for t in range(4):
                        tr = pe.matmul(ps[:, Y_BANKS[g % 4], P * t:P * t + P], y[:, HB * h + t, P * g:P * g + P],
                                       diag_y[:, g // 2, t], start=True, stop=True)
                    tr.then_inc(s_nt, 1)

                def column_loop(base, J, nk, xh, xl, tiles=None):
                    with pe.Fori(0, KD // 2, 1) as i:
                        for j in range(2):
                            gemm((base + j) % 2, nk, [(2 + j, xh, xl)], base + j + 1 + 2 * i,
                                 (s_res, J + j + 1 + 2 * i), tiles=tiles if j == 0 else None)

                nb = half_base(h)
                J = 4 * KD * h
                column_loop(nb, J, KD, lambda kk: y_hi[:, kk], lambda kk: y_lo[:, kk],
                            tiles=lambda kk: (s_nl, n0 + kk + 1))
                over_features(2 + 2 * h, 6, sum2, diag2)
                for g, nf, nu, nd, f0 in group_bases(h):
                    F = 2 + NF * h + f0
                    with pe.Fori(0, nf // 2, 1) as i:
                        for u in range(2):
                            f = F + u + 2 * i
                            for j, bank, s_ in ((0, u, s_cin), (1, 4 + u, s_act)):
                                gemm((nu + j) % 2, KD, [(bank, lambda kk: h2_hi[:, kk], lambda kk: h2_lo[:, kk])],
                                     nu + j + 1 + 2 * u + 4 * i, (s_, f - 1),
                                     tiles=(lambda kk: (s_nl, n0 + KD + kk + 1)) if (g, u, j) == (0, 0, 0) else None)
                    J += KD
                    column_loop(nd, J, nf, lambda kk: act_hi[:, kk], lambda kk: act_lo[:, kk],
                                tiles=lambda kk: (s_alo, F + kk + 1))
                over_features(3 + 2 * h, 6, sum2, diag2)


def bias_onehot():
    rel = P - 1 - np.arange(S + P)
    n = np.abs(rel)
    nf = np.maximum(n, 1).astype(np.float32)
    large = 8 + (np.log(nf / np.float32(8)) / np.float32(np.log(1024 / 8)) * np.float32(8)).astype(np.int32)
    bucket = np.where(rel > 0, 16, 0) + np.where(n < 8, n, np.minimum(large, 15))
    return (np.arange(32)[:, None] == bucket[None, :]).astype(np.float32)


def pool_counts():
    t = np.arange(1, 17, dtype=np.float32)
    rows = [1 / np.minimum(t, np.float32(w)) for w in (2, 4, 8, 16)]
    c = np.stack([np.stack([rows[0], rows[2]]), np.stack([rows[1], rows[3]])])
    return np.repeat(c, 64, axis=0).astype(np.float32)


def weight_units(w_in, w_out, w_up, w_down):
    def cols(*runs):
        part = np.concatenate([w_in[:, x0:x1] for x0, x1 in runs], axis=1)
        if part.shape[1] < P:
            part = np.concatenate([part, np.zeros((D, P - part.shape[1]), np.float32)], axis=1)
        return part

    def unit(m):
        return m.reshape(-1, P, P).transpose(1, 0, 2)

    def tiles(x0, n):
        return [cols((x0 + P * i, x0 + P * i + P)) for i in range(n)]

    zc, zdq = 1576, 1832
    units = (tiles(1280, 2) + [cols((1536, 1576))] + tiles(512, 2) + tiles(768, 2) + tiles(1024, 2)
             + tiles(zc, 2)
             + [cols((zdq + 64 * i, zdq + 64 * i + 64), (zdq + 128 + 64 * i, zdq + 192 + 64 * i)) for i in range(2)]
             + tiles(2088, 1) + tiles(2216, 1) + tiles(0, 4))
    units = [unit(u) for u in units]
    units += [unit(w_out[:, P * j:P * j + P]) for j in range(KD)]
    f0 = 0
    for nf in GROUPS:
        for f in range(f0, f0 + nf):
            units += [unit(w_up[:, P * f:P * f + P]), unit(w_up[:, DFF + P * f:DFF + P * f + P])]
        rows = w_down[P * f0:P * (f0 + nf)]
        if nf < KD:
            rows = np.concatenate([rows, np.zeros((P * (KD - nf), D), np.float32)], axis=0)
        units += [unit(rows[:, P * j:P * j + P]) for j in range(KD)]
        f0 += nf
    return np.ascontiguousarray(np.stack(units))


def kernel(x, c, w_ada, b_ada, norm1_g, norm2_g, w_in, gmlp_ws, gmlp_bs, pool_w, pool_scale,
           swa_sinks, rel_bias, mix_out_g, w_out, ffn_w_up, ffn_conv_w, ffn_conv_b, ffn_w_down,
           final_g):
    import concourse.bacc as bacc
    from concourse.bass_utils import run_bass_kernel_spmd

    def by_feature(vec):
        return np.asarray(vec).reshape(-1, P).T

    arrays = {
        "x": np.asarray(x)[0].T,
        "c": np.asarray(c)[0],
        "w_ada": np.asarray(w_ada)[0].T,
        "b_ada": by_feature(np.asarray(b_ada)[0]),
        "norm_g": np.stack([by_feature(np.asarray(norm1_g)[0]), by_feature(np.asarray(norm2_g)[0])], axis=1),
        "mix_g": by_feature(np.asarray(mix_out_g)[0]),
        "conv_w": np.stack([by_feature(t) for t in (*np.asarray(ffn_conv_w)[0], np.asarray(ffn_conv_b)[0])], axis=2),
        "gm_b": np.asarray(gmlp_bs)[0].T,
        "ident": np.eye(P, dtype=np.float32),
        "ws_t": np.asarray(gmlp_ws)[0].transpose(2, 0, 1),
        "pool_w": np.asarray(pool_w)[0].reshape(2, P, 64).transpose(1, 0, 2),
        "pool_c": pool_counts(),
        "sinks": np.asarray(swa_sinks)[0],
        "pool_s": np.asarray(pool_scale)[0],
        "rel_bias": np.asarray(rel_bias),
        "onehot": bias_onehot(),
        "fin_g": by_feature(np.asarray(final_g)),
        "w": weight_units(np.asarray(w_in)[0], np.asarray(w_out)[0], np.asarray(ffn_w_up)[0],
                          np.asarray(ffn_w_down)[0]),
    }
    arrays = {n: np.ascontiguousarray(v) for n, v in arrays.items()}
    nc = bacc.Bacc("TRN2", target_bir_lowering=False, num_devices=1)
    ins = {n: nc.dram_tensor(f"in_{n}", v.shape, F32, kind="ExternalInput").ap() for n, v in arrays.items()}
    out = nc.dram_tensor("out", (D, S), F32, kind="ExternalOutput").ap()
    build(nc, ins, out)
    res = run_bass_kernel_spmd(nc, [{f"in_{n}": v for n, v in arrays.items()}], core_ids=[0])
    return np.ascontiguousarray(res.results[0]["out"].T).reshape(1, S, D)
```

```python
from contextlib import ExitStack

import numpy as np

import concourse.bass as bass
from concourse import mybir

F32 = mybir.dt.float32
F32R = mybir.dt.float32r
ALU = mybir.AluOpType
ACT = mybir.ActivationFunctionType
AX = mybir.AxisListType.X

P = 128
D = 1024
S = 1024
KD = D // P
NBLK = S // P
HALF = 512
HB = HALF // P
W = 256
DFF = 2816
NF = DFF // P
GROUPS = (8, 8, 6)
EPS = 1e-6
NEG = -1e30
IDX_HEADS, IDX_DIM = 8, 32
HEADS, HD = 4, 64
TOPK = 256
ROUNDS = TOPK // 8
NO_KEY = -3.0e38
TAKEN = -3.4e38
TAKEN_BELOW = -3.2e38

U_QI, U_KIWI, U_Q, U_K, U_V, U_C, U_DQ, U_DK, U_DV, U_A = 0, 2, 3, 5, 7, 9, 11, 13, 14, 15
N_IN = 19
N_OUT = KD
N_FFN = 2 * NF + len(GROUPS) * KD
N_HALF = N_OUT + N_FFN
N_UNITS = N_IN + N_HALF
WI_COL = 32
TOP_BLOCKS = range(2, NBLK)
LATE_BLOCKS = range(HB, NBLK)

BASE = 16512


def score_columns():
    at, n = {}, 0
    for b in TOP_BLOCKS:
        at[b] = n
        n += P * (b + 1)
    return at, n


def dot_chunks():
    return [(b, k0, min(512, P * (b + 1) - k0), h)
            for b in TOP_BLOCKS for k0 in range(0, P * (b + 1), 512) for h in range(IDX_HEADS)]


def build(nc, a, out):
    with ExitStack() as ctx:
        def at(name, shape, offset):
            return nc.alloc_sbuf_tensor_at(name, shape, F32, offset=BASE + offset)

        def sem(name):
            return ctx.enter_context(nc.semaphore(name))

        RA, RB, RC, RD, RE, RG, RH = 0, 65536, 98304, 131072, 155648, 163840, 180736
        RM = RH + 24576
        h_hi = at("h_hi", [P, KD, S], RA)
        h_lo = at("h_lo", [P, KD, S], RA + 32768)
        q_st = [at(f"q_st_{i}", [P, 2, HEADS, P], RA + o) for i, o in enumerate((0, 4096, 12288, 28672))]
        logit = at("logit", [P, 2, HEADS, 2 * P + 1], RA + 8192)
        vn = at("vn", [P, NBLK, W], RA + 16512)
        gm = at("gm", [P, NBLK, 2 * W], RA + 24704)
        gm_sq = at("gm_sq", [P, 2, W], RA + 41088)
        y_hi = at("y_hi", [P, KD, HALF], RA)
        y_lo = at("y_lo", [P, KD, HALF], RA + 16384)
        act_hi = at("act_hi", [P, 8, HALF], RA)
        act_lo = at("act_lo", [P, 8, HALF], RA + 16384)
        x2 = at("x2", [P, KD, HALF], RA + 32768)
        bias_0 = at("bias_0", [P, HEADS, S], RA + 49152)
        conv_in = at("conv_in", [P, 2, 2 + HALF], RA + 49152)
        conv_t = at("conv_t", [P, 2, HALF], RA + 53760)
        act_f = at("act_f", [P, 2, HALF], RA + 57856)
        h2_t = at("h2_t", [P, 2, HALF], RA + 57856)
        fin_o = at("fin_o", [P, KD, HALF], RA + 49152)
        qi_hi = at("qi_hi", [P, 2, S], RB)
        qi_st = at("qi_st", [3 * IDX_DIM, 2, IDX_HEADS, P], RB)
        ki_st = at("ki_st", [3 * IDX_DIM, S], RB + 8192)
        dq = at("dq", [P, 2, S], RB + 12288)
        dk = at("dk", [P, S], RB + 20480)
        dv = at("dv", [P, NBLK, P], RB + 24576)
        swa_bias = at("swa_bias", [P, HEADS, 2 * P], RB + 28672)
        win_a = at("win_a", [P, 16 + S], RB)
        win_b = at("win_b", [P, 16 + S], RB + 4160)
        p_t = at("p_t", [P, 2, NBLK, P], RB)
        h2_hi = at("h2_hi", [P, KD, HALF], RB)
        h2_lo = at("h2_lo", [P, KD, HALF], RB + 16384)
        sq_x = at("sq_x", [P, 2, S], RB)
        sum_x = at("sum_x", [P, S], RB + 8192)
        diag_x = at("diag_x", [P, S], RB + 16384)
        h_t = at("h_t", [P, 2, HALF], RB + 12288)
        logit4 = at("logit4", [P, 4, S], RB + 8192)
        junk = at("junk", [P, 4, W], RB + 24576)
        cond = at("cond", [P, D], RB + 28672)
        x_sb = at("x_sb", [P, KD, S], RC)
        za_t = at("za_t", [P, 4, S], RC)
        kiwi = at("kiwi", [P, S], RC)
        stage = [at("stage_0", [P, S], RC + 24704), at("stage_1", [P, S], RC + 4096)]
        relu_r = at("relu_r", [P, 4, 512], RC + 8192)
        zc = [at("zc_0", [P, 16 + S], RC + 16384), at("zc_1", [P, 16 + S], RC + 20544)]
        y = at("y", [P, NBLK, D], RC)
        bias_1 = at("bias_1", [P, HEADS, S], RC)
        qk_f = at("qk_f", [P, S], RD)
        qk_hi = at("qk_hi", [P, S], RD + 4096)
        qk_lo = at("qk_lo", [P, S], RD + 8192)
        k_st = at("k_st", [P, HEADS, S], RD)
        v = at("v", [P, NBLK, W], RD + 16384)
        w_ada0 = at("w_ada0", [P, 2, 4, D], RD)
        qi_lo = at("qi_lo", [P, 2, S], RD + 16384)
        w_ada1 = at("w_ada1", [P, 2, D], RE)
        pool_w = at("pool_w", [P, 2, P], RE)
        bias_m = at("bias_m", [P, 2, S], RE)
        diag_y = at("diag_y", [P, 4, HB, P], RE)
        sq2 = at("sq2", [P, 2, HALF], RB + 24576)
        sum2 = at("sum2", [P, HALF], RB + 28672)
        diag2 = at("diag2", [P, HALF], RB + 30720)
        onehot = at("onehot", [32, S + P], RG)
        fbias = at("fbias", [HEADS * 2, S + P], RG + 4608)
        SC, n_sc = score_columns()
        score = at("score", [P, n_sc], RG)
        w_raw = at("w_raw", [P, 2, KD, P], RH)
        w_hi = at("w_hi", [P, 2, KD, P], RH + 8192)
        w_lo = at("w_lo", [P, 2, KD, P], RH + 16384)

        small_at = [RM]

        def small(name, shape):
            t = at(name, shape, small_at[0])
            small_at[0] += -(-4 * int(np.prod(shape[1:])) // 32) * 32
            assert BASE + small_at[0] <= 229344, small_at[0]
            return t

        ident = small("ident", [P, P])
        ws_t = small("ws_t", [P, 4, P])
        pool_s = small("pool_s", [P, W])
        pool_c = small("pool_c", [P, 2, 16])
        b_ada = small("b_ada", [P, 48])
        norm_g = small("norm_g", [P, 2, KD])
        mix_g = small("mix_g", [P, KD])
        fin_g = small("fin_g", [P, KD])
        ones = small("ones", [P, P])
        conv_w = small("conv_w", [P, NF, 4])
        gm_b = small("gm_b", [P, 4])
        sinks = small("sinks", [P, HEADS])
        rel = small("rel", [32, 8])
        ada = small("ada", [P, 48])
        root_s = small("root_s", [P, NBLK])
        root_r = small("root_r", [P, NBLK])
        mod = small("mod", [P, 48])
        scale_g = small("scale_g", [P, 2, KD])
        halo = small("halo", [P, NF, 2])
        eps = small("eps", [P, 1])
        st = small("st", [P, 32])
        st2 = small("st2", [P, 32])
        st3 = small("st3", [P, 32])
        wis = small("wis", [P, len(TOP_BLOCKS), IDX_HEADS])
        tick = small("tick", [P, 1])
        top8 = small("top8", [P, len(TOP_BLOCKS), 8])
        sm_max = small("sm_max", [P, 3, HEADS])
        sm_neg = small("sm_neg", [P, 3, HEADS])
        sm_sum = small("sm_sum", [P, 3, HEADS])
        sm_rec = small("sm_rec", [P, 3, HEADS])

        ps = ctx.enter_context(nc.psum_tensor("ps", [P, 8, 512], F32))

        def r(ap):
            return ap.bitcast(F32R)

        f_dram = nc.dram_tensor("f_dram", (8, S + P), F32, kind="Internal")
        bias_rows = bass.AP(tensor=f_dram, offset=0, ap=[[1, P], [S + P, HEADS], [1, S]])

        qi_dram = nc.dram_tensor("qi_dram", (2, IDX_HEADS, IDX_DIM, S), F32, kind="Internal")

        qk_dram = nc.dram_tensor("qk_dram", (2, 2 * HEADS, HD, S), F32, kind="Internal")

        def backwards(ap):
            *dims, (step, n) = ap.ap
            return bass.AP(tensor=ap.tensor, offset=ap.offset + step * (n - 1), ap=[*dims, [-step, n]])

        params_loaded = sem("params_loaded")
        rel_loaded = sem("rel_loaded")
        x_loaded = [sem(f"x_loaded_{i}") for i in range(4)]
        ada_w_first = [sem(f"ada_w_first_{i}") for i in range(4)]
        ada_w_rest = [sem(f"ada_w_rest_{i}") for i in range(2)]
        consts_set = sem("consts_set")
        c_loaded = sem("c_loaded")
        cond_ready = sem("cond_ready")
        ada_summed = sem("ada_summed")
        ada_weighted = sem("ada_weighted")
        ada_pool_summed = sem("ada_pool_summed")
        mod_ready = sem("mod_ready")
        bias_row_made = sem("bias_row_made")
        bias_row_out = sem("bias_row_out")
        bias_row_stored = sem("bias_row_stored")
        table_loaded = sem("table_loaded")
        swa_table_loaded = sem("swa_table_loaded")
        squares_ready = sem("squares_ready")
        squares_added = sem("squares_added")
        mean_square = sem("mean_square")
        root_ready = sem("root_ready")
        diag_ready = sem("diag_ready")
        rms_spread = sem("rms_spread")
        y_turned = sem("y_turned")
        norm_scaled = sem("norm_scaled")
        norm_hi = sem("norm_hi")
        norm_lo = sem("norm_lo")
        w_loaded = [sem(f"w_loaded_{i}") for i in range(2)]
        w_hi_ready = sem("w_hi_ready")
        w_lo_ready = sem("w_lo_ready")
        unit_done = sem("unit_done")
        unit_out = sem("unit_out")
        wi_turned = sem("wi_turned")
        wi_scaled = sem("wi_scaled")
        qi_lo_ready = sem("qi_lo_ready")
        qi_stored = sem("qi_stored")
        qi_loaded = [sem(f"qi_loaded_{i}") for i in range(2)]
        ki_lo_ready = sem("ki_lo_ready")
        qk_hi_ready = sem("qk_hi_ready")
        qk_lo_ready = sem("qk_lo_ready")
        qk_stored = sem("qk_stored")
        k_loaded = sem("k_loaded")
        q_loaded = [sem(f"q_loaded_{i}") for i in range(2)]
        dots_done = sem("dots_done")
        relu_ready = sem("relu_ready")
        scores_added = sem("scores_added")
        top8_found = sem("top8_found")
        top8_marked = sem("top8_marked")
        v_turned = sem("v_turned")
        v_out = sem("v_out")
        gm_turned = sem("gm_turned")
        gm_out = sem("gm_out")
        ln_mean_ready = sem("ln_mean_ready")
        ln_centred = sem("ln_centred")
        ln_var_ready = sem("ln_var_ready")
        ln_root_ready = sem("ln_root_ready")
        vn_ready = sem("vn_ready")
        gate_done = sem("gate_done")
        gmlp_out = sem("gmlp_out")
        pool_padded = sem("pool_padded")
        pool_ready = sem("pool_ready")
        pool_w_loaded = sem("pool_w_loaded")
        pool_done = sem("pool_done")
        pool_out_ready = sem("pool_out_ready")
        swa_logits_ready = sem("swa_logits_ready")
        swa_max = sem("swa_max")
        swa_exp = sem("swa_exp")
        swa_turned = sem("swa_turned")
        swa_probs = sem("swa_probs")
        swa_product = sem("swa_product")
        swa_out_ready = sem("swa_out_ready")
        sink_ready = sem("sink_ready")
        dsa_logits_ready = sem("dsa_logits_ready")
        dsa_biased = sem("dsa_biased")
        dsa_max = sem("dsa_max")
        dsa_exp = sem("dsa_exp")
        dsa_turned = sem("dsa_turned")
        dsa_probs = sem("dsa_probs")
        dsa_product = sem("dsa_product")
        dsa_out_ready = sem("dsa_out_ready")
        bias_masked = sem("bias_masked")
        masks_ready = sem("masks_ready")
        bias_and_mask = sem("bias_and_mask")
        y_squares_ready = sem("y_squares_ready")
        y_root_ready = sem("y_root_ready")
        y_diag_ready = sem("y_diag_ready")
        x2_loaded = sem("x2_loaded")
        residual_added = sem("residual_added")
        halo_in = sem("halo_in")
        conv_in_ready = sem("conv_in_ready")
        conv_done = sem("conv_done")
        conv_tap_added = sem("conv_tap_added")
        gelu_ready = sem("gelu_ready")
        act_ready = sem("act_ready")
        act_hi_ready = sem("act_hi_ready")
        act_lo_ready = sem("act_lo_ready")
        final_ready = sem("final_ready")
        out_stored = sem("out_stored")
        dve_chain = sem("dve_chain")
        pool_chain = sem("pool_chain")

        DOTS = dot_chunks()
        chain = {}

        def link(eng, s, ins):
            chain[s.name] = chain.get(s.name, 0) + 1
            ins.then_inc(s, 1)
            eng.wait_ge(s, chain[s.name])

        def half_base(h):
            return N_IN + N_HALF * h

        def group_bases(h):
            n, f, res = half_base(h) + N_OUT, 0, []
            for g, nf in enumerate(GROUPS):
                res.append((g, nf, n, n + 2 * nf, f))
                n += 2 * nf + KD
                f += nf
            return res

        N_SEQ = N_IN + 2 * N_HALF

        def ada_tiles(chunk):
            return [2 * chunk, 2 * chunk + 1, KD + 2 * chunk, KD + 2 * chunk + 1]

        DOT_UNIT = 3
        DOT_STEPS = len(DOTS) // IDX_HEADS
        FIN_BANK = 0
        U_POOL = 13
        POOL_BANKS = (0, 1, 6, 7)
        GATE_BANKS = (6, 1, 7, 0)
        Y_BANKS = (0, 1, 6, 7)
        ADA_STEPS = 16
        EARLY = [b for b in TOP_BLOCKS if b not in LATE_BLOCKS]
        early_steps = {step: 3 if step < 3 else 2 for step in range(1, ADA_STEPS)}
        assert sum(early_steps.values()) == ROUNDS

        def turned_through(I):
            return sum(-(-(J // HEADS + 1) // 4) for J in range(I + 1))

        def q_place(b):
            return 2 * (b // HB) + b % 2

        def load_queries(queue, b):
            for part in range(2):
                for j in range(2):
                    queue.dma_start(q_st[q_place(b)][HD * j:HD * j + HD, part],
                                  qk_dram.ap()[part, 0:HEADS].rearrange("h d s -> d h s")[:, :, P * b:P * b + P]
                                  ).then_inc(q_loaded[b % 2], 16)

        def raw_ready(n):
            return w_loaded[n % 2], 16 * (n // 2 + 1)

        block = ctx.enter_context(nc.Block())

        @block.sync
        def _(sp):
            sp.dma_start(cond[:], a["c"].partition_broadcast(P)).then_inc(c_loaded, 16)
            sp.dma_start(rel[:], a["rel_bias"]).then_inc(rel_loaded, 16)
            sp.dma_start(onehot[:], a["onehot"]).then_inc(rel_loaded, 16)
            for name, dst in (("b_ada", b_ada), ("norm_g", norm_g), ("mix_g", mix_g), ("fin_g", fin_g),
                              ("conv_w", conv_w), ("gm_b", gm_b), ("ident", ident), ("ws_t", ws_t),
                              ("pool_c", pool_c)):
                sp.dma_start(dst[:], a[name]).then_inc(params_loaded, 16)
            sp.dma_start(sinks[:], a["sinks"].partition_broadcast(P)).then_inc(params_loaded, 16)
            sp.dma_start(pool_s[:], a["pool_s"].partition_broadcast(P)).then_inc(params_loaded, 16)
            xs = a["x"].rearrange("(k p) s -> p k s", p=P)
            for i in range(4):
                sp.dma_start(x_sb[:, 2 * i:2 * i + 2], xs[:, 2 * i:2 * i + 2]).then_inc(x_loaded[i], 16)
            w = a["w"].rearrange("u p k c -> u p (k c)")

            def load(n):
                if n >= 2:
                    sp.wait_ge(w_lo_ready, n - 1)
                sp.dma_start(w_raw[:, n % 2], w[n]).then_inc(w_loaded[n % 2], 16)

            wa = a["w_ada"].rearrange("(c p) d -> p c d", p=P)
            for i in range(4):
                if i >= 2:
                    sp.wait_ge(ada_summed, 2 * (i - 1))
                    sp.wait_ge(ada_pool_summed, 2 * (i - 1))
                if i < 2:
                    sp.wait_ge(x_loaded[1 + 2 * i], 16)
                for half, c0 in enumerate((2 * i, KD + 2 * i)):
                    sp.dma_start(w_ada0[:, i % 2, 2 * half:2 * half + 2], wa[:, c0:c0 + 2]).then_inc(ada_w_first[i], 16)
                if i < 2:
                    load(i)
            for n in range(N_IN):
                if n + 2 < N_IN:
                    load(n + 2)
                step = n - DOT_UNIT
                if 0 <= step < ADA_STEPS:
                    for c in (16 + 2 * step, 17 + 2 * step):
                        sp.wait_ge(ada_summed, max(8, c - 9))
                        sp.wait_ge(ada_pool_summed, 8)
                        sp.dma_start(w_ada1[:, c % 2], wa[:, c]).then_inc(ada_w_rest[c % 2], 16)
            load(N_IN)
            load(N_IN + 1)
            sp.wait_ge(ada_summed, 40)
            sp.wait_ge(ada_pool_summed, 8)
            sp.wait_ge(bias_row_stored, 16)
            sp.dma_start(swa_bias[:], bass.AP(tensor=f_dram, offset=HEADS * (S + P), ap=[[1, P], [S + P, HEADS], [1, 2 * P]])).then_inc(swa_table_loaded, 16)
            sp.dma_start(pool_w[:], a["pool_w"]).then_inc(pool_w_loaded, 16)
            sp.wait_ge(unit_done, N_IN)
            for b in range(2):
                load_queries(sp, b)
            for h in range(2):
                nb = half_base(h)
                with sp.Fori(1 - h, N_HALF // 2, 1) as i:
                    for j in range(2):
                        sp.wait_ge(w_lo_ready, nb + j - 1 + 2 * i)
                        sp.dma_start(w_raw[:, (nb + j) % 2], w[N_IN + j + 2 * i]
                                     ).then_inc(w_loaded[(nb + j) % 2], 16)
            for n in range(N_SEQ, N_SEQ + 2):
                sp.wait_ge(w_lo_ready, n - 1)
                sp.dma_start(w_raw[:, n % 2], w[0]).then_inc(w_loaded[n % 2], 16)

        @block.gpsimd
        def _(pool):
            def w_lo_unit(slot, ready, i=None):
                pool.wait_ge(w_hi_ready, ready)
                pool.tensor_tensor(r(w_lo[:, slot]), w_raw[:, slot], w_hi[:, slot],
                                   ALU.subtract).then_inc(w_lo_ready, 1)

            def lo(n):
                w_lo_unit(n % 2, n + 1)

            def plink(ins):
                link(pool, pool_chain, ins)

            def doubled(src, win, dst, row):
                plink(pool.tensor_tensor(dst[row:P, 2 * win - 1:], src[row:P, 2 * win - 1:],
                                         src[row:P, win - 1:16 + S - win], ALU.add))

            def pool_out(tile, row, sums, win):
                rows = slice(row, row + 64)
                plink(pool.tensor_tensor(sums[rows, 16:32], sums[rows, 16:32], pool_c[rows, tile], ALU.mult))
                plink(pool.tensor_scalar(sums[rows, 32:], sums[rows, 32:], 1.0 / win, None, ALU.mult))
                plink(pool.tensor_tensor(zc[tile][rows, 16:], sums[rows, 16:], zc[tile][rows, 16:], ALU.subtract))

            pool.memset(eps[:], EPS).then_inc(consts_set, 1)
            pool.memset(halo[:], 0.0).then_inc(consts_set, 1)
            pool.memset(ones[:], 1.0).then_inc(consts_set, 1)
            pool.wait_ge(params_loaded, 16 * 11)
            pool.wait_ge(consts_set, 3)
            pool.memset(ws_t[64:128, :, 0:64], 0.0).then_inc(consts_set, 1)
            pool.wait_ge(consts_set, 4)

            def ada_products(chunk):
                pool.wait_ge(cond_ready, 1)
                pool.wait_ge(ada_w_first[chunk], 32)
                for j in (2, 3):
                    t = w_ada0[:, chunk % 2, j]
                    pool.tensor_tensor(t, t, cond[:], ALU.mult).then_inc(ada_weighted, 1)

            ada_products(0)
            lo(0)
            for chunk in range(1, 4):
                ada_products(chunk)
            for n in range(N_IN):
                if n == U_C:
                    pool.wait_ge(norm_lo, 16)
                    pool.memset(zc[0][:, 0:16], 0.0).then_inc(pool_padded, 1)
                    pool.memset(zc[1][:, 0:16], 0.0).then_inc(pool_padded, 1)
                lo(n + 1)
                if U_Q <= n < U_V:
                    pool.wait_ge(qk_hi_ready, n - U_Q + 1)
                    if n > U_Q:
                        pool.wait_ge(qk_stored, 32 * (n - U_Q))
                    pool.tensor_tensor(qk_lo[:], qk_f[:], qk_hi[:], ALU.subtract).then_inc(qk_lo_ready, 1)
                if n >= U_POOL:
                    pool.wait_ge(w_lo_ready, n + 2)
                if n == U_POOL:
                    pool.wait_ge(unit_out, U_C + 2)
                    pool.wait_ge(dots_done, len(DOTS))
                    pool.wait_ge(pool_padded, 2)
                    doubled(zc[0], 1, win_a, 0)
                    doubled(win_a, 2, win_b, 64)
                elif n == U_POOL + 1:
                    pool_out(0, 0, win_a, 2)
                elif n == U_POOL + 2:
                    pool_out(0, 64, win_b, 4)
                elif n == U_POOL + 3:
                    doubled(zc[1], 1, win_a, 0)
                    doubled(win_a, 2, win_b, 0)
                elif n == U_POOL + 4:
                    doubled(win_b, 4, win_a, 0)
                    doubled(win_a, 8, win_b, 64)
                elif n == U_POOL + 5:
                    pool_out(1, 0, win_a, 8)
                    pool_out(1, 64, win_b, 16)
            pool.sem_inc(pool_ready, 1)
            def sink_column(b):
                pool.tensor_copy(logit[:, b % 2, :, 2 * P:2 * P + 1], sinks[:].unsqueeze(2)).then_inc(sink_ready, 1)

            pool.wait_ge(unit_done, N_IN)
            sink_column(0)
            sink_column(1)
            lo(N_IN + 1)

            def tables_ready(h):
                pool.wait_ge(bias_masked, h + 1)
                pool.wait_ge(masks_ready, h + 1)

            def masked_bias(I):
                b, hd = I // HEADS, I % HEADS
                if I >= 10:
                    pool.wait_ge(dsa_biased, I - 1)
                pool.tensor_tensor(bias_m[:, I % 2, 0:P * (b + 1)],
                                   backwards((bias_1 if b >= HB else bias_0)[:, hd, 0:P * (b + 1)]),
                                   score[:, SC[b]:SC[b] + P * (b + 1)], ALU.add).then_inc(bias_and_mask, 1)

            for b in range(NBLK):
                pool.wait_ge(ln_mean_ready, b + 1)
                if b >= 2:
                    pool.wait_ge(ln_var_ready, b - 1)
                plink(pool.tensor_tensor(vn[:, b].rearrange("p (g c) -> p g c", c=64),
                                         gm[:, b, W:].rearrange("p (g c) -> p g c", c=64),
                                         st3[:, 4 * b:4 * b + 4].unsqueeze(2).to_broadcast([P, 4, 64]), ALU.subtract))
                pool.tensor_tensor(gm_sq[:, b % 2], vn[:, b], vn[:, b], ALU.mult).then_inc(ln_centred, 1)
                if b + 2 < NBLK:
                    pool.wait_ge(swa_turned, 2 * b + 2)
                    sink_column(b + 2)
            for h in range(2):
                nb = half_base(h)

                def pairs(base, count):
                    with pool.Fori(0, count, 1) as i:
                        for j in (2, 3):
                            w_lo_unit((base + j) % 2, base + j + 1 + 2 * i)

                if h == 0:
                    tables_ready(0)
                for I in range(HEADS * max(2, HB * h) + 2 * h, HEADS * HB * (h + 1)):
                    masked_bias(I)
                pairs(nb, N_OUT // 2)
                for g, nf, nu, nd, f0 in group_bases(h):
                    F = 2 + NF * h + f0
                    with pool.Fori(0, nf // 2, 1) as i:
                        for u in range(2):
                            for j in (2, 3):
                                w_lo_unit((nu + j) % 2, nu + j + 1 + 2 * u + 4 * i)
                            pool.wait_ge(act_hi_ready, F + 1 + u + 2 * i)
                            pool.tensor_tensor(r(act_lo[:, u + 2 * i]), act_f[:, u], act_hi[:, u + 2 * i],
                                               ALU.subtract).then_inc(act_lo_ready, 1)
                    if h == 0 and g == 2:
                        tables_ready(1)
                        for I in range(HEADS * HB, HEADS * HB + 2):
                            masked_bias(I)
                    pairs(nd, KD // 2)

        @block.scalar
        def _(act):

            def split_hi(slot, ready_sem, ready, used):
                act.wait_ge(ready_sem, ready)
                if used is not None:
                    act.wait_ge(unit_done, used)
                act.activation(r(w_hi[:, slot]), w_raw[:, slot], ACT.Copy).then_inc(w_hi_ready, 1)

            def hi(n):
                rs, rv = raw_ready(n)
                split_hi(n % 2, rs, rv, n - 1 if n >= 2 else None)

            def hi_in(n, i, step=2):
                rs, rv = raw_ready(n)
                split_hi(n % 2, rs, rv + 8 * step * i, n - 1 + step * i)

            act.wait_ge(c_loaded, 16)
            act.activation(cond[:], cond[:], ACT.Silu).then_inc(cond_ready, 1)
            act.wait_ge(bias_row_made, 1)
            act.activation(fbias[:].rearrange("p (a b) -> p a b", a=3), ps[0:8, 4:7, 0:384],
                           ACT.Copy).then_inc(bias_row_out, 1)
            act.wait_ge(bias_row_out, 1)
            act.dma_start(f_dram.ap(), fbias[:]).then_inc(bias_row_stored, 16)
            act.wait_ge(bias_row_stored, 16)

            for n in range(KD):
                act.wait_ge(x_loaded[n // 2], 16)
                if n >= 2:
                    act.wait_ge(squares_added, n - 1)
                act.activation(sq_x[:, n % 2], x_sb[:, n], ACT.Square, scale=D ** -0.5).then_inc(squares_ready, 1)

            def root(m, bank, blocks=HB):
                act.wait_ge(mean_square, m + 1)
                act.activation(root_s[:, 0:blocks], ps[:, bank, 0:blocks], ACT.Sqrt, bias=eps[:]).then_inc(root_ready, 1)

            root(0, 4, NBLK)

            def split_tiles(t0, n0, count, tmp, hi_t, bias):
                for g in range(count):
                    act.wait_ge(norm_scaled, t0 + g + 1)
                    act.activation(r(hi_t(g)), tmp[:, g % 2], ACT.Identity, bias=bias(g)).then_inc(norm_hi, 1)


            for i in range(4):
                for j in (2, 3):
                    act.wait_ge(ada_weighted, 2 * i + j - 1)
                    c = ada_tiles(i)[j]
                    t = w_ada0[:, i % 2, j]
                    act.activation(t, t, ACT.Copy, accum_out=ada[:, c:c + 1]).then_inc(ada_pool_summed, 1)
                if i == 0:
                    hi(0)
                split_tiles(4 * i, 4 * i, 4, h_t, lambda n: h_hi[:, 2 * i + n // 2, HALF * (n % 2):HALF * (n % 2) + HALF],
                            lambda n: mod[:, 2 * i + n // 2:2 * i + n // 2 + 1])


            def relus(quad):
                for i in range(4 * quad, 4 * quad + 4):
                    n = DOTS[i][2]
                    act.wait_ge(dots_done, i + 1)
                    if i >= 4:
                        act.wait_ge(scores_added, i - 3)
                    act.activation(relu_r[:, i % 4, 0:n], ps[:, 4 + i % 4, 0:n], ACT.Relu,
                                   scale=IDX_DIM ** -0.5).then_inc(relu_ready, 1)
                b = DOTS[i][0]
                if b + 2 < NBLK and DOTS[i + 1][0] != b:
                    stack_queries(b + 2)

            def v_evac(g):
                act.wait_ge(v_turned, g + 1)
                col, blk = g // 2, HB * (g % 2)
                dst = v[:, blk:blk + HB, P * col:P * col + P] if col < 2 else dv[:, blk:blk + HB]
                act.activation(dst, ps[:, 6].rearrange("p (b c) -> p b c", b=HB), ACT.Copy).then_inc(v_out, 1)

            def stack_queries(b):
                for j, part in enumerate((0, 1, 0)):
                    act.dma_start(qi_st[IDX_DIM * j:IDX_DIM * j + IDX_DIM, b % 2],
                                  qi_dram.ap()[part].rearrange("h d s -> d h s")[:, :, P * b:P * b + P]
                                  ).then_inc(qi_loaded[b % 2], 16)

            def evac(n):
                act.wait_ge(unit_done, n + 1)
                src = ps[:, 2 * (n % 2):2 * (n % 2) + 2].rearrange("p b c -> p (b c)")
                f = ACT.Copy
                if n == U_KIWI:
                    for j in range(2):
                        act.activation(r(ki_st[IDX_DIM * j:IDX_DIM * j + IDX_DIM]), src[0:IDX_DIM], ACT.Copy)
                    dst = kiwi[:]
                elif n < U_KIWI:
                    dst = r(qi_hi[:, n])
                elif n < U_V:
                    if n > U_Q:
                        act.wait_ge(qk_lo_ready, n - U_Q)
                    dst = qk_f[:]
                elif n < U_C:
                    dst = stage[n - U_V][:]
                elif n < U_DQ:
                    dst = zc[n - U_C][:, 16:]
                elif n < U_DK:
                    dst = dq[:, n - U_DQ]
                elif n == U_DK:
                    dst = dk[:]
                elif n == U_DV:
                    act.wait_ge(v_turned, 4)
                    dst = stage[0][:]
                else:
                    if n == U_A:
                        act.wait_ge(scores_added, len(DOTS))
                    dst, f = za_t[:, n - U_A], ACT.Gelu_apprx_tanh
                act.activation(dst, src, f).then_inc(unit_out, 1)
                if U_Q <= n < U_V:
                    act.wait_ge(unit_out, n + 1)
                    if n > U_Q:
                        act.wait_ge(qk_stored, 32 * (n - U_Q))
                    act.activation(r(qk_hi[:]), qk_f[:], ACT.Copy).then_inc(qk_hi_ready, 1)


            for n in range(N_IN):
                hi(n + 1)
                if n in (1, 2):
                    act.wait_ge(unit_out, n)
                    act.wait_ge(qi_lo_ready, n)
                    for part, t in enumerate((qi_hi, qi_lo)):
                        act.dma_start(qi_dram.ap()[part, 4 * (n - 1):4 * n].rearrange("h d s -> (h d) s"),
                                      t[:, n - 1]).then_inc(qi_stored, 16)
                step = n - DOT_UNIT
                if 0 <= step < DOT_STEPS:
                    relus(2 * step)
                if U_Q < n <= U_V:
                    act.wait_ge(qk_lo_ready, n - U_Q)
                    for part, t in enumerate((qk_hi, qk_lo)):
                        act.dma_start(qk_dram.ap()[part, 2 * (n - 1 - U_Q):2 * (n - U_Q)].rearrange("h d s -> (h d) s"),
                                      t[:]).then_inc(qk_stored, 16)
                if n == U_V + 1:
                    act.wait_ge(qk_stored, 128)
                    for part in range(2):
                        act.dma_start(k_st[HD * part:HD * part + HD],
                                      qk_dram.ap()[part, HEADS:].rearrange("h d s -> d h s")).then_inc(k_loaded, 16)
                evac(n)
                if n == U_KIWI:
                    act.wait_ge(qi_stored, 64)
                    for b in TOP_BLOCKS[:2]:
                        stack_queries(b)
                if 0 <= step < DOT_STEPS:
                    relus(2 * step + 1)
                if n == 13:
                    for g in range(4):
                        v_evac(g)
                if n == 16:
                    for g in range(4, 6):
                        v_evac(g)
            for b in range(NBLK):
                act.wait_ge(gm_turned, b + 1)
                act.activation(gm[:, b], ps[:, 4 + b % 2], ACT.Copy).then_inc(gm_out, 1)
            hi(N_IN + 1)
            act.dma_start(bias_0[:], bias_rows).then_inc(table_loaded, 16)

            for b in range(NBLK):
                c0 = P if b == 0 else 0
                act.wait_ge(swa_max, b + 1)
                lg = logit[:, b % 2]
                for h in range(HEADS):
                    act.activation(lg[:, h, c0:], lg[:, h, c0:], ACT.Exp, bias=sm_neg[:, b % 3, h:h + 1],
                                   accum_out=sm_sum[:, b % 3, h:h + 1]).then_inc(swa_exp, 1)
                for j in range(2):
                    act.wait_ge(swa_turned, 2 * b + j + 1)
                    if b >= 2 and j == 0:
                        act.wait_ge(swa_product, b - 1)
                    src = ps[:, 6 if j == 0 else 1].rearrange("p (h c) -> p h c", h=4)
                    if c0:
                        act.activation(p_t[:, b % 2, 4 * j + 1:4 * j + 4:2], src[:, 1::2], ACT.Copy).then_inc(swa_probs, 1)
                    else:
                        act.activation(p_t[:, b % 2, 4 * j:4 * j + 4], src, ACT.Copy).then_inc(swa_probs, 1)

            act.wait_ge(ln_var_ready, NBLK)
            act.activation(st2[:, 0:32], st[:, 0:32], ACT.Sqrt, bias=eps[:], scale=1.0 / 64).then_inc(ln_root_ready, 1)

            n_pt = [0]
            for h in range(2):
                nb = half_base(h)
                def exps(i):
                    b = HB * h + i // 2
                    for e in range(2):
                        hd = 2 * (i % 2) + e
                        I = HEADS * b + hd
                        lg = logit4[:, I % 4, 0:P * (b + 1)]
                        act.wait_ge(dsa_max, I + 1)
                        act.activation(lg, lg, ACT.Exp, bias=sm_neg[:, b % 2, hd:hd + 1],
                                       accum_out=sm_sum[:, b % 2, hd:hd + 1]).then_inc(dsa_exp, 1)

                def probs_back(i):
                    b = HB * h + i // 2
                    for e in range(2):
                        I = HEADS * b + 2 * (i % 2) + e
                        for t in range(0, b + 1, 4):
                            m = min(4, b + 1 - t)
                            act.wait_ge(dsa_turned, n_pt[0] + 1)
                            if t == 0 and I >= 2:
                                act.wait_ge(dsa_product, I - 1)
                            act.activation(p_t[:, I % 2, t:t + m],
                                           ps[:, 6 if n_pt[0] % 2 == 0 else 1].rearrange("p (h c) -> p h c", h=4)[:, 0:m],
                                           ACT.Copy).then_inc(dsa_probs, 1)
                            n_pt[0] += 1

                def y_squares(b):
                    act.wait_ge(dsa_out_ready, b + 1)
                    if b == 0:
                        act.wait_ge(gmlp_out, 4)
                        act.wait_ge(pool_out_ready, 1)
                        act.wait_ge(swa_out_ready, NBLK)
                    else:
                        act.wait_ge(y_squares_ready, 4 * b)
                    for m in range(4):
                        at_ = 4 * (b % HB) + m
                        act.activation(junk[:, m], y[:, b, W * m:W * m + W], ACT.Square,
                                       accum_out=st[:, at_:at_ + 1]).then_inc(y_squares_ready, 1)

                def results(hh):
                    for g in range(KD):
                        act.wait_ge(final_ready, KD * hh + g + 1)
                        act.dma_start(out.rearrange("(k p) s -> p k s", p=P)[:, g, HALF * hh:HALF * hh + HALF],
                                      fin_o[:, g]).then_inc(out_stored, 16)

                if h == 1:
                    root(2, FIN_BANK)
                exps(0)
                for i in range(2 * HB):
                    probs_back(i)
                    if i in (0, 2):
                        b = HB * h + i // 2
                        act.wait_ge(dsa_logits_ready, HEADS * (b + 1))
                        load_queries(act, b + 2)
                    if h == 1 and i == 1:
                        results(0)
                    if i % 2 == 0 and i > 0:
                        y_squares(HB * h + i // 2 - 1)
                    if i + 1 < 2 * HB:
                        exps(i + 1)
                y_squares(HB * h + HB - 1)
                act.wait_ge(y_squares_ready, 16 * (h + 1))
                act.activation(st2[:, 0:16], st[:, 0:16], ACT.Sqrt, bias=eps[:], scale=1.0 / W).then_inc(y_root_ready, 1)
                if h == 1:
                    act.wait_ge(final_ready, KD)
                act.dma_start(x2[:], a["x"].rearrange("(k p) s -> p k s", p=P)[:, :, HALF * h:HALF * h + HALF]
                              ).then_inc(x2_loaded, 16)
                n0 = 16 + 16 * h
                for g in range(KD):
                    act.wait_ge(y_turned, KD * h + g + 1)
                    act.activation(r(y_hi[:, g]), ps[:, Y_BANKS[g % 4]], ACT.Copy, scale=mix_g[:, g:g + 1]).then_inc(norm_hi, 1)
                if h == 0:
                    act.dma_start(bias_1[:], bias_rows).then_inc(table_loaded, 16)

                def column_loop(base, J, q0):
                    with act.Fori(0, KD // 2, 1) as i:
                        for j in range(2):
                            hi_in(base + 2 + j, i)
                            if q0:
                                act.wait_ge(squares_added, q0 + j - 1 + 2 * i)
                                act.wait_ge(residual_added, J + j + 3 + 2 * i)
                                act.activation(sq2[:, j], x2[:, j + 2 * i], ACT.Square,
                                               scale=D ** -0.5).then_inc(squares_ready, 1)

                J = 4 * KD * h
                column_loop(nb, J, n0 - KD)
                root(1 + 2 * h, 6)
                split_tiles(16 + KD * h, n0 + KD, KD, h2_t, lambda g: h2_hi[:, g],
                            lambda g: mod[:, 3 * KD + g:3 * KD + g + 1])
                if h == 1:
                    act.wait_ge(out_stored, 16 * KD)
                for g, nf, nu, nd, f0 in group_bases(h):
                    F = 2 + NF * h + f0
                    with act.Fori(0, nf // 2, 1) as i:
                        for u in range(2):
                            f = F + u + 2 * i
                            hi_in(nu + 2 + 2 * u, i, 4)
                            act.wait_ge(conv_done, f - 1)
                            act.activation(conv_in[:, u, 0:2], halo[:, f0 + u + 2 * i], ACT.Copy).then_inc(halo_in, 1)
                            act.activation(conv_t[:, u], ps[:, u], ACT.Identity, bias=conv_w[:, f0 + u + 2 * i, 3:4],
                                           scale=conv_w[:, f0 + u + 2 * i, 2:3])
                            act.wait_ge(halo_in, f + 1)
                            act.activation(conv_in[:, u, 2:], ps[:, u], ACT.Copy)
                            act.activation(halo[:, f0 + u + 2 * i], ps[:, u, HALF - 2:], ACT.Copy).then_inc(conv_in_ready, 1)
                            act.wait_ge(conv_done, f + 1)
                            act.activation(conv_t[:, u], conv_t[:, u], ACT.Gelu_apprx_tanh).then_inc(gelu_ready, 1)
                            hi_in(nu + 3 + 2 * u, i, 4)
                            act.wait_ge(act_ready, f + 1)
                            act.activation(r(act_hi[:, u + 2 * i]), act_f[:, u], ACT.Copy).then_inc(act_hi_ready, 1)
                    if h == 0 and g == 2:
                        for b in range(HB, HB + 2):
                            load_queries(act, b)
                    column_loop(nd, J + 8 + 8 * g, n0 if g == 2 else 0)
            root(4, FIN_BANK)
            results(1)
            act.wait_ge(out_stored, 16 * 2 * KD)

        @block.vector
        def _(dve):
            def vlink(ins):
                link(dve, dve_chain, ins)

            dve.wait_ge(params_loaded, 16 * 11)

            def add_squares(n0, count, ring, acc):
                for n in range(n0, n0 + count):
                    dve.wait_ge(squares_ready, n + 1)
                    dve.tensor_tensor(acc, acc, ring[:, n % 2], ALU.add).then_inc(squares_added, 1)
                    dve.wait_ge(squares_added, n + 1)

            def root(m, diag, blocks=HB):
                dve.wait_ge(root_ready, m + 1)
                vlink(dve.reciprocal(root_r[:, 0:blocks], root_s[:, 0:blocks]))
                dve.tensor_tensor(diag.rearrange("p (t c) -> p t c", c=P),
                                  ident[:].unsqueeze(1).to_broadcast([P, blocks, P]),
                                  root_r[:, 0:blocks].unsqueeze(2).to_broadcast([P, blocks, P]),
                                  ALU.mult).then_inc(diag_ready, 1)
                dve.wait_ge(rms_spread, m + 1)

            def ada_tile(c, src, loaded, value):
                dve.wait_ge(loaded, value)
                dve.wait_ge(cond_ready, 1)
                dve.scalar_tensor_tensor(out=src, in0=src, scalar=1.0, in1=cond[:], op0=ALU.mult, op1=ALU.mult,
                                         accum_out=ada[:, c:c + 1]).then_inc(ada_summed, 1)

            vlink(dve.memset(sum_x[:], 0.0))
            add_squares(0, KD, sq_x, sum_x[:])
            root(0, diag_x[:], NBLK)

            def split_tiles(t0, n0, count, make, tmp, lo_t, shift):
                if n0:
                    dve.wait_ge(norm_lo, n0)
                make(0).then_inc(norm_scaled, 1)
                for g in range(count):
                    if g + 1 < count:
                        if g >= 1:
                            dve.wait_ge(norm_lo, n0 + g)
                        make(g + 1).then_inc(norm_scaled, 1)
                    dve.wait_ge(norm_hi, n0 + g + 1)
                    lo_, hi_ = lo_t(g)
                    dve.scalar_tensor_tensor(out=r(lo_), in0=tmp[:, g % 2], scalar=shift(g), in1=hi_,
                                             op0=ALU.add, op1=ALU.subtract).then_inc(norm_lo, 1)

            def xcols(t, n):
                return t[:, n // 2, HALF * (n % 2):HALF * (n % 2) + HALF]

            for i in range(4):
                for j in range(2):
                    ada_tile(2 * i + j, w_ada0[:, i % 2, j], ada_w_first[i], 32)
                dve.wait_ge(ada_summed, 2 * i + 2)
                dve.wait_ge(ada_pool_summed, 2 * i + 2)
                for c0 in (2 * i, KD + 2 * i):
                    ins = dve.tensor_tensor(mod[:, c0:c0 + 2], ada[:, c0:c0 + 2], b_ada[:, c0:c0 + 2], ALU.add)
                vlink(ins)
                sg = scale_g[:, 0, 2 * i:2 * i + 2]
                vlink(dve.tensor_scalar(sg, mod[:, KD + 2 * i:KD + 2 * i + 2], 1.0, None, ALU.add))
                vlink(dve.tensor_tensor(sg, sg, norm_g[:, 0, 2 * i:2 * i + 2], ALU.mult))
                split_tiles(4 * i, 4 * i, 4,
                            lambda n, i=i: dve.scalar_tensor_tensor(
                                out=h_t[:, n % 2], in0=xcols(x_sb, 4 * i + n),
                                scalar=scale_g[:, 0, 2 * i + n // 2:2 * i + n // 2 + 1], in1=ps[:, 4 + n % 2],
                                op0=ALU.mult, op1=ALU.mult),
                            h_t, lambda n, i=i: (xcols(h_lo, 4 * i + n), xcols(h_hi, 4 * i + n)),
                            lambda n, i=i: mod[:, 2 * i + n // 2:2 * i + n // 2 + 1])

            for n in range(2):
                dve.wait_ge(unit_out, n + 1)
                dve.tensor_tensor(r(qi_lo[:, n]), ps[:, 2 * n:2 * n + 2].rearrange("p b c -> p (b c)"), qi_hi[:, n],
                                  ALU.subtract).then_inc(qi_lo_ready, 1)
            dve.wait_ge(unit_out, U_KIWI + 1)
            dve.tensor_tensor(r(ki_st[2 * IDX_DIM:]), ps[0:IDX_DIM, 0:2].rearrange("p b c -> p (b c)"),
                              ki_st[0:IDX_DIM], ALU.subtract).then_inc(ki_lo_ready, 1)
            dve.wait_ge(wi_turned, 1)
            dve.tensor_scalar(wis[:], ps[:, 6, 0:48].rearrange("p (b h) -> p b h", b=6), IDX_HEADS ** -0.5, None,
                              ALU.mult).then_inc(wi_scaled, 1)
            dve.wait_ge(wi_scaled, 1)
            def accumulate(quad):
                for i in range(4 * quad, 4 * quad + 4):
                    b, k0, n, h = DOTS[i]
                    dst = score[:, SC[b] + k0:SC[b] + k0 + n]
                    wgt = wis[:, b - 2, h:h + 1]
                    dve.wait_ge(relu_ready, i + 1)
                    if h == 0:
                        dve.tensor_scalar(dst, relu_r[:, i % 4, 0:n], wgt, None, ALU.mult).then_inc(scores_added, 1)
                    else:
                        dve.wait_ge(scores_added, i)
                        dve.scalar_tensor_tensor(out=dst, in0=relu_r[:, i % 4, 0:n], scalar=wgt, in1=dst,
                                                 op0=ALU.mult, op1=ALU.add).then_inc(scores_added, 1)
                if h == IDX_HEADS - 1 and k0 + n == P * (b + 1):
                    dve.wait_ge(scores_added, 4 * quad + 4)
                    vlink(dve.memset(score[0:64, SC[b] + P * (b + 1) - 64:SC[b] + P * (b + 1)], NO_KEY))

            def sc_of(b):
                return score[:, SC[b]:SC[b] + P * (b + 1)]

            def wait_apart(signal, value):
                dve.wait_ge(signal, value)
                dve.memset(tick[:], 0.0)

            def top_max(blocks, base):
                wait_apart(top8_marked, base)
                for b in blocks:
                    dve.max(top8[:, b - 2], sc_of(b)).then_inc(top8_found, 1)

            def top_mark(blocks, base):
                wait_apart(top8_found, base + len(blocks))
                for b in blocks:
                    dve.match_replace(sc_of(b), top8[:, b - 2], sc_of(b), TAKEN).then_inc(top8_marked, 1)

            def top_round(blocks, base):
                top_max(blocks, base)
                top_mark(blocks, base)

            def mask_of(b):
                vlink(dve.tensor_scalar(sc_of(b), sc_of(b), TAKEN_BELOW, NEG, ALU.is_gt, ALU.mult))

            taken = 0
            for step in range(ADA_STEPS):
                if step < DOT_STEPS:
                    accumulate(2 * step)
                for c in (16 + 2 * step, 17 + 2 * step):
                    ada_tile(c, w_ada1[:, c % 2], ada_w_rest[c % 2], 16 * (step + 1))
                if step < DOT_STEPS:
                    accumulate(2 * step + 1)
                if step in early_steps:
                    with dve.Fori(0, early_steps[step], 1) as i:
                        top_round(EARLY, len(EARLY) * (taken + i))
                    taken += early_steps[step]
            dve.wait_ge(top8_marked, len(EARLY) * ROUNDS)
            for b in EARLY:
                mask_of(b)
            dve.sem_inc(masks_ready, 1)
            dve.wait_ge(ada_summed, 40)
            vlink(dve.tensor_tensor(mod[:, 16:48], ada[:, 16:48], b_ada[:, 16:48], ALU.add))
            vlink(dve.tensor_scalar(scale_g[:, 1], mod[:, 4 * KD:5 * KD], 1.0, None, ALU.add))
            dve.tensor_tensor(scale_g[:, 1], scale_g[:, 1], norm_g[:, 1], ALU.mult).then_inc(mod_ready, 1)

            def by_group(ap):
                return ap.rearrange("p (g c) -> p g c", c=64)

            def ln_mean(b):
                mean = st3[:, 4 * b:4 * b + 4]
                dve.wait_ge(gm_out, b + 1)
                vlink(dve.tensor_reduce(mean, by_group(gm[:, b, W:]), AX, ALU.add))
                dve.tensor_scalar(mean, mean, 1.0 / 64, None, ALU.mult).then_inc(ln_mean_ready, 1)

            def ln_var(b):
                dve.wait_ge(ln_centred, b + 1)
                dve.tensor_reduce(st[:, 4 * b:4 * b + 4], by_group(gm_sq[:, b % 2]), AX, ALU.add).then_inc(ln_var_ready, 1)

            dve.wait_ge(swa_table_loaded, 16)
            vlink(dve.memset(swa_bias[:, :, 192:256], NEG))
            vlink(dve.memset(swa_bias[64:128, :, 128:192], NEG))
            vlink(dve.memset(swa_bias[0:64, :, 0:64], NEG))

            def swa_softmax(b):
                c0 = P if b == 0 else 0
                lg = logit[:, b % 2]
                src = ps[:, 4 - 2 * (b % 2):6 - 2 * (b % 2)].rearrange("p a (h c) -> p (a h) c", h=2)
                dve.wait_ge(swa_logits_ready, b + 1)
                if b >= 2:
                    dve.wait_ge(swa_turned, 2 * b - 2)
                vlink(dve.scalar_tensor_tensor(out=lg[:, :, c0:2 * P], in0=src[:, :, c0:], scalar=HD ** -0.5,
                                               in1=backwards(swa_bias[:, :, 0:2 * P - c0]), op0=ALU.mult, op1=ALU.add))
                dve.wait_ge(sink_ready, b + 1)
                vlink(dve.tensor_reduce(sm_max[:, b % 3], lg[:, :, c0:], AX, ALU.max))
                dve.tensor_scalar(sm_neg[:, b % 3], sm_max[:, b % 3], -1.0, None, ALU.mult).then_inc(swa_max, 1)

            def swa_out(b):
                dve.wait_ge(swa_exp, HEADS * (b + 1))
                vlink(dve.reciprocal(sm_rec[:, b % 3], sm_sum[:, b % 3]))
                dve.wait_ge(swa_product, b + 1)
                dve.tensor_tensor(y[:, b, 3 * W:].rearrange("p (h c) -> p h c", h=HEADS),
                                  ps[:, 7 if b % 2 == 0 else 0, 0:W].rearrange("p (h c) -> p h c", h=HEADS),
                                  sm_rec[:, b % 3].unsqueeze(2).to_broadcast([P, HEADS, HD]),
                                  ALU.mult).then_inc(swa_out_ready, 1)

            swa_softmax(0)
            swa_softmax(1)
            dve.wait_ge(pool_done, 1)
            for q4 in range(4):
                ins = dve.tensor_tensor(y[:, 2 * q4:2 * q4 + 2, 2 * W:3 * W],
                                        ps[:, POOL_BANKS[q4]].rearrange("p (b c) -> p b c", b=2),
                                        pool_s[:].unsqueeze(1).to_broadcast([P, 2, W]), ALU.mult)
            ins.then_inc(pool_out_ready, 1)
            for b in range(NBLK):
                if 1 <= b < NBLK - 1:
                    swa_softmax(b + 1)
                ln_mean(b)
                if b >= 1:
                    ln_var(b - 1)
                    swa_out(b - 1)
            ln_var(NBLK - 1)
            swa_out(NBLK - 1)

            def gmlp_outputs():
                dve.wait_ge(ln_root_ready, 1)
                vlink(dve.reciprocal(st3[:, 0:32], st2[:, 0:32]))
                vg = vn[:].rearrange("p b (g c) -> p (b g) c", c=64)
                dve.tensor_tensor(vg, vg, st3[:, 0:32].unsqueeze(2).to_broadcast([P, 4 * NBLK, 64]),
                                  ALU.mult).then_inc(vn_ready, 1)
                for g in range(4):
                    cols = slice(64 * g, 64 * g + 64)
                    dve.wait_ge(gate_done, g + 1)
                    dve.scalar_tensor_tensor(out=y[:, :, cols],
                                             in0=ps[:, GATE_BANKS[g]].rearrange("p (b c) -> p b c", b=NBLK),
                                             scalar=gm_b[:, g:g + 1], in1=gm[:, :, cols],
                                             op0=ALU.add, op1=ALU.mult).then_inc(gmlp_out, 1)

            R0 = 2 * ROUNDS
            m = len(LATE_BLOCKS)
            rounds = [0]
            for h in range(2):
                nb = half_base(h)
                bias_t = bias_1 if h else bias_0
                if h == 0:
                    dve.wait_ge(table_loaded, 16)
                    dve.memset(bias_0[0:64, :, 0:64], NEG).then_inc(bias_masked, 1)
                    dve.wait_ge(bias_masked, 1)

                def soft(i):
                    b = HB * h + i // 2
                    n = P * (b + 1)
                    for e in range(2):
                        hd = 2 * (i % 2) + e
                        I = HEADS * b + hd
                        dve.wait_ge(dsa_logits_ready, I + 1)
                        if I >= 4:
                            dve.wait_ge(dsa_turned, turned_through(I - 4))
                        if b >= 2:
                            dve.wait_ge(bias_and_mask, I - 7)
                            bias = bias_m[:, I % 2, 0:n]
                        else:
                            bias = backwards(bias_t[:, hd, 0:n])
                        dve.scalar_tensor_tensor(out=logit4[:, I % 4, 0:n],
                                                 in0=ps[:, 2 + 2 * e:4 + 2 * e].rearrange("p a c -> p (a c)")[:, 0:n],
                                                 scalar=HD ** -0.5, in1=bias,
                                                 op0=ALU.mult, op1=ALU.add).then_inc(dsa_biased, 1)
                    for e in range(2):
                        hd = 2 * (i % 2) + e
                        I = HEADS * b + hd
                        dve.wait_ge(dsa_biased, I + 1)
                        vlink(dve.tensor_reduce(sm_max[:, b % 2, hd:hd + 1], logit4[:, I % 4, 0:n], AX, ALU.max))
                        dve.tensor_scalar(sm_neg[:, b % 2, hd:hd + 1], sm_max[:, b % 2, hd:hd + 1], -1.0, None,
                                          ALU.mult).then_inc(dsa_max, 1)

                def final_norm(hh):
                    for g in range(KD):
                        dve.scalar_tensor_tensor(out=fin_o[:, g], in0=x2[:, g], scalar=fin_g[:, g:g + 1],
                                                 in1=ps[:, FIN_BANK], op0=ALU.mult, op1=ALU.mult).then_inc(final_ready, 1)

                soft(0)
                if h == 0:
                    gmlp_outputs()
                else:
                    root(2, diag2[:])
                soft(1)
                if h == 1:
                    final_norm(0)
                for i in range(2 * HB):
                    if i + 2 < 2 * HB:
                        soft(i + 2)
                    if i % 2 == 1:
                        b = HB * h + i // 2
                        dve.wait_ge(dsa_exp, HEADS * (b + 1))
                        vlink(dve.reciprocal(sm_rec[:, b % 2], sm_sum[:, b % 2]))
                        dve.wait_ge(dsa_product, HEADS * (b + 1))
                        dve.tensor_tensor(y[:, b, W:2 * W].rearrange("p (h c) -> p h c", h=HEADS),
                                          ps[:, 7 if b % 2 == 0 else 0, 0:W].rearrange("p (h c) -> p h c", h=HEADS),
                                          sm_rec[:, b % 2].unsqueeze(2).to_broadcast([P, HEADS, HD]),
                                          ALU.mult).then_inc(dsa_out_ready, 1)
                dve.wait_ge(y_root_ready, h + 1)
                vlink(dve.reciprocal(st3[:, 0:16], st2[:, 0:16]))
                for m_ in range(4):
                    dve.tensor_tensor(diag_y[:, m_], ident[:].unsqueeze(1).to_broadcast([P, HB, P]),
                                      st3[:, 0:16].rearrange("p (t m) -> p m t", m=4)[:, m_].unsqueeze(2)
                                      .to_broadcast([P, HB, P]), ALU.mult).then_inc(y_diag_ready, 1)
                n0 = 16 + 16 * h
                for g in range(KD):
                    dve.wait_ge(norm_hi, n0 + g + 1)
                    dve.scalar_tensor_tensor(out=r(y_lo[:, g]), in0=ps[:, Y_BANKS[g % 4]], scalar=mix_g[:, g:g + 1],
                                             in1=y_hi[:, g], op0=ALU.mult, op1=ALU.subtract).then_inc(norm_lo, 1)

                def column_loop(base, gate, q0, beside=lambda i: None, i0=0, i1=KD // 2, sums=True):
                    if q0 and sums:
                        vlink(dve.memset(sum2[:], 0.0))
                    with dve.Fori(i0, i1, 1) as i:
                        for j in range(2):
                            dve.wait_ge(unit_done, base + j + 1 + 2 * i)
                            o = x2[:, j + 2 * i]
                            dve.scalar_tensor_tensor(out=o, in0=ps[:, 2 + j], scalar=mod[:, bass.ds(gate + j + 2 * i, 1)],
                                                     in1=o, op0=ALU.mult, op1=ALU.add).then_inc(residual_added, 1)
                            if q0:
                                dve.wait_ge(squares_ready, q0 + j + 1 + 2 * i)
                                dve.wait_ge(squares_added, q0 + j + 2 * i)
                                dve.tensor_tensor(sum2[:], sum2[:], sq2[:, j], ALU.add).then_inc(squares_added, 1)
                        beside(i)

                dve.wait_ge(x2_loaded, 16 * (h + 1))
                if h == 0:
                    rounds[0] = 2
                    column_loop(nb, 2 * KD, n0 - KD, lambda i: top_round(LATE_BLOCKS, R0 + m * i), 0, rounds[0])
                    column_loop(nb, 2 * KD, n0 - KD, i0=rounds[0], sums=False)
                else:
                    column_loop(nb, 2 * KD, n0 - KD)
                root(1 + 2 * h, diag2[:])
                split_tiles(16 + KD * h, n0 + KD, KD,
                            lambda g: dve.scalar_tensor_tensor(out=h2_t[:, g % 2], in0=x2[:, g],
                                                               scalar=scale_g[:, 1, g:g + 1], in1=ps[:, 6],
                                                               op0=ALU.mult, op1=ALU.mult),
                            h2_t, lambda g: (h2_lo[:, g], h2_hi[:, g]),
                            lambda g: mod[:, 3 * KD + g:3 * KD + g + 1])
                for g, nf, nu, nd, f0 in group_bases(h):
                    F = 2 + NF * h + f0
                    with dve.Fori(0, nf // 2, 1) as i:
                        for u in range(2):
                            f = F + u + 2 * i
                            dve.wait_ge(conv_in_ready, f + 1)
                            dve.wait_ge(act_ready, f - 1)
                            dve.scalar_tensor_tensor(out=conv_t[:, u], in0=conv_in[:, u, 1:HALF + 1],
                                                     scalar=conv_w[:, f0 + u + 2 * i, 1:2], in1=conv_t[:, u],
                                                     op0=ALU.mult, op1=ALU.add).then_inc(conv_tap_added, 1)
                            dve.wait_ge(conv_tap_added, f + 1)
                            dve.scalar_tensor_tensor(out=conv_t[:, u], in0=conv_in[:, u, 0:HALF],
                                                     scalar=conv_w[:, f0 + u + 2 * i, 0:1], in1=conv_t[:, u],
                                                     op0=ALU.mult, op1=ALU.add).then_inc(conv_done, 1)
                            base = R0 + m * rounds[0] + m * u + 2 * m * i
                            if h == 0:
                                top_max(LATE_BLOCKS, base)
                            dve.wait_ge(gelu_ready, f + 1)
                            dve.wait_ge(unit_done, nu + 2 + 2 * u + 4 * i)
                            dve.wait_ge(act_lo_ready, f - 1)
                            dve.tensor_tensor(act_f[:, u], conv_t[:, u], ps[:, 4 + u], ALU.mult).then_inc(act_ready, 1)
                            if h == 0:
                                top_mark(LATE_BLOCKS, base)
                    if h == 0:
                        rounds[0] += nf
                    q0 = n0 if g == 2 else 0
                    beside = lambda i: top_round(LATE_BLOCKS, R0 + m * rounds[0] + m * i)
                    if h == 0 and g < 2:
                        column_loop(nd, 5 * KD, q0, beside)
                        rounds[0] += KD // 2
                    else:
                        if h == 0:
                            assert rounds[0] == ROUNDS
                            dve.wait_ge(top8_marked, R0 + m * ROUNDS)
                            for b in LATE_BLOCKS:
                                mask_of(b)
                            dve.sem_inc(masks_ready, 1)
                            dve.wait_ge(table_loaded, 32)
                            dve.memset(bias_1[0:64, :, 0:64], NEG).then_inc(bias_masked, 1)
                        column_loop(nd, 5 * KD, q0)
            root(4, diag2[:])
            final_norm(1)

        @block.tensor
        def _(pe):
            for signal in (halo_in, conv_in_ready, conv_done, gelu_ready, act_ready, act_hi_ready, act_lo_ready, conv_tap_added):
                pe.sem_inc(signal, 2)
            pe.sem_inc(residual_added, 2)
            pe.wait_ge(rel_loaded, 32)
            for i in range(3):
                last = pe.matmul(ps[0:8, 4 + i, 0:384], rel[:], onehot[:, 384 * i:384 * i + 384], start=True, stop=True)
            last.then_inc(bias_row_made, 1)

            def over_features(m, count, bank, sums, diag, blocks=HB):
                pe.wait_ge(squares_added, count)
                for t in range(blocks):
                    mm = pe.matmul(ps[:, bank, t:t + 1], sums[:, P * t:P * t + P], ones[:, 0:1], start=True, stop=True)
                mm.then_inc(mean_square, 1)
                pe.wait_ge(diag_ready, m + 1)
                for i in range(blocks // HB):
                    mm = pe.matmul(ps[:, bank + i], ones[:], diag[:, HALF * i:HALF * i + HALF], start=True, stop=True)
                mm.then_inc(rms_spread, 1)

            pe.wait_ge(consts_set, 4)
            pe.wait_ge(bias_row_out, 1)
            over_features(0, KD, 4, sum_x, diag_x, NBLK)

            def gemm(slot, nk, parts, ready, *waits, tiles=None, beside=None):
                pe.wait_ge(w_lo_ready, ready)
                for signal, val in waits:
                    pe.wait_ge(signal, val)
                for kk in range(nk):
                    first, last_k = kk == 0, kk == nk - 1
                    if tiles:
                        pe.wait_ge(*tiles(kk))
                    for bank, xh, xl in parts:
                        pe.matmul(ps[:, bank], r(w_hi[:, slot, kk]), r(xh(kk)), start=first, stop=False)
                        pe.matmul(ps[:, bank], r(w_hi[:, slot, kk]), r(xl(kk)), start=False, stop=False)
                    for bank, xh, xl in parts:
                        mm = pe.matmul(ps[:, bank], r(w_lo[:, slot, kk]), r(xh(kk)), start=False, stop=last_k)
                    if beside and not last_k:
                        beside(kk)
                mm.then_inc(unit_done, 1)

            def in_parts(n):
                return [(2 * (n % 2) + i,
                         lambda kk, i=i: h_hi[:, kk, HALF * i:HALF * i + HALF],
                         lambda kk, i=i: h_lo[:, kk, HALF * i:HALF * i + HALF]) for i in range(2)]

            def dots(quad):
                if quad == 0:
                    pe.wait_ge(wi_scaled, 1)
                    pe.wait_ge(ki_lo_ready, 1)
                else:
                    pe.wait_ge(relu_ready, 4 * quad)
                b = DOTS[4 * quad][0]
                pe.wait_ge(qi_loaded[b % 2], 48 * (b // 2))
                for i in range(4 * quad, 4 * quad + 4):
                    b, k0, n, h = DOTS[i]
                    pe.matmul(ps[:, 4 + i % 4, 0:n], r(qi_st[:, b % 2, h]), r(ki_st[:, k0:k0 + n]),
                              start=True, stop=True).then_inc(dots_done, 1)

            def v_turn(g, src):
                if g > 0:
                    pe.wait_ge(v_out, g)
                for t in range(HB):
                    blk = HB * (g % 2) + t
                    tr = pe.transpose(ps[:, 6, P * t:P * t + P], src[:, P * blk:P * blk + P], ident[:])
                tr.then_inc(v_turned, 1)

            for n in range(N_IN):
                if n == DOT_UNIT:
                    pe.wait_ge(unit_out, U_KIWI + 1)
                    pe.wait_ge(norm_lo, 16)
                    for b in TOP_BLOCKS:
                        mm = pe.matmul(ps[:, 6, 8 * (b - 2):8 * (b - 2) + 8], kiwi[:, P * b:P * b + P],
                                       ident[:, WI_COL:WI_COL + IDX_HEADS], start=True, stop=True)
                    mm.then_inc(wi_turned, 1)
                step = n - DOT_UNIT
                gemm(n % 2, KD, in_parts(n), n + 1, *([(unit_out, n - 1)] if n >= 2 else []),
                     *([(qi_lo_ready, n - 1)] if n in (2, 3) else []), *([(ki_lo_ready, 1)] if n == U_KIWI + 2 else []),
                     tiles=(lambda kk: (norm_lo, 2 * kk + 2)) if n == 0 else None,
                     beside=(lambda kk: {2: lambda: dots(2 * step), 6: lambda: dots(2 * step + 1)}.get(kk, int)())
                     if 0 <= step < DOT_STEPS else None)
                if n == 13:
                    pe.wait_ge(relu_ready, len(DOTS))
                    pe.wait_ge(unit_out, U_V + 2)
                    for g in range(4):
                        v_turn(g, stage[g // 2])
                if n == 16:
                    pe.wait_ge(unit_out, U_DV + 1)
                    for g in range(4, 6):
                        v_turn(g, stage[0])

            pe.wait_ge(unit_out, N_IN)
            pe.wait_ge(relu_ready, len(DOTS))
            for b in range(NBLK):
                if b >= 2:
                    pe.wait_ge(gm_out, b - 1)
                for t in range(4):
                    tr = pe.transpose(ps[:, 4 + b % 2, P * t:P * t + P], za_t[:, t, P * b:P * b + P], ident[:])
                tr.then_inc(gm_turned, 1)

            pe.wait_ge(v_out, 6)
            pe.wait_ge(gm_out, NBLK)
            pe.wait_ge(mod_ready, 1)

            def swa_logits(b):
                c0 = P if b == 0 else 0
                if b >= 2:
                    pe.wait_ge(swa_max, b - 1)
                bank = 4 - 2 * (b % 2)
                for h in (0, 2, 1, 3):
                    rows = slice(64 * (h // 2), 64 * (h // 2) + 64)
                    mm = pe.matmul(ps[:, bank + h // 2, 2 * P * (h % 2) + c0:2 * P * (h % 2) + 2 * P],
                                   dq[rows, h % 2, P * b:P * b + P], dk[rows, P * (b - 1) + c0:P * (b + 1)],
                                   start=True, stop=True)
                mm.then_inc(swa_logits_ready, 1)

            swa_logits(0)
            swa_logits(1)
            pe.wait_ge(pool_ready, 1)
            pe.wait_ge(pool_w_loaded, 16)
            for b in range(NBLK):
                for t in range(2):
                    at_ = W * (b % 2) + P * t
                    mm = pe.matmul(ps[:, POOL_BANKS[b // 2], at_:at_ + P], zc[t][:, 16 + P * b:16 + P * b + P],
                                   pool_w[:, t], start=True, stop=True)
            mm.then_inc(pool_done, 1)

            def swa_values(b):
                cs = [1] if b == 0 else [0, 1]
                pe.wait_ge(swa_probs, 2 * b + 2)
                if b >= 2:
                    pe.wait_ge(swa_out_ready, b - 1)
                for h in range(HEADS):
                    for c in cs:
                        mm = pe.matmul(ps[:, 7 if b % 2 == 0 else 0, HD * h:HD * h + HD],
                                       p_t[:, b % 2, 2 * h + c], dv[:, b - 1 + c, HD * (h // 2):HD * (h // 2) + HD],
                                       start=(c == cs[0]), stop=(c == 1))
                mm.then_inc(swa_product, 1)

            for b in range(NBLK):
                if 1 <= b < NBLK - 1:
                    swa_logits(b + 1)
                if b == 0:
                    pe.wait_ge(pool_out_ready, 1)
                pe.wait_ge(swa_exp, HEADS * b + 2)
                lg = logit[:, b % 2]
                for j in range(2):
                    if b >= 1:
                        pe.wait_ge(swa_probs, 2 * b - 1 + j)
                    if j == 1:
                        pe.wait_ge(swa_exp, HEADS * b + 4)
                    for hh in range(2):
                        for c in ([1] if b == 0 else [0, 1]):
                            at_ = P * (2 * hh + c)
                            tr = pe.transpose(ps[:, 6 if j == 0 else 1, at_:at_ + P],
                                              lg[:, 2 * j + hh, P * c:P * c + P], ident[:])
                    tr.then_inc(swa_turned, 1)
                if b >= 1:
                    swa_values(b - 1)
            swa_values(NBLK - 1)

            def gmlp_gating():
                pe.wait_ge(consts_set, 4)
                pe.wait_ge(swa_probs, 2 * NBLK)
                pe.wait_ge(swa_out_ready, NBLK)
                pe.wait_ge(vn_ready, 1)
                for g in range(4):
                    pe.matmul(ps[:, GATE_BANKS[g]], ws_t[:, g], vn[:, :, 64 * g:64 * g + 64],
                              start=True, stop=True).then_inc(gate_done, 1)
                pe.wait_ge(gmlp_out, 4)

            n_pt = [0]
            for h in range(2):
                def logits(i):
                    b, t = HB * h + i // 2, i % 2
                    I = HEADS * b + 2 * t
                    n = P * (b + 1)
                    if I > 0:
                        pe.wait_ge(dsa_biased, I)
                    pe.wait_ge(k_loaded, 32)
                    pe.wait_ge(q_loaded[b % 2], 64 * (b // 2 + 1))
                    for e in range(2):
                        for c in range(0, n, 512):
                            w_ = min(512, n - c)
                            for part in range(2):
                                mm = pe.matmul(ps[:, 2 + 2 * e + c // 512, 0:w_], r(q_st[q_place(b)][:, part, 2 * t + e]),
                                               r(k_st[:, 2 * t + e, c:c + w_]), start=(part == 0), stop=(part == 1))
                        mm.then_inc(dsa_logits_ready, 1)

                if h == 0:
                    pe.wait_ge(swa_max, NBLK)
                else:
                    pe.wait_ge(residual_added, 2 + 4 * KD)
                logits(0)
                if h == 0:
                    gmlp_gating()
                else:
                    over_features(2, 3 * KD, FIN_BANK, sum2, diag2)
                logits(1)
                for i in range(2 * HB):
                    b = HB * h + i // 2
                    turned = []
                    for e in range(2):
                        I = HEADS * b + 2 * (i % 2) + e
                        pe.wait_ge(dsa_exp, I + 1)
                        for t0 in range(0, b + 1, 4):
                            if n_pt[0] >= 2:
                                pe.wait_ge(dsa_probs, n_pt[0] - 1)
                            for t in range(t0, min(t0 + 4, b + 1)):
                                tr = pe.transpose(ps[:, 6 if n_pt[0] % 2 == 0 else 1, P * (t - t0):P * (t - t0) + P],
                                                  logit4[:, I % 4, P * t:P * t + P], ident[:])
                            tr.then_inc(dsa_turned, 1)
                            n_pt[0] += 1
                        turned.append(n_pt[0])
                    if i + 2 < 2 * HB:
                        logits(i + 2)
                    for e in range(2):
                        hd = 2 * (i % 2) + e
                        I = HEADS * b + hd
                        pe.wait_ge(dsa_probs, turned[e])
                        if hd == 0 and b >= 2:
                            pe.wait_ge(dsa_out_ready, b - 1)
                        if hd == 0 and b == HB + 1:
                            pe.wait_ge(final_ready, KD)
                        for t in range(b + 1):
                            mm = pe.matmul(ps[:, 7 if b % 2 == 0 else 0, HD * hd:HD * hd + HD], p_t[:, I % 2, t],
                                           v[:, t, HD * hd:HD * hd + HD], start=(t == 0), stop=(t == b))
                        mm.then_inc(dsa_product, 1)
                pe.wait_ge(dsa_out_ready, HB * (h + 1))
                n0 = 16 + 16 * h
                for g in range(KD):
                    pe.wait_ge(y_diag_ready, 4 * h + g // 2 + 1)
                    if g >= 4:
                        pe.wait_ge(norm_lo, n0 + g - 3)
                    for t in range(4):
                        tr = pe.matmul(ps[:, Y_BANKS[g % 4], P * t:P * t + P], y[:, HB * h + t, P * g:P * g + P],
                                       diag_y[:, g // 2, t], start=True, stop=True)
                    tr.then_inc(y_turned, 1)

                def column_loop(base, J, nk, xh, xl, tiles=None):
                    with pe.Fori(0, KD // 2, 1) as i:
                        for j in range(2):
                            gemm((base + j) % 2, nk, [(2 + j, xh, xl)], base + j + 1 + 2 * i,
                                 (residual_added, J + j + 1 + 2 * i), tiles=tiles if j == 0 else None)

                nb = half_base(h)
                J = 4 * KD * h
                column_loop(nb, J, KD, lambda kk: y_hi[:, kk], lambda kk: y_lo[:, kk],
                            tiles=lambda kk: (norm_lo, n0 + kk + 1))
                over_features(1 + 2 * h, n0, 6, sum2, diag2)
                for g, nf, nu, nd, f0 in group_bases(h):
                    F = 2 + NF * h + f0
                    with pe.Fori(0, nf // 2, 1) as i:
                        for u in range(2):
                            f = F + u + 2 * i
                            for j, bank, signal in ((0, u, conv_in_ready), (1, 4 + u, act_ready)):
                                gemm((nu + j) % 2, KD, [(bank, lambda kk: h2_hi[:, kk], lambda kk: h2_lo[:, kk])],
                                     nu + j + 1 + 2 * u + 4 * i, (signal, f - 1),
                                     tiles=(lambda kk: (norm_lo, n0 + KD + kk + 1)) if (g, u, j) == (0, 0, 0) else None)
                    J += KD
                    column_loop(nd, J, nf, lambda kk: act_hi[:, kk], lambda kk: act_lo[:, kk],
                                tiles=lambda kk: (act_lo_ready, F + kk + 1))
            over_features(4, 5 * KD, FIN_BANK, sum2, diag2)


def bias_onehot():
    rel = P - 1 - np.arange(S + P)
    n = np.abs(rel)
    nf = np.maximum(n, 1).astype(np.float32)
    large = 8 + (np.log(nf / np.float32(8)) / np.float32(np.log(1024 / 8)) * np.float32(8)).astype(np.int32)
    bucket = np.where(rel > 0, 16, 0) + np.where(n < 8, n, np.minimum(large, 15))
    return (np.arange(32)[:, None] == bucket[None, :]).astype(np.float32)


def pool_counts():
    t = np.arange(1, 17, dtype=np.float32)
    rows = [1 / np.minimum(t, np.float32(w)) for w in (2, 4, 8, 16)]
    c = np.stack([np.stack([rows[0], rows[2]]), np.stack([rows[1], rows[3]])])
    return np.repeat(c, 64, axis=0).astype(np.float32)


def pool_blocks(w):
    out = np.zeros((2, P, P), np.float32)
    for g in range(4):
        rows = slice(64 * (g % 2), 64 * (g % 2) + 64)
        out[g // 2, rows, rows] = w[g]
    return out.transpose(1, 0, 2)


def weight_units(w_in, w_out, w_up, w_down):
    def cols(*runs):
        part = np.concatenate([w_in[:, x0:x1] for x0, x1 in runs], axis=1)
        if part.shape[1] < P:
            part = np.concatenate([part, np.zeros((D, P - part.shape[1]), np.float32)], axis=1)
        return part

    def unit(m):
        return m.reshape(-1, P, P).transpose(1, 0, 2)

    def tiles(x0, n):
        return [cols((x0 + P * i, x0 + P * i + P)) for i in range(n)]

    zc, zdq = 1576, 1832
    units = (tiles(1280, 2) + [cols((1536, 1576))] + tiles(512, 2) + tiles(768, 2) + tiles(1024, 2)
             + tiles(zc, 2)
             + [cols((zdq + 64 * i, zdq + 64 * i + 64), (zdq + 128 + 64 * i, zdq + 192 + 64 * i)) for i in range(2)]
             + tiles(2088, 1) + tiles(2216, 1) + tiles(0, 4))
    units = [unit(u) for u in units]
    units += [unit(w_out[:, P * j:P * j + P]) for j in range(KD)]
    f0 = 0
    for nf in GROUPS:
        for f in range(f0, f0 + nf):
            units += [unit(w_up[:, P * f:P * f + P]), unit(w_up[:, DFF + P * f:DFF + P * f + P])]
        rows = w_down[P * f0:P * (f0 + nf)]
        if nf < KD:
            rows = np.concatenate([rows, np.zeros((P * (KD - nf), D), np.float32)], axis=0)
        units += [unit(rows[:, P * j:P * j + P]) for j in range(KD)]
        f0 += nf
    return np.ascontiguousarray(np.stack(units))


def kernel(x, c, w_ada, b_ada, norm1_g, norm2_g, w_in, gmlp_ws, gmlp_bs, pool_w, pool_scale,
           swa_sinks, rel_bias, mix_out_g, w_out, ffn_w_up, ffn_conv_w, ffn_conv_b, ffn_w_down,
           final_g):
    import concourse.bacc as bacc
    from concourse.bass_utils import run_bass_kernel_spmd

    def by_feature(vec):
        return np.asarray(vec).reshape(-1, P).T

    arrays = {
        "x": np.asarray(x)[0].T,
        "c": np.asarray(c)[0],
        "w_ada": np.asarray(w_ada)[0].T,
        "b_ada": by_feature(np.asarray(b_ada)[0]),
        "norm_g": np.stack([by_feature(np.asarray(norm1_g)[0]), by_feature(np.asarray(norm2_g)[0])], axis=1),
        "mix_g": by_feature(np.asarray(mix_out_g)[0]),
        "conv_w": np.stack([by_feature(t) for t in (*np.asarray(ffn_conv_w)[0], np.asarray(ffn_conv_b)[0])], axis=2),
        "gm_b": np.asarray(gmlp_bs)[0].T,
        "ident": np.eye(P, dtype=np.float32),
        "ws_t": np.asarray(gmlp_ws)[0].transpose(2, 0, 1),
        "pool_w": pool_blocks(np.asarray(pool_w)[0]),
        "pool_c": pool_counts(),
        "sinks": np.asarray(swa_sinks)[0],
        "pool_s": np.asarray(pool_scale)[0],
        "rel_bias": np.asarray(rel_bias),
        "onehot": bias_onehot(),
        "fin_g": by_feature(np.asarray(final_g)),
        "w": weight_units(np.asarray(w_in)[0], np.asarray(w_out)[0], np.asarray(ffn_w_up)[0],
                          np.asarray(ffn_w_down)[0]),
    }
    arrays = {n: np.ascontiguousarray(v) for n, v in arrays.items()}
    nc = bacc.Bacc("TRN2", target_bir_lowering=False, num_devices=1)
    ins = {n: nc.dram_tensor(f"in_{n}", v.shape, F32, kind="ExternalInput").ap() for n, v in arrays.items()}
    out = nc.dram_tensor("out", (D, S), F32, kind="ExternalOutput").ap()
    build(nc, ins, out)
    res = run_bass_kernel_spmd(nc, [{f"in_{n}": v for n, v in arrays.items()}], core_ids=[0])
    return np.ascontiguousarray(res.results[0]["out"].T).reshape(1, S, D)
```
